# Optimizing a Trainium2 kernel written in Bass

```python
import math
import jax, jax.numpy as jnp
from jax import lax
import numpy as np

D_MODEL = 1024
BATCH = 1
SEQ = 1024
DEPTH = 1
DEC_BATCH = 8
DEC_SEQ = 8
PAST_LEN = 2048
PAGE_SIZE = 128

N_HEADS = 8
NOPE_DIM = 64
ROPE_DIM = 32
V_HEAD = 64
Q_LORA = 384
KV_LORA = 256
ATTN_WIDTH = N_HEADS * V_HEAD
CONV_CH = 512
CONV_K = 31
IN_WIDTH = Q_LORA + KV_LORA + ROPE_DIM + 2 * CONV_CH
MIX_WIDTH = ATTN_WIDTH + CONV_CH
D_FF = ((8 * D_MODEL // 3 + 255) // 256) * 256
PLE_DIM = 256
ROPE_THETA = 10000.0
Q_BLOCK = 128
EPS = 1e-6
NEG_INF = -1e30
SCALE = 1.0 / math.sqrt(NOPE_DIM + ROPE_DIM)

kernel_name = "hymba_conformer_mla_decoder_step"

F32 = jnp.float32

def rms_norm(x, g):
    xf = x.astype(F32)
    y = xf * lax.rsqrt(jnp.mean(xf * xf, axis=-1, keepdims=True) + EPS)
    return (y * g.astype(F32)).astype(x.dtype)

def layer_norm(x, g, b):
    xf = x.astype(F32)
    mu = jnp.mean(xf, axis=-1, keepdims=True)
    var = jnp.mean(jnp.square(xf - mu), axis=-1, keepdims=True)
    y = (xf - mu) * lax.rsqrt(var + EPS) * g.astype(F32) + b.astype(F32)
    return y.astype(x.dtype)

def rope_tables(pos):
    inv = 1.0 / (ROPE_THETA ** (jnp.arange(0, ROPE_DIM, 2, dtype=F32) / ROPE_DIM))
    ang = pos.astype(F32)[:, None] * inv[None, :]
    return jnp.cos(ang), jnp.sin(ang)

def apply_rope(x, cos, sin):
    x1, x2 = jnp.split(x.astype(F32), 2, axis=-1)
    return jnp.concatenate([x1 * cos - x2 * sin, x2 * cos + x1 * sin], axis=-1).astype(x.dtype)

def mixer_inputs(h, pos, lp):
    z = h @ lp["w_in"]
    c_q, c_kv, k_pe, u = jnp.split(z, [Q_LORA, Q_LORA + KV_LORA, Q_LORA + KV_LORA + ROPE_DIM], axis=-1)
    c_q = rms_norm(c_q, lp["q_lora_norm"])
    q = (c_q @ lp["w_uq"]).reshape(*c_q.shape[:-1], N_HEADS, NOPE_DIM + ROPE_DIM)
    cos, sin = rope_tables(pos)
    q_nope = rms_norm(q[..., :NOPE_DIM], lp["q_nope_norm"])
    q_pe = apply_rope(rms_norm(q[..., NOPE_DIM:], lp["q_pe_norm"]), cos[:, None], sin[:, None])
    c_kv = rms_norm(c_kv, lp["kv_norm"])
    k_pe = apply_rope(rms_norm(k_pe, lp["k_pe_norm"]), cos, sin)
    return q_nope, q_pe, c_kv, k_pe, u

def expand_kv(c_kv, lp):
    k_nope = (c_kv @ lp["w_uk"]).reshape(*c_kv.shape[:-1], N_HEADS, NOPE_DIM)
    k_nope = rms_norm(k_nope, lp["k_nope_norm"])
    v = (c_kv @ lp["w_uv"]).reshape(*c_kv.shape[:-1], N_HEADS, V_HEAD)
    return k_nope, v

def attn_scores(q_nope, q_pe, k_nope, k_pe):
    s = jnp.einsum("bqhd,bkhd->bhqk", q_nope, k_nope).astype(F32)
    s = s + jnp.einsum("bqhr,bkr->bhqk", q_pe, k_pe).astype(F32)
    return s * SCALE

def attend_prompt(q_nope, q_pe, c_kv, k_pe, lp):
    B, T = q_nope.shape[:2]
    k_nope, v = expand_kv(c_kv, lp)
    kpos = jnp.arange(T)

    def block(i):
        s0 = i * Q_BLOCK
        qn = lax.dynamic_slice_in_dim(q_nope, s0, Q_BLOCK, axis=1)
        qp = lax.dynamic_slice_in_dim(q_pe, s0, Q_BLOCK, axis=1)
        sc = attn_scores(qn, qp, k_nope, k_pe)
        qpos = s0 + jnp.arange(Q_BLOCK)
        sc = jnp.where(kpos[None, :] <= qpos[:, None], sc, NEG_INF)
        p = jax.nn.softmax(sc, axis=-1)
        return jnp.einsum("bhqk,bkhd->bqhd", p.astype(v.dtype), v)

    o = lax.map(block, jnp.arange(T // Q_BLOCK))
    return jnp.moveaxis(o, 0, 1).reshape(B, T, ATTN_WIDTH)

def online_update(carry, sc, v):
    m, l, acc = carry
    m_new = jnp.maximum(m, jnp.max(sc, axis=-1))
    alpha = jnp.exp(m - m_new)
    p = jnp.exp(sc - m_new[..., None])
    l = l * alpha + jnp.sum(p, axis=-1)
    acc = acc * alpha[..., None] + jnp.einsum("bhqk,bkhd->bhqd", p, v.astype(F32))
    return (m_new, l, acc)

def attend_sample(q_nope, q_pe, c_kv, k_pe, cache_ckv, cache_kpe, page_table, layer, lp):
    Bd, Tq = q_nope.shape[:2]
    init = (jnp.full((Bd, N_HEADS, Tq), NEG_INF, F32),
            jnp.zeros((Bd, N_HEADS, Tq), F32),
            jnp.zeros((Bd, N_HEADS, Tq, V_HEAD), F32))

    def page_step(carry, pages):
        ckv = cache_ckv[layer, pages]
        kpe = cache_kpe[layer, pages]
        k_nope, v = expand_kv(ckv.astype(q_nope.dtype), lp)
        sc = attn_scores(q_nope, q_pe, k_nope, kpe.astype(q_pe.dtype))
        return online_update(carry, sc, v), None

    carry, _ = lax.scan(page_step, init, page_table.T)
    k_nope, v = expand_kv(c_kv, lp)
    sc = attn_scores(q_nope, q_pe, k_nope, k_pe)
    idx = jnp.arange(Tq)
    sc = jnp.where(idx[None, :] <= idx[:, None], sc, NEG_INF)
    m, l, acc = online_update(carry, sc, v)
    o = (acc / l[..., None]).astype(q_nope.dtype)
    return jnp.transpose(o, (0, 2, 1, 3)).reshape(Bd, Tq, ATTN_WIDTH)

def conv_mixer(u, conv_state, lp):
    a, g = jnp.split(u, 2, axis=-1)
    glu = a * jax.nn.sigmoid(g)
    xc = jnp.concatenate([conv_state.astype(glu.dtype), glu], axis=1)
    y = lax.conv_general_dilated(xc, lp["conv_w"][:, None, :].astype(glu.dtype), (1,), "VALID",
                                 dimension_numbers=("NWC", "WIO", "NWC"),
                                 feature_group_count=CONV_CH) + lp["conv_b"]
    y = jax.nn.silu(layer_norm(y, lp["conv_ln_g"], lp["conv_ln_b"]))
    return y, xc[:, -(CONV_K - 1):]

def layer_forward(x, pe, pos, conv_state, attend, lp):
    h = rms_norm(x, lp["norm_mix"])
    q_nope, q_pe, c_kv, k_pe, u = mixer_inputs(h, pos, lp)
    attn = attend(q_nope, q_pe, c_kv, k_pe)
    conv, new_conv = conv_mixer(u, conv_state, lp)
    mix = jnp.concatenate([rms_norm(attn, lp["norm_out_attn"]), rms_norm(conv, lp["norm_out_conv"])], axis=-1)
    x = x + mix @ lp["w_out"]
    h = rms_norm(x, lp["norm_ffn"])
    x = x + (jax.nn.silu(h @ lp["w_gate"]) * (h @ lp["w_up"])) @ lp["w_down"]
    x = x + jax.nn.sigmoid(rms_norm(x, lp["norm_ple"]) @ lp["w_ple_gate"]) * (pe @ lp["w_ple_proj"])
    return x, c_kv, k_pe, new_conv

def setup_inputs(seed: int = 0) -> dict:
    key = jax.random.key(seed)
    ks = iter(jax.random.split(key, 48))

    def nrm(shape, scale=1.0):
        return jax.random.normal(next(ks), shape, F32) * scale

    def gain(n):
        return 1.0 + nrm((DEPTH, n), 0.05)

    n_pages = PAST_LEN // PAGE_SIZE
    n_used = DEC_BATCH * n_pages
    n_pool = n_used + n_used // 4
    page_table = jax.random.permutation(next(ks), n_pool)[:n_used].reshape(DEC_BATCH, n_pages).astype(jnp.int32)
    return {
        "x_prompt": nrm((BATCH, SEQ, D_MODEL)),
        "x_sample": nrm((DEC_BATCH, DEC_SEQ, D_MODEL)),
        "cache_ckv": nrm((DEPTH, n_pool, PAGE_SIZE, KV_LORA)),
        "cache_kpe": nrm((DEPTH, n_pool, PAGE_SIZE, ROPE_DIM)),
        "state_conv": nrm((DEPTH, DEC_BATCH, CONV_K - 1, CONV_CH), 0.5),
        "page_table": page_table,
        "p_prompt": nrm((DEPTH, BATCH, SEQ, PLE_DIM)),
        "p_sample": nrm((DEPTH, DEC_BATCH, DEC_SEQ, PLE_DIM)),
        "norm_mix": gain(D_MODEL),
        "w_in": nrm((DEPTH, D_MODEL, IN_WIDTH), D_MODEL ** -0.5),
        "q_lora_norm": gain(Q_LORA),
        "w_uq": nrm((DEPTH, Q_LORA, N_HEADS * (NOPE_DIM + ROPE_DIM)), Q_LORA ** -0.5),
        "kv_norm": gain(KV_LORA),
        "w_uk": nrm((DEPTH, KV_LORA, N_HEADS * NOPE_DIM), KV_LORA ** -0.5),
        "w_uv": nrm((DEPTH, KV_LORA, N_HEADS * V_HEAD), KV_LORA ** -0.5),
        "q_nope_norm": gain(NOPE_DIM),
        "k_nope_norm": gain(NOPE_DIM),
        "q_pe_norm": gain(ROPE_DIM),
        "k_pe_norm": gain(ROPE_DIM),
        "conv_w": nrm((DEPTH, CONV_K, CONV_CH), CONV_K ** -0.5),
        "conv_b": nrm((DEPTH, CONV_CH), 0.02),
        "conv_ln_g": gain(CONV_CH),
        "conv_ln_b": nrm((DEPTH, CONV_CH), 0.02),
        "norm_out_attn": gain(ATTN_WIDTH),
        "norm_out_conv": gain(CONV_CH),
        "w_out": nrm((DEPTH, MIX_WIDTH, D_MODEL), MIX_WIDTH ** -0.5),
        "norm_ffn": gain(D_MODEL),
        "w_gate": nrm((DEPTH, D_MODEL, D_FF), D_MODEL ** -0.5),
        "w_up": nrm((DEPTH, D_MODEL, D_FF), D_MODEL ** -0.5),
        "w_down": nrm((DEPTH, D_FF, D_MODEL), D_FF ** -0.5),
        "norm_ple": gain(D_MODEL),
        "w_ple_gate": nrm((DEPTH, D_MODEL, D_MODEL), D_MODEL ** -0.5),
        "w_ple_proj": nrm((DEPTH, PLE_DIM, D_MODEL), PLE_DIM ** -0.5),
    }

def reference(x_prompt, x_sample, cache_ckv, cache_kpe, state_conv, page_table, p_prompt, p_sample,
              norm_mix, w_in, q_lora_norm, w_uq, kv_norm, w_uk, w_uv, q_nope_norm, k_nope_norm,
              q_pe_norm, k_pe_norm, conv_w, conv_b, conv_ln_g, conv_ln_b, norm_out_attn, norm_out_conv,
              w_out, norm_ffn, w_gate, w_up, w_down, norm_ple, w_ple_gate, w_ple_proj):
    B, T = x_prompt.shape[:2]
    Bd, Tq = x_sample.shape[:2]
    pos_prompt = jnp.arange(T)
    pos_sample = PAST_LEN + jnp.arange(Tq)
    zero_conv = jnp.zeros((B, CONV_K - 1, CONV_CH), x_prompt.dtype)
    xp, xs = x_prompt, x_sample
    ckv_p, kpe_p, conv_p, ckv_s, kpe_s, conv_s = [], [], [], [], [], []
    for i in range(DEPTH):
        lp = {
            "norm_mix": norm_mix[i], "w_in": w_in[i], "q_lora_norm": q_lora_norm[i], "w_uq": w_uq[i],
            "kv_norm": kv_norm[i], "w_uk": w_uk[i], "w_uv": w_uv[i], "q_nope_norm": q_nope_norm[i],
            "k_nope_norm": k_nope_norm[i], "q_pe_norm": q_pe_norm[i], "k_pe_norm": k_pe_norm[i],
            "conv_w": conv_w[i], "conv_b": conv_b[i], "conv_ln_g": conv_ln_g[i], "conv_ln_b": conv_ln_b[i],
            "norm_out_attn": norm_out_attn[i], "norm_out_conv": norm_out_conv[i], "w_out": w_out[i],
            "norm_ffn": norm_ffn[i], "w_gate": w_gate[i], "w_up": w_up[i], "w_down": w_down[i],
            "norm_ple": norm_ple[i], "w_ple_gate": w_ple_gate[i], "w_ple_proj": w_ple_proj[i],
        }
        att_p = lambda qn, qp, ckv, kpe, lp=lp: attend_prompt(qn, qp, ckv, kpe, lp)
        att_s = lambda qn, qp, ckv, kpe, lp=lp, i=i: attend_sample(qn, qp, ckv, kpe, cache_ckv, cache_kpe,
                                                                   page_table, i, lp)
        xp, c1, k1, v1 = layer_forward(xp, p_prompt[i], pos_prompt, zero_conv, att_p, lp)
        xs, c2, k2, v2 = layer_forward(xs, p_sample[i], pos_sample, state_conv[i], att_s, lp)
        ckv_p.append(c1); kpe_p.append(k1); conv_p.append(v1)
        ckv_s.append(c2); kpe_s.append(k2); conv_s.append(v2)
    return (xp, xs, jnp.stack(ckv_p), jnp.stack(kpe_p), jnp.stack(conv_p),
            jnp.stack(ckv_s), jnp.stack(kpe_s), jnp.stack(conv_s))


_drawn_inputs = setup_inputs


def setup_inputs(seed=0):
    import zlib

    import numpy as np

    out = dict(_drawn_inputs(seed))
    spreads = {}
    factors = {'q_pe_norm': 6.385,
     'conv_ln_b': 5.203,
     'norm_ple': 8.0,
     'q_nope_norm': 4.556,
     'k_nope_norm': 3.422}
    for name, (base, spread) in spreads.items():
        noise = np.random.default_rng([zlib.crc32(name.encode()), seed]).standard_normal(out[name].shape)
        drawn = base * np.exp(spread * noise) if base else spread * noise
        out[name] = __import__('jax').numpy.asarray(drawn.astype(out[name].dtype))
    for name, factor in factors.items():
        out[name] = (out[name] * factor).astype(out[name].dtype)
    return out
```

```python
from contextlib import ExitStack, contextmanager

import numpy as np
import concourse.bass as bass
from concourse import mybir

P = 128
DM = 1024
SEQ = 1024
NSEQ, TQ = 8, 8
NS = NSEQ * TQ
PAST, PAGE = 2048, 128
NPAGE = PAST // PAGE
NH, DN, DR, DV = 8, 64, 32, 64
DQ = DN + DR
QL, KL = 384, 256
CC, CK = 512, 31
HIST = CK - 1
INW = QL + KL + DR + 2 * CC
DFF = 2816
PLE = 256
EPS = 1e-6
SCALE = 1.0 / float(np.sqrt(np.float32(DN + DR)))
NEG = -1e30
TILES = SEQ // P
NT = TILES + 1
NTOK = SEQ + NS
KC = DM // P
LC = KL // P
CCH = CC // P
HALF = 512
GROUPS = DFF // (2 * P)
BLOCKS = [(0, 384), (384, 384), (768, 320)]

F32 = mybir.dt.float32
I32 = mybir.dt.int32
ALU = mybir.AluOpType
ACT = mybir.ActivationFunctionType
AXX = mybir.AxisListType.X

COLS = {}
for _n, _k in (("norm_mix", 8), ("norm_out_attn", 4), ("norm_out_conv", 4), ("norm_ffn", 8),
               ("norm_ple", 8), ("conv_b", 4)):
    COLS[_n] = (sum(k for _, k in COLS.values()), _k)
NCOL = sum(k for _, k in COLS.values())


class Chain:

    def __init__(self, eng, sem):
        self.eng, self.sem, self.base, self.n = eng, sem, 0, 0

    def link(self, ins):
        self.n += 1
        ins.then_inc(self.sem, 1)
        self.eng.wait_ge(self.sem, self.base + self.n)

    @contextmanager
    def loop(self, count, per):
        before = self.n
        with self.eng.Fori(0, count) as i:
            self.base, self.n = i * per + before, 0
            yield i
            assert self.n == per, f"a loop's body links {self.n}"
        self.base, self.n = 0, before + count * per


def build(nc, A, O):
    ctx = ExitStack()
    with ctx:
        ctx.enter_context(nc.allow_non_contiguous_dma("weights by slices, gains broadcast"))
        def sb(name, shape, dt=F32):
            return ctx.enter_context(nc.sbuf_tensor(name, shape, dt))

        def sem(name):
            return ctx.enter_context(nc.semaphore(name))

        ident = sb("ident", [P, P])
        causal = sb("causal", [P, P])
        self_mask = sb("self_mask", [NS, NS])
        mhalf = sb("mhalf", [P, 4 * NH])
        inv_n = sb("inv_n", [P, 3 + 3 * NH])
        gcol = sb("gcol", [P, NCOL])
        g_q = sb("g_q", [P, QL])
        g_kv = sb("g_kv", [P, KL])
        g_kpe = sb("g_kpe", [P, DR])
        g_qn = sb("g_qn", [P, DN])
        g_qpe = sb("g_qpe", [P, DR])
        ckv_keep = sb("ckv_keep", [NS, KL])
        rope = sb("rope", [P, NT, DR])
        tapw = sb("tapw", [P, CCH, CK])
        table = sb("table", [1, NSEQ * NPAGE], I32)
        w_uk = sb("w_uk", [P, LC, NH * DN])
        w_uv = sb("w_uv", [P, LC, NH * DV])
        stats = sb("stats", [P, 160])
        glu_s = sb("glu_s", [P, CCH, NSEQ, HIST + TQ])
        qT_s = sb("qT_s", [DQ, NH, NS])
        kT_s = sb("kT_s", [DQ, NH, NS])
        arena_cols = 46720
        arena = sb("arena", [P, arena_cols])

        class Region:
            def __init__(self, start):
                self.at = start

            def take(self, *shape, rows=P):
                n = int(np.prod(shape))
                v = arena[0:rows, self.at:self.at + n]
                self.at += n
                assert self.at <= arena_cols, (self.at, arena_cols)
                if len(shape) == 2:
                    v = v.rearrange("p (a b) -> p a b", b=shape[1])
                if len(shape) == 3:
                    v = v.rearrange("p (a b c) -> p a b c", b=shape[1], c=shape[2])
                if len(shape) == 4:
                    v = v.rearrange("p (a b c d) -> p a b c d", b=shape[1], c=shape[2], d=shape[3])
                return v

        R = Region(0)
        qT = R.take(NH, SEQ, rows=DQ)
        kT = R.take(NH, SEQ, rows=DQ)
        V = R.take(TILES, NH * DV)
        glu = R.take(CCH, HIST + SEQ)
        shared_end = R.at
        w_in = R.take(KC, INW)
        w_uq = R.take(QL // P, NH * DQ)
        x_in = [R.take(DM), R.take(DM)]
        hT = R.take(KC, P)
        x_scr = hT.rearrange("p a n -> p (a n)")
        sq = x_scr[:, 0:2 * QL].rearrange("p (a n) -> p a n", a=2)
        tap_rows = x_scr[0:CK, 0:CC]
        hist = x_in[1].rearrange("p (a n) -> p a n", a=2)
        ckvn = R.take(KL)
        kr = R.take(DR)
        kn = R.take(DR)
        rk = R.take(4, DR // 2)
        glu_t = R.take(CC)
        sig = glu_t
        gain_rows = glu_t[0:NCOL, 0:P]
        g_kn = glu_t[:, P:P + DN]
        cT = R.take(5, P)
        qh = R.take(NH, DQ)
        z_scr = qh.rearrange("p a n -> p (a n)")
        cqn = z_scr[:, 0:QL]
        kh = R.take(NH, DQ)
        k_scr = kh.rearrange("p a n -> p (a n)")
        rt = k_scr[:, 0:4 * NH * DR // 2].rearrange("p (a b c) -> p a b c", a=4, c=DR // 2)
        R = Region(shared_end)
        attn_tok = R.take(NT, NH * DV)
        conv_tok = R.take(NT, CC)
        b_keep_end = R.at
        qTh = [R.take(SEQ, rows=DQ), R.take(SEQ, rows=DQ)]
        prob = [R.take(SEQ), R.take(SEQ)]
        pT = R.take(SEQ)
        y_c = R.take(SEQ)
        y_s = R.take(NSEQ, TQ)
        R = Region(0)
        pages = [R.take(NPAGE + 1, KL + 1), R.take(NPAGE + 1, KL + 1)]
        kpe = [R.take(NPAGE, DR), R.take(NPAGE, DR)]
        s_tok = [R.take(NPAGE + 1, NS), R.take(NPAGE + 1, NS)]
        assert R.at <= 2 * NH * SEQ
        R = Region(b_keep_end)
        p_tok = R.take(NPAGE + 1, NS)
        w_ukT = R.take(NH, KL, rows=DN)
        q_abs = R.take(LC, NH, NS)
        q_pe = R.take(NH, NS, rows=DR)
        s_self = R.take(NH, NSEQ, TQ)
        cT_ring = [R.take(LC, P), R.take(LC, P)]
        kpeT_ring = [R.take(P, rows=DR), R.take(P, rows=DR)]
        ksq = [R.take(NH * DN), R.take(NH * DN)]
        ms_k = R.take(NPAGE, NH)
        rstd_k = R.take(NPAGE, NH)
        s_part = R.take(4, NH, TQ)
        m_part = R.take(NS)
        m_row = R.take(P)
        o_lat = R.take(KL)
        oT_lat = R.take(LC, NH, NSEQ, TQ)
        R = Region(0)
        x2 = R.take(NT, DM)
        hT2 = R.take(KC, NTOK)
        c_end = R.at
        assert c_end <= shared_end, (c_end, shared_end)
        R = Region(b_keep_end)
        w_out = R.take(KC, DM)
        mixn = R.take(DM)
        mT = R.take(KC, P)
        conv_n = R.take(CC)
        ln_g = R.take(CC)
        ln_b = R.take(CC)
        xn2 = R.take(DM)
        R = Region(c_end)
        wg = [R.take(KC, P), R.take(KC, P)]
        wu = [R.take(KC, P), R.take(KC, P)]
        f_at = R.at
        xr = [R.take(DM), R.take(DM)]
        assert R.at <= shared_end
        R = Region(shared_end)
        wd = R.take(2, DM)
        aT = [R.take(NTOK), R.take(NTOK)]
        gate_s = R.take(3, 384)
        w_pg = R.take(KC, DM)
        w_pp = R.take(PLE // P, DM)
        sg = R.take(DM)
        y_out = [R.take(DM), R.take(DM)]
        xn4 = R.take(DM)
        junk4 = R.take(DM)
        R = Region(f_at)
        p_in = [R.take(PLE), R.take(PLE)]
        p_T = R.take(PLE // P, P)
        hT4 = R.take(KC, P)
        assert R.at <= shared_end

        ps = ctx.enter_context(nc.psum_tensor("ps", [P, 8, 512], F32))

        S = {}

        def s_(name):
            if name not in S:
                S[name] = sem(name)
            return S[name]

        win_v = A["w_in"][0].rearrange("(k p) n -> p k n", p=P)
        xp_v = A["x_prompt"][0].rearrange("(t p) n -> t p n", p=P)
        xs_v = A["x_sample"].rearrange("b q n -> (b q) n")
        st = lambda a, n=1: stats[:, a:a + n]
        HD2 = DR // 2

        def pairs(chain, per):
            def run(tile):
                with chain.loop(TILES // 2, per) as p:
                    for s in range(2):
                        tile(2 * p + s, s, P, p)
                tile(TILES, 0, NS, TILES // 2)
            return run

        def nt_act(act, stage, n, src, rows, col, scratch):
            nc.scalar.activation(scratch[0:rows, :], src, ACT.Square,
                                 accum_out=st(col)[0:rows]).then_inc(s_(stage + "_sumsq"), 1)

        def nt_dve_scale(dve, stage, n, src, rows, col, out):
            dve.wait_ge(s_(stage + "_sumsq"), n)
            nc.vector.tensor_scalar(st(col + 1)[0:rows], st(col)[0:rows], 1.0 / DM, EPS, ALU.mult,
                                    ALU.add).then_inc(s_(stage + "_ms"), 1)
            dve.wait_ge(s_(stage + "_rstd"), n)
            nc.vector.tensor_scalar(out[0:rows, :], src, st(col + 2)[0:rows], None,
                                    ALU.mult).then_inc(s_(stage + "_xn"), 1)

        def nt_pool(pool, stage, n, rows, col):
            pool.wait_ge(s_(stage + "_ms"), n)
            nc.gpsimd.tensor_tensor(st(col + 2)[0:rows], st(col + 1)[0:rows], mhalf[0:rows, 0:1],
                                    ALU.pow).then_inc(s_(stage + "_rstd"), 1)

        def nt_pe(pe, stage, n, rows, src, bank):
            pe.wait_ge(s_(stage + "_xn"), n)
            for k in range(KC):
                last = nc.tensor.transpose(ps[:, bank + k // 4, (k % 4) * P:(k % 4) * P + rows],
                                           src[0:rows, k * P:(k + 1) * P], ident[0:rows, 0:rows])
            last.then_inc(s_(stage + "_xT"), 1)

        def nt_dve_gain(dve, stage, n, rows, bank, gain, out):
            dve.wait_ge(s_(stage + "_xT"), n)
            g0 = COLS[gain][0] if isinstance(gain, str) else gain
            for b in range(2):
                src = ps[:, bank + b, :].rearrange("p (k c) -> p k c", c=P)[:, :, 0:rows]
                g = gcol[:, g0 + 4 * b:g0 + 4 * b + 4].unsqueeze(2).to_broadcast([P, 4, rows])
                last = nc.vector.tensor_tensor(out[:, 4 * b:4 * b + 4, :], src, g, ALU.mult)
            last.then_inc(s_(stage + "_hT"), 1)

        T0, T1, Z0, Z1, Z2, Z3, P0, P1 = 0, 1, 2, 3, 4, 5, 6, 7
        c_scr = ps[:, 6:8, :].rearrange("p a n -> p (a n)")
        block = ctx.enter_context(nc.Block())

        @block.sync
        def _(sp):
            col = 0
            for name in COLS:
                c0, k = COLS[name]
                sp.dma_start(gain_rows[c0:c0 + k, :], A[name][0].rearrange("(k p) -> k p", p=P)).then_inc(s_("consts"), 16)
            sp.dma_start(tap_rows, A["conv_w"][0]).then_inc(s_("consts"), 16)
            sp.dma_start(x_in[0], xp_v[0]).then_inc(s_("x_loaded0"), 16)
            sp.dma_start(x_in[1], xp_v[1]).then_inc(s_("x_loaded1"), 16)
            for k in range(KC):
                sp.dma_start(w_in[:, k, :], win_v[:, k, :]).then_inc(s_("w_in_loaded"), 16)
            sp.dma_start(w_uq, A["w_uq"][0].rearrange("(k p) n -> p k n", p=P)).then_inc(s_("w_u_loaded"), 16)
            sp.dma_start(w_uk[:, :, :], A["w_uk"][0].rearrange("(k p) n -> p k n", p=P)).then_inc(s_("w_u_loaded"), 16)
            sp.dma_start(w_uv[:, :, :], A["w_uv"][0].rearrange("(k p) n -> p k n", p=P)).then_inc(s_("w_u_loaded"), 16)

            def tile_a(t, s, rows, p):
                out_ckv = O[2][0, 0, bass.ds(t * P, P), :] if rows == P else O[5][0].rearrange("b q n -> (b q) n")
                out_kpe = O[3][0, 0, bass.ds(t * P, P), :] if rows == P else O[6][0].rearrange("b q n -> (b q) n")
                sp.wait_ge(s_("lat_ready"), t + 1)
                sp.dma_start(out_ckv, ckvn[0:rows, :]).then_inc(s_("lat_stored"), 16)
                sp.wait_ge(s_("kpe_ready"), t + 1)
                sp.dma_start(out_kpe, kr[0:rows, :]).then_inc(s_("lat_stored"), 16)

            with sp.Fori(0, TILES // 2 - 1) as p:
                for s in range(2):
                    tile_a(2 * p + s, s, P, p)
                    sp.wait_ge(s_("a_xT"), 2 * p + s + 1)
                    sp.dma_start(x_in[s], xp_v[bass.ds(2 * p + s + 2, 1)].rearrange("a p n -> (a p) n")).then_inc(s_(f"x_loaded{s}"), 16)
            sp.wait_ge(s_("a_xT"), TILES - 1)
            sp.dma_start(x_in[0][0:NS, :], xs_v).then_inc(s_("x_loaded0"), 16)
            for t in range(TILES - 2, TILES + 1):
                tile_a(t, t % 2, P if t < TILES else NS, t // 2)
                if t == TILES - 1:
                    for a in range(2):
                        sp.dma_start(hist[0:120, a, :], A["state_conv"][0, 4 * a:4 * a + 4].rearrange("b n c -> (b n) c")).then_inc(s_("hist_loaded"), 16)
                    sp.wait_ge(s_("glu_ready"), TILES)
                    sp.dma_start(O[4][0, 0], glu_t[P - HIST:P, :]).then_inc(s_("tail_stored"), 16)
            sp.wait_ge(s_("glu_ready"), NT)
            for b in range(NSEQ):
                sp.dma_start(O[7][0, b, HIST - TQ:HIST, :], glu_t[b * TQ:(b + 1) * TQ, :]).then_inc(s_("out_stored"), 16)
            sp.dma_start(O[7][0, :, 0:HIST - TQ, :], A["state_conv"][0, :, TQ:HIST, :]).then_inc(s_("out_stored"), 16)

            sp.wait_ge(s_("b_done"), 1)
            sp.wait_ge(s_("b_ones"), 1)
            sp.wait_ge(s_("table_loaded"), 16)

            def load_pages(b, s):
                for g in range(NPAGE):
                    idx = sp.value_load(table[0:1, bass.ds(b * NPAGE + g, 1)], min_val=0, max_val=A["cache_ckv"].shape[1] - 1)
                    sp.dma_start(pages[s][:, g, 0:KL], A["cache_ckv"][0, bass.ds(idx, 1)].rearrange("a p n -> (a p) n")).then_inc(s_(f"pages_loaded{s}"), 16)
                    sp.dma_start(kpe[s][:, g, :], A["cache_kpe"][0, bass.ds(idx, 1)].rearrange("a p n -> (a p) n")).then_inc(s_(f"pages_loaded{s}"), 16)
            for s in range(2):
                load_pages(s, s)
            with sp.Fori(0, NSEQ // 2 - 1) as p:
                for s in range(2):
                    sp.wait_ge(s_("pv_s_done"), 2 * p + s + 1)
                    load_pages(2 * p + s + 2, s)

            sp.wait_ge(s_("s_done"), 1)
            sp.dma_start(w_out, A["w_out"][0].rearrange("(k p) n -> p k n", p=P)).then_inc(s_("w_out_loaded"), 16)
            for dst, name in ((ln_g, "conv_ln_g"), (ln_b, "conv_ln_b")):
                sp.dma_start(dst, A[name][0].partition_broadcast(P)).then_inc(s_("ln_loaded"), 16)
            for s in range(2):
                sp.dma_start(xr[s], xp_v[s]).then_inc(s_(f"xr_loaded{s}"), 16)
            wg_v = A["w_gate"][0].rearrange("(k p) n -> p k n", p=P)
            wu_v = A["w_up"][0].rearrange("(k p) n -> p k n", p=P)
            wd_v = A["w_down"][0].rearrange("(f p) n -> p f n", p=P)

            def load_gu(f, s):
                sp.dma_start(wg[s], wg_v[:, :, bass.ds(f * P, P)]).then_inc(s_(f"gu_loaded{s}"), 16)
                sp.dma_start(wu[s], wu_v[:, :, bass.ds(f * P, P)]).then_inc(s_(f"gu_loaded{s}"), 16)
            for s in range(2):
                load_gu(s, s)
            with sp.Fori(0, TILES // 2 - 1) as p:
                for s in range(2):
                    sp.wait_ge(s_("x2_ready"), 2 * p + s + 1)
                    sp.dma_start(xr[s], xp_v[bass.ds(2 * p + s + 2, 1)].rearrange("a p n -> (a p) n")).then_inc(s_(f"xr_loaded{s}"), 16)
            sp.wait_ge(s_("x2_ready"), TILES - 1)
            sp.dma_start(xr[0][0:NS, :], xs_v).then_inc(s_("xr_loaded0"), 16)

            sp.wait_ge(s_("c_hT"), NT)
            sp.dma_start(wd, wd_v[:, 0:2, :]).then_inc(s_("wd_loaded"), 16)
            with sp.Fori(0, GROUPS - 1) as g:
                for s in range(2):
                    sp.wait_ge(s_("up_done"), 6 * g + 3 * s + 3)
                    load_gu(2 * g + s + 2, s)
                sp.wait_ge(s_("dn_done"), 2 * NT * (g + 1))
                sp.dma_start(wd, wd_v[:, bass.ds(2 * g + 2, 2), :]).then_inc(s_("wd_loaded"), 16)

            pp_v = A["p_prompt"][0, 0].rearrange("(t p) n -> t p n", p=P)
            ps_v = A["p_sample"][0].rearrange("b q n -> (b q) n")
            yp_v = O[0][0].rearrange("(t p) n -> t p n", p=P)
            sp.dma_start(w_pg, A["w_ple_gate"][0].rearrange("(k p) n -> p k n", p=P)).then_inc(s_("w_d_loaded"), 16)
            sp.dma_start(w_pp, A["w_ple_proj"][0].rearrange("(k p) n -> p k n", p=P)).then_inc(s_("w_d_loaded"), 16)
            for s in range(2):
                sp.dma_start(p_in[s], pp_v[s]).then_inc(s_(f"p_loaded{s}"), 16)

            def store_y(t, s):
                sp.wait_ge(s_("y_ready"), t + 1)
                sp.dma_start(yp_v[bass.ds(t, 1)].rearrange("a p n -> (a p) n"), y_out[s]).then_inc(s_(f"y_stored{s}"), 16)
            with sp.Fori(0, TILES // 2 - 1) as p:
                for s in range(2):
                    store_y(2 * p + s, s)
                    sp.dma_start(p_in[s], pp_v[bass.ds(2 * p + s + 2, 1)].rearrange("a p n -> (a p) n")).then_inc(s_(f"p_loaded{s}"), 16)
            store_y(TILES - 2, 0)
            sp.dma_start(p_in[0][0:NS, :], ps_v).then_inc(s_("p_loaded0"), 16)
            store_y(TILES - 1, 1)
            sp.wait_ge(s_("y_ready"), NT)
            sp.dma_start(O[1].rearrange("b q n -> (b q) n"), y_out[0][0:NS, :]).then_inc(s_("y_stored0"), 16)
            sp.wait_ge(s_("y_stored0"), 16 * (TILES // 2 + 1))
            sp.wait_ge(s_("y_stored1"), 16 * (TILES // 2))
            sp.wait_ge(s_("lat_stored"), 32 * NT)
            sp.wait_ge(s_("tail_stored"), 16)
            sp.wait_ge(s_("out_stored"), 16 * (NSEQ + 1))

        @block.gpsimd
        def _(pool):
            ch = Chain(pool, s_("pool_own"))
            ch.link(nc.gpsimd.memset(ident[:, :], 0.0))
            nc.gpsimd.affine_select(out=ident[:, :], in_=ident[:, :], compare_op=ALU.not_equal, fill=1.0,
                                    base=0, pattern=[[-1, P]], channel_multiplier=1).then_inc(s_("ident_ready"), 1)
            nc.gpsimd.memset(mhalf[:, :], -0.5)
            for i, n in enumerate((QL, KL, DR)):
                nc.gpsimd.memset(inv_n[:, i:i + 1], 1.0 / n)
            nc.gpsimd.memset(inv_n[:, 3:3 + NH], 1.0 / DN)
            nc.gpsimd.memset(inv_n[:, 3 + NH:3 + 2 * NH], 1.0 / DR)
            ch.link(nc.gpsimd.memset(inv_n[:, 3 + 2 * NH:3 + 3 * NH], 1.0 / DN))
            nc.gpsimd.memset(glu[:, :, 0:HIST], 0.0)
            ch.link(nc.gpsimd.memset(causal[:, :], 0.0))
            nc.gpsimd.affine_select(out=causal[:, :], in_=causal[:, :], compare_op=ALU.is_ge, fill=NEG,
                                    base=0, pattern=[[-1, P]], channel_multiplier=1)
            ch.link(nc.gpsimd.memset(self_mask[:, :], 0.0))
            sm = self_mask[:, :].rearrange("p (b q) -> p b q", q=TQ)
            ch.link(nc.gpsimd.affine_select(out=sm, in_=sm, compare_op=ALU.is_ge, fill=NEG, base=0,
                                            pattern=[[TQ, NSEQ], [1, TQ]], channel_multiplier=-1))
            nc.gpsimd.affine_select(out=sm, in_=sm, compare_op=ALU.is_ge, fill=NEG, base=0,
                                    pattern=[[-TQ, NSEQ], [0, TQ]], channel_multiplier=1).then_inc(s_("pool_consts"), 1)

            for dst, name in ((g_q, "q_lora_norm"), (g_kv, "kv_norm"), (g_kpe, "k_pe_norm"), (g_qn, "q_nope_norm"),
                              (g_kn, "k_nope_norm"), (g_qpe, "q_pe_norm")):
                pool.dma_start(dst[0:P], A[name][0].partition_broadcast(P)).then_inc(s_("gains"), 16)
            pool.dma_start(rope[:, 0:TILES, :], A["rope"][0:SEQ, :].rearrange("(t p) n -> p t n", p=P)).then_inc(s_("gains"), 16)
            pool.dma_start(rope[0:NS, TILES, :], A["rope"][SEQ:NTOK, :]).then_inc(s_("gains"), 16)
            pool.dma_start(table[:, :], A["page_table"].rearrange("b g -> (b g)").unsqueeze(0)).then_inc(s_("table_loaded"), 16)

            def tile_a(t, s, rows, p):
                nt_pool(pool, "a", t + 1, rows, 0)
                pool.wait_ge(s_("msz_ready"), t + 1)
                nc.gpsimd.tensor_tensor(st(16, 3)[0:rows], st(12, 3)[0:rows], mhalf[0:rows, 0:3], ALU.pow).then_inc(s_("rstd_z"), 1)
                pool.wait_ge(s_("msq_ready"), t + 1)
                nc.gpsimd.tensor_tensor(st(80, 24)[0:rows], st(50, 24)[0:rows], mhalf[0:rows, 0:24], ALU.pow).then_inc(s_("rstd_q"), 1)
            pairs(ch, 0)(tile_a)

            pool.wait_ge(s_("b_done"), 1)
            for s in range(2):
                ch.link(nc.gpsimd.memset(pages[s][:, :, KL:KL + 1], 1.0))
            ch.link(nc.gpsimd.memset(s_self[64:P, :, :, :], NEG))
            ch.link(nc.gpsimd.memset(pages[0][:, NPAGE, 0:KL], 0.0))
            ch.link(nc.gpsimd.memset(pages[1][:, NPAGE, 0:KL], 0.0))
            pool.wait_ge(s_("ckv_kept"), 1)
            for s in range(2):
                last = nc.gpsimd.tensor_copy(pages[s][0:NS, NPAGE, 0:KL], ckv_keep[:, :])
            last.then_inc(s_("b_ones"), 1)
            with ch.loop(NSEQ, 0) as b:
                for q in range(4):
                    pool.wait_ge(s_("msk_ready"), 4 * b + q + 1)
                    nc.gpsimd.tensor_tensor(rstd_k[:, 4 * q:4 * q + 4, :], ms_k[:, 4 * q:4 * q + 4, :],
                                            mhalf[:, 0:4 * NH].rearrange("p (g h) -> p g h", h=NH), ALU.pow).then_inc(s_("rstdk_ready"), 1)

            def tile_c(t, s, rows, p):
                pool.wait_ge(s_("var_ready"), t + 1)
                nc.gpsimd.tensor_tensor(st(6)[0:rows], st(7)[0:rows], mhalf[0:rows, 0:1], ALU.pow).then_inc(s_("rstd_ln"), 1)
                pool.wait_ge(s_("msm_ready"), t + 1)
                nc.gpsimd.tensor_tensor(st(22, 2)[0:rows], st(20, 2)[0:rows], mhalf[0:rows, 0:2], ALU.pow).then_inc(s_("rstd_m"), 1)
                nt_pool(pool, "c", t + 1, rows, 0)
            pairs(ch, 0)(tile_c)

            pairs(ch, 0)(lambda t, s, rows, p: nt_pool(pool, "d", t + 1, rows, 0))

        @block.scalar
        def _(act):
            ch = Chain(act, s_("act_own"))
            act.wait_ge(s_("pool_consts"), 1)
            act.wait_ge(s_("colT_done"), 1)

            def tile_a(t, s, rows, p):
                act.wait_ge(s_(f"x_loaded{s}"), 16 * (p + 1))
                nt_act(act, "a", t + 1, x_in[s][0:rows, :], rows, 0, x_scr)
                act.wait_ge(s_("z_lat_done"), t + 1)
                nc.scalar.activation(z_scr[0:rows, 0:QL], ps[0:rows, Z0, 0:QL], ACT.Square, accum_out=st(8)[0:rows])
                nc.scalar.activation(z_scr[0:rows, QL:QL + KL], ps[0:rows, Z1, 0:KL], ACT.Square, accum_out=st(9)[0:rows])
                nc.scalar.activation(z_scr[0:rows, QL + KL:QL + KL + DR], ps[0:rows, Z1, KL:KL + DR], ACT.Square,
                                     accum_out=st(10)[0:rows]).then_inc(s_("z_sumsq"), 1)
                act.wait_ge(s_("z_glu_done"), t + 1)
                nc.scalar.activation(sig[0:rows, :], ps[0:rows, Z3, :], ACT.Sigmoid).then_inc(s_("sig_ready"), 1)
                act.wait_ge(s_("cT_done"), t + 1)
                nc.scalar.activation(cT[:, 0:4, 0:rows], ps[:, T0, :].rearrange("p (k c) -> p k c", c=P)[:, :, 0:rows], ACT.Copy)
                nc.scalar.activation(cT[:, 4, 0:rows], ps[:, T1, 0:rows], ACT.Copy).then_inc(s_("cT_ready"), 1)
                act.wait_ge(s_("gluT_done"), t + 1)
                src = ps[:, Z2, :].rearrange("p (k c) -> p k c", c=P)[:, :, 0:rows]
                if rows == P:
                    nc.scalar.activation(glu[:, :, bass.ds(HIST + t * P, P)], src, ACT.Copy)
                else:
                    for c in range(CCH):
                        nc.scalar.activation(glu_s[:, c, :, HIST:HIST + TQ], src[:, c, :].rearrange("p (b q) -> p b q", q=TQ), ACT.Copy)
                act.wait_ge(s_("q_done"), t + 1)
                nc.scalar.activation(sq[0:rows, :, :], ps[0:rows, P0:P0 + 2, 0:QL], ACT.Square).then_inc(s_("q_sq"), 1)
                act.wait_ge(s_("kv_done"), t + 1)
                nc.scalar.activation(k_scr[0:rows, 0:NH * DN], ps[0:rows, Z0, :], ACT.Square).then_inc(s_("k_sq"), 1)
                if rows == P:
                    nc.scalar.activation(V[:, bass.ds(t, 1), :], ps[:, Z1, :].unsqueeze(1), ACT.Copy)
                act.wait_ge(s_("qT_done"), t + 1)
                src = ps[0:DQ, T0:T0 + 2, :].rearrange("p a (k c) -> p (a k) c", c=P)[:, :, 0:rows]
                dst = qT[:, :, bass.ds(t * P, P)] if rows == P else qT_s[:, :, :]
                nc.scalar.activation(dst, src, ACT.Copy).then_inc(s_("qT_ready"), 1)
            pairs(ch, 0)(tile_a)
            act.wait_ge(s_("hist_done"), 1)
            for a in range(2):
                last = nc.scalar.activation(glu_s[:, :, 4 * a:4 * a + 4, 0:HIST],
                                            ps[:, Z2 + a, 0:CCH * 120].rearrange("p (c b n) -> p c b n", b=4, n=HIST), ACT.Copy)
            last.then_inc(s_("hist_ready"), 1)

            act.wait_ge(s_("kT_ready"), NT)
            with ch.loop(NH // 2, 0) as c:
                for hp in range(2):
                    nc.scalar.activation(qTh[hp], qT[:, bass.ds(2 * c + hp, 1), :].rearrange("p a n -> p (a n)"), ACT.Copy)\
                        .then_inc(s_("qTh_ready"), 1)

                def expo(m):
                    n = (m % 8 + 1) * P
                    act.wait_ge(s_("nmax_ready"), 16 * c + m + 1)
                    if m >= 2:
                        act.wait_ge(s_("pv_done"), 16 * c + m - 1)
                    nc.scalar.activation(prob[m % 2][:, 0:n], ps[:, 2 * (m % 2):2 * (m % 2) + 2, :].rearrange("p a n -> p (a n)")[:, 0:n],
                                         ACT.Exp, bias=st(120 + m), accum_out=st(136 + m)).then_inc(s_("prob_ready"), 1)
                expo(0)
                for m in range(16):
                    if m < 15:
                        expo(m + 1)
                    i = m % 8
                    if i >= 4:
                        act.wait_ge(s_("ptB_done"), 8 * c + 4 * (m // 8) + i - 3)
                        nc.scalar.activation(pT[:, 512:(i + 1) * P], ps[:, 5, 0:(i - 3) * P], ACT.Copy).then_inc(s_("ptB_ready"), 1)
                act.wait_ge(s_("yT_done"), c + 1)
                nc.scalar.activation(conv_tok[:, 0:TILES, bass.ds(c * P, P)],
                                     ps[:, 0:2, :].rearrange("p a (k c) -> p (a k) c", c=P), ACT.Copy)
                nc.scalar.activation(conv_tok[0:NS, TILES, bass.ds(c * P, P)], ps[0:NS, 4, 0:P], ACT.Copy).then_inc(s_("yT_ready"), 1)

            act.wait_ge(s_("wukT_done"), 1)
            nc.scalar.activation(w_ukT, ps[0:DN, 0:4, :].rearrange("p a (h c) -> p (a h) c", c=KL), ACT.Copy)
            nc.scalar.activation(q_pe, qT_s[DN:DQ, :, :], ACT.Copy).then_inc(s_("wukT_ready"), 1)
            act.wait_ge(s_("qabs_done"), 1)
            nc.scalar.activation(q_abs, ps[:, 4:4 + LC, :].rearrange("p a (h n) -> p a h n", h=NH), ACT.Copy).then_inc(s_("qabs_ready"), 1)

            def soft_exp(b, s):
                act.wait_ge(s_("s_shift"), b + 1)
                nc.scalar.activation(p_tok, s_tok[s], ACT.Exp).then_inc(s_("ptok_ready"), 1)

            def seq_act(b, s, prev):
                for g in range(NPAGE):
                    r = g % 2
                    act.wait_ge(s_("ctr_done"), NPAGE * b + g + 1)
                    nc.scalar.activation(cT_ring[r], ps[:, r, 0:LC * P].rearrange("p (k c) -> p k c", c=P), ACT.Copy)
                    nc.scalar.activation(kpeT_ring[r], ps[0:DR, r, LC * P:LC * P + P], ACT.Copy).then_inc(s_("ctr_ready"), 1)
                    act.wait_ge(s_("k_done"), NPAGE * b + g + 1)
                    if g >= 2 or prev:
                        act.wait_ge(s_("ksum_done"), NPAGE * b + g - 1)
                    nc.scalar.activation(ksq[r], ps[:, 2 + r, :], ACT.Square).then_inc(s_("ksq_ready"), 1)
                    if g == 9 and prev:
                        soft_exp(b - 1, 1 - s)
            seq_act(0, 0, False)
            seq_act(1, 1, True)
            with ch.loop(NSEQ // 2 - 1, 0) as p:
                for s in range(2):
                    seq_act(2 * p + s + 2, s, True)
            soft_exp(NSEQ - 1, 1)
            act.wait_ge(s_("ov_done"), 1)
            nc.scalar.activation(attn_tok[0:NS, TILES, :], ps[0:NS, 0, :], ACT.Copy).then_inc(s_("s_done"), 1)

            def tile_c(t, s, rows, p):
                act.wait_ge(s_("centred"), t + 1)
                nc.scalar.activation(c_scr[0:rows, CC:2 * CC], conv_n[0:rows, :], ACT.Square, accum_out=st(24)[0:rows]).then_inc(s_("var_sumsq"), 1)
                nc.scalar.activation(c_scr[0:rows, 0:CC], attn_tok[0:rows, bass.ds(t, 1), :].rearrange("p a n -> p (a n)"),
                                     ACT.Square, accum_out=st(16)[0:rows])
                act.wait_ge(s_("ln_ready"), t + 1)
                ch.link(nc.scalar.activation(conv_n[0:rows, :], conv_n[0:rows, :], ACT.Silu))
                nc.scalar.activation(c_scr[0:rows, CC:2 * CC], conv_n[0:rows, :], ACT.Square,
                                     accum_out=st(17)[0:rows]).then_inc(s_("mix_sumsq"), 1)
                act.wait_ge(s_("x2_ready"), t + 1)
                nt_act(act, "c", t + 1, x2[0:rows, bass.ds(t, 1), :].rearrange("p a n -> p (a n)"), rows, 0, c_scr)
            act.wait_ge(s_("s_done"), 1)
            with ch.loop(TILES // 2, 2) as p:
                for s in range(2):
                    tile_c(2 * p + s, s, P, p)
            tile_c(TILES, 0, NS, TILES // 2)

            with ch.loop(GROUPS, 0) as g:
                for s in range(2):
                    for b, (at, n) in enumerate(BLOCKS):
                        act.wait_ge(s_("gate_done"), 6 * g + 3 * s + b + 1)
                        nc.scalar.activation(gate_s[:, b, 0:n], ps[:, 2 * b, 0:n], ACT.Silu).then_inc(s_("silu_ready"), 1)

            act.wait_ge(s_("dn_evac"), 2 * NT * GROUPS)

            def tile_d(t, s, rows, p):
                nt_act(act, "d", t + 1, x2[0:rows, bass.ds(t, 1), :].rearrange("p a n -> p (a n)"), rows, 0, junk4)
                act.wait_ge(s_("ppT_done"), t + 1)
                nc.scalar.activation(p_T[:, :, 0:rows], ps[:, 2, 0:2 * P].rearrange("p (k c) -> p k c", c=P)[:, :, 0:rows], ACT.Copy)\
                    .then_inc(s_("ppT_ready"), 1)
                act.wait_ge(s_("pg_done"), t + 1)
                nc.scalar.activation(sg[0:rows, :], ps[0:rows, 3:5, :].rearrange("p a n -> p (a n)"), ACT.Sigmoid).then_inc(s_("sg_ready"), 1)
            pairs(ch, 0)(tile_d)

        @block.vector
        def _(dve):
            ch = Chain(dve, s_("dve_own"))
            dve.wait_ge(s_("gains"), 16 * 8)
            dve.wait_ge(s_("pool_consts"), 1)
            ch.link(nc.vector.tensor_tensor(g_qn[:, :], g_qn[:, :], g_kn[:, :], ALU.mult))
            ch.link(nc.vector.tensor_scalar(g_qn[:, :], g_qn[:, :], SCALE, None, ALU.mult))
            ch.link(nc.vector.tensor_scalar(g_qpe[:, :], g_qpe[:, :], SCALE, None, ALU.mult))
            dve.wait_ge(s_("colT_done"), 1)
            nc.vector.tensor_copy(gcol[:, :], ps[:, P0, 0:NCOL])
            ch.link(nc.vector.tensor_copy(tapw[:, :, :], ps[:, P1, 0:CCH * CK].rearrange("p (c k) -> p c k", k=CK)))

            def rotate(out1, out2, x1, x2_, cos, sin, a, b, c, d):
                nc.vector.tensor_tensor(a, x1, cos, ALU.mult)
                nc.vector.tensor_tensor(b, x2_, sin, ALU.mult)
                nc.vector.tensor_tensor(c, x2_, cos, ALU.mult)
                ch.link(nc.vector.tensor_tensor(d, x1, sin, ALU.mult))
                nc.vector.tensor_tensor(out1, a, b, ALU.subtract)
                return nc.vector.tensor_tensor(out2, c, d, ALU.add)

            def tile_a(t, s, rows, p):
                r = slice(0, rows)
                nt_dve_scale(dve, "a", t + 1, x_in[s][r, :], rows, 0, x_in[s])
                nt_dve_gain(dve, "a", t + 1, rows, T0, "norm_mix", hT[:, :, 0:rows])
                dve.wait_ge(s_("z_sumsq"), t + 1)
                ch.link(nc.vector.tensor_tensor(st(12, 3)[r], st(8, 3)[r], inv_n[r, 0:3], ALU.mult))
                nc.vector.tensor_scalar(st(12, 3)[r], st(12, 3)[r], EPS, None, ALU.add).then_inc(s_("msz_ready"), 1)
                dve.wait_ge(s_("rstd_z"), t + 1)
                nc.vector.scalar_tensor_tensor(cqn[r, :], ps[r, Z0, 0:QL], st(16)[r], g_q[r, :], ALU.mult, ALU.mult)
                ch.link(nc.vector.scalar_tensor_tensor(kn[r, :], ps[r, Z1, KL:KL + DR], st(18)[r], g_kpe[r, :], ALU.mult, ALU.mult))
                nc.vector.scalar_tensor_tensor(ckvn[r, :], ps[r, Z1, 0:KL], st(17)[r], g_kv[r, :], ALU.mult, ALU.mult).then_inc(s_("lat_ready"), 1)
                cos = rope[r, bass.ds(t, 1), 0:HD2].rearrange("p a n -> p (a n)")
                sin = rope[r, bass.ds(t, 1), HD2:DR].rearrange("p a n -> p (a n)")
                rotate(kr[r, 0:HD2], kr[r, HD2:DR], kn[r, 0:HD2], kn[r, HD2:DR], cos, sin,
                       *(rk[r, j, :] for j in range(4))).then_inc(s_("kpe_ready"), 1)
                dve.wait_ge(s_("sig_ready"), t + 1)
                nc.vector.tensor_tensor(glu_t[r, :], ps[r, Z2, :], sig[r, :], ALU.mult).then_inc(s_("glu_ready"), 1)
                dve.wait_ge(s_("q_sq"), t + 1)
                sqh = sq[r, :, :].rearrange("p a (h d) -> p (a h) d", d=DQ)
                nc.vector.reduce_sum(st(20, NH)[r], sqh[:, :, 0:DN], AXX)
                nc.vector.reduce_sum(st(28, NH)[r], sqh[:, :, DN:DQ], AXX)
                dve.wait_ge(s_("k_sq"), t + 1)
                ch.link(nc.vector.reduce_sum(st(36, NH)[r], k_scr[r, 0:NH * DN].rearrange("p (h d) -> p h d", d=DN), AXX))
                ch.link(nc.vector.tensor_tensor(st(50, 24)[r], st(20, 24)[r], inv_n[r, 3:27], ALU.mult))
                nc.vector.tensor_scalar(st(50, 24)[r], st(50, 24)[r], EPS, None, ALU.add).then_inc(s_("msq_ready"), 1)
                dve.wait_ge(s_("rstd_q"), t + 1)
                qv = ps[r, P0:P0 + 2, 0:QL].rearrange("p a (h d) -> p a h d", d=DQ)
                qh4 = qh[r, :, :].rearrange("p (a h) d -> p a h d", a=2)
                rq = st(80, NH)[r].rearrange("p (a h) -> p a h", a=2)
                rp = st(88, NH)[r].rearrange("p (a h) -> p a h", a=2)
                nc.vector.tensor_tensor(qh4[:, :, :, 0:DN], qv[:, :, :, 0:DN], rq.unsqueeze(3).to_broadcast([rows, 2, 4, DN]), ALU.mult)
                ch.link(nc.vector.tensor_tensor(qh4[:, :, :, DN:DQ], qv[:, :, :, DN:DQ], rp.unsqueeze(3).to_broadcast([rows, 2, 4, DR]), ALU.mult))
                nc.vector.tensor_tensor(qh[r, :, 0:DN], qh[r, :, 0:DN], g_qn[r, :].unsqueeze(1).to_broadcast([rows, NH, DN]), ALU.mult)
                ch.link(nc.vector.tensor_tensor(qh[r, :, DN:DQ], qh[r, :, DN:DQ], g_qpe[r, :].unsqueeze(1).to_broadcast([rows, NH, DR]), ALU.mult))
                cosb = rope[r, bass.ds(t, 1), 0:HD2].to_broadcast([rows, NH, HD2])
                sinb = rope[r, bass.ds(t, 1), HD2:DR].to_broadcast([rows, NH, HD2])
                rotate(qh[r, :, DN:DN + HD2], qh[r, :, DN + HD2:DQ], qh[r, :, DN:DN + HD2], qh[r, :, DN + HD2:DQ],
                       cosb, sinb, *(rt[r, j, :, :] for j in range(4))).then_inc(s_("qh_ready"), 1)
                dve.wait_ge(s_("qh_ready"), t + 1)
                nc.vector.tensor_tensor(kh[r, :, 0:DN], ps[r, Z0, :].rearrange("p (h d) -> p h d", d=DN),
                                        st(96, NH)[r].unsqueeze(2).to_broadcast([rows, NH, DN]), ALU.mult)
                dve.wait_ge(s_("kpe_ready"), t + 1)
                nc.vector.tensor_copy(kh[r, :, DN:DQ], kr[r, :].unsqueeze(1).to_broadcast([rows, NH, DR])).then_inc(s_("kh_ready"), 1)
                dve.wait_ge(s_("kT_done"), t + 1)
                src = ps[0:DQ, P0:P0 + 2, :].rearrange("p a (k c) -> p (a k) c", c=P)[:, :, 0:rows]
                dst = kT[:, :, bass.ds(t * P, P)] if rows == P else kT_s[:, :, :]
                nc.vector.tensor_copy(dst, src).then_inc(s_("kT_ready"), 1)
                dve.wait_ge(s_("lat_stored"), 32 * (t + 1))
            with ch.loop(TILES // 2, 2 * 8) as p:
                for s in range(2):
                    tile_a(2 * p + s, s, P, p)
            dve.wait_ge(s_("tail_stored"), 16)
            tile_a(TILES, 0, NS, TILES // 2)
            nc.vector.tensor_copy(ckv_keep[:, :], ckvn[0:NS, :]).then_inc(s_("ckv_kept"), 1)
            dve.wait_ge(s_("hist_ready"), 1)
            dve.wait_ge(s_("out_stored"), 16 * (NSEQ + 1))

            with ch.loop(NH // 2, 62) as c:
                def s_view(m):
                    return ps[:, 2 * (m % 2):2 * (m % 2) + 2, :].rearrange("p a n -> p (a n)")

                def row_max(m):
                    i = m % 8
                    dve.wait_ge(s_("scores_done"), 16 * c + m + 1)
                    d = s_view(m)[:, i * P:(i + 1) * P]
                    ch.link(nc.vector.tensor_tensor(d, d, causal[:, :], ALU.add))
                    nc.vector.tensor_reduce(st(120 + m), s_view(m)[:, 0:(i + 1) * P], AXX, ALU.max, negate=True).then_inc(s_("nmax_ready"), 1)

                def out_rows(m):
                    i = m % 8
                    dve.wait_ge(s_("pv_done"), 16 * c + m + 1)
                    ch.link(nc.vector.reciprocal(st(104), st(136 + m)))
                    nc.vector.tensor_scalar(attn_tok[:, i, bass.ds((2 * c + m // 8) * DV, DV)], ps[:, 6 + m % 2, 0:DV],
                                            st(104), None, ALU.mult).then_inc(s_("o_evac"), 1)

                def w_(k):
                    return tapw[:, bass.ds(c, 1), k:k + 1].rearrange("p a n -> p (a n)")

                def tap(k):
                    src = glu[:, bass.ds(c, 1), k:k + SEQ].rearrange("p a n -> p (a n)")
                    src_s = glu_s[:, bass.ds(c, 1), :, k:k + TQ].rearrange("p a b n -> p (a b) n")
                    if k == 0:
                        bias = gcol[:, bass.ds(c + COLS["conv_b"][0], 1)]
                        nc.vector.tensor_scalar(y_c, src, w_(k), bias, ALU.mult, ALU.add)
                        ch.link(nc.vector.tensor_scalar(y_s[:, :, :], src_s, w_(k), bias, ALU.mult, ALU.add))
                    else:
                        nc.vector.scalar_tensor_tensor(y_c, src, w_(k), y_c, ALU.mult, ALU.add)
                        ins = nc.vector.scalar_tensor_tensor(y_s[:, :, :], src_s, w_(k), y_s[:, :, :], ALU.mult, ALU.add)
                        if k == CK - 1:
                            ins.then_inc(s_("y_ready_c"), 1)
                        else:
                            ch.link(ins)
                row_max(0)
                for m in range(16):
                    if m >= 1:
                        out_rows(m - 1)
                    if m < 15:
                        row_max(m + 1)
                    dve.wait_ge(s_("ptA_done"), 16 * c + m + 1)
                    n = min(m % 8 + 1, 4) * P
                    nc.vector.tensor_copy(pT[:, 0:n], ps[:, 4, 0:n]).then_inc(s_("ptA_ready"), 1)
                    for k in (2 * m, 2 * m + 1):
                        if k < CK:
                            tap(k)
                out_rows(15)
                dve.wait_ge(s_("yT_done"), c + 1)
            dve.wait_ge(s_("b_ones"), 1)
            dve.wait_ge(s_("self_done"), 1)
            nc.vector.tensor_tensor(s_self[0:NS, :, :, :].rearrange("p h b q -> p h (b q)"),
                                    ps[0:NS, 7, :].rearrange("p (h n) -> p h n", h=NH),
                                    self_mask[:, :].unsqueeze(1).to_broadcast([NS, NH, NS]), ALU.add).then_inc(s_("self_ready"), 1)
            dve.wait_ge(s_("self_ready"), 1)

            def col_max(b, s):
                nc.vector.tensor_reduce(m_part, s_tok[s].rearrange("p g n -> p n g"), AXX, ALU.max).then_inc(s_("mpart_ready"), 1)

            def row_of_max(b, s):
                dve.wait_ge(s_("mT_done"), b + 1)
                ch.link(nc.vector.reduce_max(st(107)[0:NS], ps[0:NS, 6, 0:P], AXX))
                nc.vector.tensor_copy(m_row[0:NS, :], st(107)[0:NS].to_broadcast([NS, P])).then_inc(s_("mrow_ready"), 1)

            def shift(b, s):
                dve.wait_ge(s_("mB_done"), b + 1)
                nc.vector.tensor_tensor(s_tok[s], s_tok[s], ps[:, 6, P:P + NS].unsqueeze(1).to_broadcast([P, NPAGE + 1, NS]),
                                        ALU.subtract).then_inc(s_("s_shift"), 1)

            def out_lat(b, s):
                dve.wait_ge(s_("pv_s_done"), b + 1)
                ch.link(nc.vector.reciprocal(st(105)[0:NS], ps[0:NS, 7, KL:KL + 1]))
                nc.vector.tensor_scalar(o_lat[0:NS, :], ps[0:NS, 7, 0:KL], st(105)[0:NS], None, ALU.mult).then_inc(s_("olat_ready"), 1)

            def out_latT(b, s):
                dve.wait_ge(s_("olT_done"), b + 1)
                for c in range(LC):
                    last = nc.vector.tensor_copy(oT_lat[:, c, :, bass.ds(b, 1), :].rearrange("p h a q -> p (h a) q"),
                                                 ps[:, 6, 256 + c * NS:256 + (c + 1) * NS].rearrange("p (h q) -> p h q", q=TQ))
                last.then_inc(s_("olT_ready"), 1)

            def seq_dve(b, s, prev):
                for q in range(4):
                    if prev and q == 3:
                        out_lat(b - 1, 1 - s)
                    for g in range(4 * q, 4 * q + 4):
                        r = g % 2
                        dve.wait_ge(s_("ksq_ready"), NPAGE * b + g + 1)
                        ins = nc.vector.reduce_sum(ms_k[:, g, :], ksq[r].rearrange("p (h d) -> p h d", d=DN), AXX)
                        ins.then_inc(s_("ksum_done"), 1)
                    dve.wait_ge(s_("ksum_done"), NPAGE * b + 4 * q + 4)
                    nc.vector.tensor_scalar(ms_k[:, 4 * q:4 * q + 4, :], ms_k[:, 4 * q:4 * q + 4, :], 1.0 / DN, EPS,
                                            ALU.mult, ALU.add).then_inc(s_("msk_ready"), 1)
                    dve.wait_ge(s_("rstdk_ready"), 4 * b + q + 1)
                    dve.wait_ge(s_("sc_done"), 4 * b + q + 1)
                    sc = ps[:, 4 + q % 2, :].rearrange("p (g k n) -> p g k n", g=4, k=2)
                    ch.link(nc.vector.tensor_tensor(s_part, sc[:, :, 0, :].rearrange("p g (h q) -> p g h q", q=TQ),
                                                    rstd_k[:, 4 * q:4 * q + 4, :].unsqueeze(3).to_broadcast([P, 4, NH, TQ]), ALU.mult))
                    nc.vector.tensor_tensor(s_tok[s][:, 4 * q:4 * q + 4, :], s_part.rearrange("p g h q -> p g (h q)"),
                                            sc[:, :, 1, :], ALU.add).then_inc(s_("sc_used"), 1)
                    if prev and q == 0:
                        row_of_max(b - 1, 1 - s)
                    if prev and q == 1:
                        shift(b - 1, 1 - s)
                if prev:
                    out_latT(b - 1, 1 - s)
                ch.link(nc.vector.tensor_copy(s_tok[s][:, NPAGE, :].rearrange("p (h q) -> p h q", q=TQ),
                                              s_self[:, :, bass.ds(b, 1), :].rearrange("p h a q -> p (h a) q")))
                dve.wait_ge(s_("sc_used"), 4 * b + 4)
                col_max(b, s)
            seq_dve(0, 0, False)
            seq_dve(1, 1, True)
            with ch.loop(NSEQ // 2 - 1, 14) as p:
                for s in range(2):
                    seq_dve(2 * p + s + 2, s, True)
            row_of_max(NSEQ - 1, 1)
            shift(NSEQ - 1, 1)
            out_lat(NSEQ - 1, 1)
            out_latT(NSEQ - 1, 1)

            dve.wait_ge(s_("s_done"), 1)

            def tile_c(t, s, rows, p):
                r = slice(0, rows)
                cv = conv_tok[r, bass.ds(t, 1), :].rearrange("p a n -> p (a n)")
                ch.link(nc.vector.reduce_sum(st(4)[r], cv, AXX))
                ch.link(nc.vector.tensor_scalar(st(5)[r], st(4)[r], 1.0 / CC, None, ALU.mult))
                nc.vector.tensor_scalar(conv_n[r, :], cv, st(5)[r], None, ALU.subtract).then_inc(s_("centred"), 1)
                dve.wait_ge(s_("var_sumsq"), t + 1)
                nc.vector.tensor_scalar(st(7)[r], st(24)[r], 1.0 / CC, EPS, ALU.mult, ALU.add).then_inc(s_("var_ready"), 1)
                dve.wait_ge(s_("ln_loaded"), 32)
                dve.wait_ge(s_("rstd_ln"), t + 1)
                ch.link(nc.vector.scalar_tensor_tensor(conv_n[r, :], conv_n[r, :], st(6)[r], ln_g[r, :], ALU.mult, ALU.mult))
                nc.vector.tensor_tensor(conv_n[r, :], conv_n[r, :], ln_b[r, :], ALU.add).then_inc(s_("ln_ready"), 1)
                dve.wait_ge(s_("mix_sumsq"), t + 1)
                nc.vector.tensor_scalar(st(20, 2)[r], st(16, 2)[r], 1.0 / CC, EPS, ALU.mult, ALU.add).then_inc(s_("msm_ready"), 1)
                dve.wait_ge(s_("rstd_m"), t + 1)
                nc.vector.tensor_scalar(mixn[r, 0:CC], attn_tok[r, bass.ds(t, 1), :].rearrange("p a n -> p (a n)"), st(22)[r], None, ALU.mult)
                nc.vector.tensor_scalar(mixn[r, CC:2 * CC], conv_n[r, :], st(23)[r], None, ALU.mult).then_inc(s_("m_xn"), 1)
                nt_dve_gain(dve, "m", t + 1, rows, 0, "norm_out_attn", mT[:, :, 0:rows])
                dve.wait_ge(s_(f"xr_loaded{s}"), 16 * (p + 1))
                dve.wait_ge(s_("c_wout_done"), t + 1)
                nc.vector.tensor_tensor(x2[r, bass.ds(t, 1), :].rearrange("p a n -> p (a n)"),
                                        ps[r, 2:4, :].rearrange("p a n -> p (a n)"), xr[s][r, :], ALU.add).then_inc(s_("x2_ready"), 1)
                nt_dve_scale(dve, "c", t + 1, x2[r, bass.ds(t, 1), :].rearrange("p a n -> p (a n)"), rows, 0, xn2)
                dst = hT2[:, :, bass.ds(t * P, rows)]
                nt_dve_gain(dve, "c", t + 1, rows, 4, "norm_ffn", dst)
            with ch.loop(TILES // 2, 2 * 3) as p:
                for s in range(2):
                    tile_c(2 * p + s, s, P, p)
            tile_c(TILES, 0, NS, TILES // 2)

            with ch.loop(GROUPS, 0) as g:
                for s in range(2):
                    for b, (at, n) in enumerate(BLOCKS):
                        dve.wait_ge(s_("silu_ready"), 6 * g + 3 * s + b + 1)
                        dve.wait_ge(s_("up_done"), 6 * g + 3 * s + b + 1)
                        nc.vector.tensor_tensor(aT[s][:, at:at + n], gate_s[:, b, 0:n], ps[:, 2 * b + 1, 0:n], ALU.mult).then_inc(s_("aT_ready"), 1)
                for t in range(NT):
                    rows = P if t < TILES else NS
                    for h in range(2):
                        dve.wait_ge(s_("dn_done"), 2 * NT * g + 2 * t + h + 1)
                        d = x2[0:rows, t, h * HALF:(h + 1) * HALF]
                        nc.vector.tensor_tensor(d, d, ps[0:rows, 6 + h, :], ALU.add).then_inc(s_("dn_evac"), 1)

            def tile_d(t, s, rows, p):
                r = slice(0, rows)
                xv = x2[r, bass.ds(t, 1), :].rearrange("p a n -> p (a n)")
                nt_dve_scale(dve, "d", t + 1, xv, rows, 0, xn4)
                nt_dve_gain(dve, "d", t + 1, rows, 0, "norm_ple", hT4[:, :, 0:rows])
                dve.wait_ge(s_("sg_ready"), t + 1)
                dve.wait_ge(s_("pp_done"), t + 1)
                ch.link(nc.vector.tensor_tensor(sg[r, :], sg[r, :], ps[r, 5:7, :].rearrange("p a n -> p (a n)"), ALU.mult))
                nc.vector.tensor_tensor(y_out[s][r, :], sg[r, :], xv, ALU.add).then_inc(s_("y_ready"), 1)
            with ch.loop(TILES // 2, 2) as p:
                for s in range(2):
                    tile_d(2 * p + s, s, P, p)
                for s in range(2):
                    dve.wait_ge(s_(f"y_stored{s}"), 16 * (p + 1))
            tile_d(TILES, 0, NS, TILES // 2)

        @block.tensor
        def _(pe):
            ch = Chain(pe, s_("pe_own"))
            mm, tr = nc.tensor.matmul, nc.tensor.transpose
            pe.wait_ge(s_("ident_ready"), 1)
            pe.wait_ge(s_("consts"), 16 * (len(COLS) + 1))
            tr(ps[:, P0, 0:NCOL], gain_rows, ident[0:NCOL, 0:NCOL])
            for c in range(CCH):
                last = tr(ps[:, P1, c * CK:(c + 1) * CK], tap_rows[:, c * P:(c + 1) * P], ident[0:CK, 0:CK])
            last.then_inc(s_("colT_done"), 1)

            def tile_a(t, s, rows, p):
                nt_pe(pe, "a", t + 1, rows, x_in[s], T0)
                pe.wait_ge(s_("a_hT"), t + 1)
                pe.wait_ge(s_("w_in_loaded"), 16 * KC)
                for bank, c0, n in ((Z0, 0, QL), (Z1, QL, KL + DR)):
                    for k in range(KC):
                        last = mm(ps[0:rows, bank, 0:n], hT[:, k, 0:rows], w_in[:, k, c0:c0 + n], start=(k == 0), stop=(k == KC - 1))
                last.then_inc(s_("z_lat_done"), 1)
                for bank, c0 in ((Z3, QL + KL + DR + CC), (Z2, QL + KL + DR)):
                    for k in range(KC):
                        last = mm(ps[0:rows, bank, :], hT[:, k, 0:rows], w_in[:, k, c0:c0 + CC], start=(k == 0), stop=(k == KC - 1))
                last.then_inc(s_("z_glu_done"), 1)
                pe.wait_ge(s_("lat_ready"), t + 1)
                for k in range(5):
                    src = cqn[0:rows, k * P:(k + 1) * P] if k < 3 else ckvn[0:rows, (k - 3) * P:(k - 2) * P]
                    last = tr(ps[:, T0 + k // 4, (k % 4) * P:(k % 4) * P + rows], src, ident[0:rows, 0:rows])
                last.then_inc(s_("cT_done"), 1)
                pe.wait_ge(s_("glu_ready"), t + 1)
                for k in range(CCH):
                    last = tr(ps[:, Z2, k * P:k * P + rows], glu_t[0:rows, k * P:(k + 1) * P], ident[0:rows, 0:rows])
                last.then_inc(s_("gluT_done"), 1)
                pe.wait_ge(s_("w_u_loaded"), 48)
                pe.wait_ge(s_("cT_ready"), t + 1)
                for a in range(2):
                    for k in range(QL // P):
                        last = mm(ps[0:rows, P0 + a, 0:QL], cT[:, k, 0:rows], w_uq[:, k, a * QL:(a + 1) * QL], start=(k == 0), stop=(k == QL // P - 1))
                last.then_inc(s_("q_done"), 1)
                for bank, w in ((Z0, w_uk), (Z1, w_uv)):
                    for k in range(LC):
                        last = mm(ps[0:rows, bank, :], cT[:, 3 + k, 0:rows], w[:, k, :], start=(k == 0), stop=(k == LC - 1))
                last.then_inc(s_("kv_done"), 1)
                pe.wait_ge(s_("qh_ready"), t + 1)
                for h in range(NH):
                    last = tr(ps[0:DQ, T0 + h // 4, (h % 4) * P:(h % 4) * P + rows], qh[0:rows, h, :], ident[0:rows, 0:rows])
                last.then_inc(s_("qT_done"), 1)
                pe.wait_ge(s_("kh_ready"), t + 1)
                for h in range(NH):
                    last = tr(ps[0:DQ, P0 + h // 4, (h % 4) * P:(h % 4) * P + rows], kh[0:rows, h, :], ident[0:rows, 0:rows])
                last.then_inc(s_("kT_done"), 1)
                pe.wait_ge(s_("qT_ready"), t + 1)
            pairs(ch, 0)(tile_a)
            pe.wait_ge(s_("hist_loaded"), 32)
            for a in range(2):
                for c in range(CCH):
                    last = tr(ps[:, Z2 + a, c * 120:(c + 1) * 120], hist[0:120, a, c * P:(c + 1) * P], ident[0:120, 0:120])
            last.then_inc(s_("hist_done"), 1)

            pe.wait_ge(s_("kT_ready"), NT)
            pe.wait_ge(s_("hist_ready"), 1)
            with ch.loop(NH // 2, 0) as c:
                def scores(m):
                    hp, i = m // 8, m % 8
                    if i == 0:
                        pe.wait_ge(s_("qTh_ready"), 2 * c + hp + 1)
                    if m >= 2:
                        pe.wait_ge(s_("prob_ready"), 16 * c + m - 1)
                    n = (i + 1) * P
                    for a in range(0, n, 512):
                        w = min(512, n - a)
                        last = mm(ps[:, 2 * (m % 2) + a // 512, 0:w], qTh[hp][:, i * P:(i + 1) * P],
                                  kT[:, bass.ds(2 * c + hp, 1), a:a + w].rearrange("p a n -> p (a n)"), start=True, stop=True)
                    last.then_inc(s_("scores_done"), 1)
                scores(0)
                for m in range(16):
                    hp, i = m // 8, m % 8
                    if m < 15:
                        scores(m + 1)
                    pe.wait_ge(s_("prob_ready"), 16 * c + m + 1)
                    for j in range(i + 1):
                        last = tr(ps[:, 4 + j // 4, (j % 4) * P:(j % 4 + 1) * P], prob[m % 2][:, j * P:(j + 1) * P], ident[:, :])
                        if j == min(i, 3):
                            last.then_inc(s_("ptA_done"), 1)
                    if i >= 4:
                        last.then_inc(s_("ptB_done"), 1)
                    if m >= 2:
                        pe.wait_ge(s_("o_evac"), 16 * c + m - 1)
                    pe.wait_ge(s_("ptA_ready"), 16 * c + m + 1)
                    for j in range(i + 1):
                        if j == 4:
                            pe.wait_ge(s_("ptB_ready"), 8 * c + 4 * hp + i - 3)
                        last = mm(ps[:, 6 + m % 2, 0:DV], pT[:, j * P:(j + 1) * P],
                                  V[:, j, bass.ds((2 * c + hp) * DV, DV)], start=(j == 0), stop=(j == i))
                    last.then_inc(s_("pv_done"), 1)
                pe.wait_ge(s_("o_evac"), 16 * c + 16)
                pe.wait_ge(s_("y_ready_c"), c + 1)
                for t in range(TILES):
                    tr(ps[:, t // 4, (t % 4) * P:(t % 4 + 1) * P], y_c[:, t * P:(t + 1) * P], ident[:, :])
                tr(ps[0:NS, 4, 0:P], y_s[:, :, :].rearrange("p b q -> p (b q)"), ident[:, :]).then_inc(s_("yT_done"), 1)
                pe.wait_ge(s_("yT_ready"), c + 1)
            for h in range(NH):
                for k in range(LC):
                    last = tr(ps[0:DN, h // 2, (h % 2) * KL + k * P:(h % 2) * KL + (k + 1) * P], w_uk[:, k, h * DN:(h + 1) * DN], ident[:, :])
                    if h == 0 and k == 0:
                        last.then_inc(s_("b_done"), 1)
            last.then_inc(s_("wukT_done"), 1)
            for h in range(NH):
                last = mm(ps[0:NS, 7, h * NS:(h + 1) * NS], kT_s[:, h, :], qT_s[:, h, :], start=True, stop=True)
            last.then_inc(s_("self_done"), 1)
            pe.wait_ge(s_("wukT_ready"), 1)
            for h in range(NH):
                for k in range(LC):
                    last = mm(ps[:, 4 + k, h * NS:(h + 1) * NS], w_ukT[:, h, k * P:(k + 1) * P], qT_s[0:DN, h, :], start=True, stop=True)
            last.then_inc(s_("qabs_done"), 1)
            pe.wait_ge(s_("qabs_ready"), 1)
            pe.wait_ge(s_("self_ready"), 1)

            def seq_pe(b, s, prev, visits):
                pe.wait_ge(s_(f"pages_loaded{s}"), 32 * NPAGE * visits)

                def page_T(g):
                    r = g % 2
                    for k in range(LC):
                        tr(ps[:, r, k * P:(k + 1) * P], pages[s][:, g, k * P:(k + 1) * P], ident[:, :])
                    tr(ps[0:DR, r, LC * P:(LC + 1) * P], kpe[s][:, g, :], ident[:, :]).then_inc(s_("ctr_done"), 1)
                page_T(0)
                for g in range(NPAGE):
                    r, q = g % 2, g // 4
                    if g < NPAGE - 1:
                        page_T(g + 1)
                    pe.wait_ge(s_("ctr_ready"), NPAGE * b + g + 1)
                    if g >= 2:
                        pe.wait_ge(s_("ksq_ready"), NPAGE * b + g - 1)
                    for k in range(LC):
                        last = mm(ps[:, 2 + r, :], cT_ring[r][:, k, :], w_uk[:, k, :], start=(k == 0), stop=(k == LC - 1))
                    last.then_inc(s_("k_done"), 1)
                    if g % 4 == 0 and q >= 2:
                        pe.wait_ge(s_("sc_used"), 4 * b + q - 1)
                    o = (g % 4) * P
                    for k in range(LC):
                        mm(ps[:, 4 + q % 2, o:o + NS], cT_ring[r][:, k, :], q_abs[:, k, :, bass.ds(b * TQ, TQ)], start=(k == 0), stop=(k == LC - 1))
                    last = mm(ps[:, 4 + q % 2, o + NS:o + 2 * NS], kpeT_ring[r], q_pe[:, :, bass.ds(b * TQ, TQ)], start=True, stop=True)
                    if g % 4 == 3:
                        last.then_inc(s_("sc_done"), 1)
                    if prev and g == 0:
                        max_T(b - 1)
                    if prev and g == 6:
                        max_B(b - 1)
                    if prev and g == 12:
                        pv(b - 1, 1 - s)
                    if prev and g == 15:
                        lat_T(b - 1)
                pe.wait_ge(s_("sc_used"), 4 * b + 4)
                pe.wait_ge(s_("ksq_ready"), NPAGE * b + NPAGE)

            def max_T(b):
                pe.wait_ge(s_("mpart_ready"), b + 1)
                mm(ps[0:NS, 6, 0:P], m_part, ident[:, :], start=True, stop=True).then_inc(s_("mT_done"), 1)

            def max_B(b):
                pe.wait_ge(s_("mrow_ready"), b + 1)
                mm(ps[:, 6, P:P + NS], m_row[0:NS, :], ident[0:NS, 0:NS], start=True, stop=True).then_inc(s_("mB_done"), 1)

            def pv(b, s):
                pe.wait_ge(s_("ptok_ready"), b + 1)
                for g in range(NPAGE + 1):
                    last = mm(ps[0:NS, 7, 0:KL + 1], p_tok[:, g, :], pages[s][:, g, :], start=(g == 0), stop=(g == NPAGE))
                last.then_inc(s_("pv_s_done"), 1)

            def lat_T(b):
                pe.wait_ge(s_("olat_ready"), b + 1)
                for k in range(LC):
                    last = mm(ps[:, 6, 256 + k * NS:256 + (k + 1) * NS], o_lat[0:NS, k * P:(k + 1) * P], ident[0:NS, 0:NS], start=True, stop=True)
                last.then_inc(s_("olT_done"), 1)
            seq_pe(0, 0, False, 1)
            seq_pe(1, 1, True, 1)
            with ch.loop(NSEQ // 2 - 1, 0) as p:
                for s in range(2):
                    seq_pe(2 * p + s + 2, s, True, p + 2)
            max_T(NSEQ - 1)
            max_B(NSEQ - 1)
            pv(NSEQ - 1, 1)
            lat_T(NSEQ - 1)
            pe.wait_ge(s_("olT_ready"), NSEQ)
            for h in range(NH):
                for k in range(LC):
                    last = mm(ps[0:NS, 0, h * DV:(h + 1) * DV], oT_lat[:, k, h, :, :].rearrange("p b q -> p (b q)"),
                              w_uv[:, k, h * DV:(h + 1) * DV], start=(k == 0), stop=(k == LC - 1))
            last.then_inc(s_("ov_done"), 1)
            pe.wait_ge(s_("s_done"), 1)

            pe.wait_ge(s_("w_out_loaded"), 16)

            def tile_c(t, s, rows, p):
                nt_pe(pe, "m", t + 1, rows, mixn, 0)
                pe.wait_ge(s_("m_hT"), t + 1)
                for h in range(2):
                    for k in range(KC):
                        last = mm(ps[0:rows, 2 + h, :], mT[:, k, 0:rows], w_out[:, k, h * HALF:(h + 1) * HALF], start=(k == 0), stop=(k == KC - 1))
                last.then_inc(s_("c_wout_done"), 1)
                nt_pe(pe, "c", t + 1, rows, xn2, 4)
            pairs(ch, 0)(tile_c)

            pe.wait_ge(s_("c_hT"), NT)

            def group(g, first):
                for s in range(2):
                    pe.wait_ge(s_(f"gu_loaded{s}"), 32 * (g + 1))
                    for b, (at, n) in enumerate(BLOCKS):
                        if not (first and s == 0):
                            pe.wait_ge(s_("aT_ready"), 6 * g + 3 * (s - 1) + b + 1)
                        for k in range(KC):
                            last = mm(ps[:, 2 * b, 0:n], wg[s][:, k, :], hT2[:, k, at:at + n], start=(k == 0), stop=(k == KC - 1))
                        last.then_inc(s_("gate_done"), 1)
                        for k in range(KC):
                            last = mm(ps[:, 2 * b + 1, 0:n], wu[s][:, k, :], hT2[:, k, at:at + n], start=(k == 0), stop=(k == KC - 1))
                        last.then_inc(s_("up_done"), 1)
                pe.wait_ge(s_("wd_loaded"), 16 * (g + 1))
                for t in range(NT):
                    rows = P if t < TILES else NS
                    pe.wait_ge(s_("aT_ready"), 6 * g + 3 + [i for i, (at, n) in enumerate(BLOCKS) if at <= t * P][-1] + 1)
                    for h in range(2):
                        if not (first and t == 0):
                            pe.wait_ge(s_("dn_evac"), 2 * NT * g + 2 * (t - 1) + h + 1)
                        for s in range(2):
                            last = mm(ps[0:rows, 6 + h, :], aT[s][:, t * P:t * P + rows], wd[:, s, h * HALF:(h + 1) * HALF], start=(s == 0), stop=(s == 1))
                        last.then_inc(s_("dn_done"), 1)
            group(0, True)
            with pe.Fori(1, GROUPS) as g:
                group(g, False)

            pe.wait_ge(s_("dn_evac"), 2 * NT * GROUPS)
            pe.wait_ge(s_("w_d_loaded"), 32)

            def tile_d(t, s, rows, p):
                pe.wait_ge(s_(f"p_loaded{s}"), 16 * (p + 1))
                for k in range(PLE // P):
                    last = tr(ps[:, 2, k * P:k * P + rows], p_in[s][0:rows, k * P:(k + 1) * P], ident[0:rows, 0:rows])
                last.then_inc(s_("ppT_done"), 1)
                nt_pe(pe, "d", t + 1, rows, xn4, 0)
                pe.wait_ge(s_("ppT_ready"), t + 1)
                for h in range(2):
                    for k in range(PLE // P):
                        last = mm(ps[0:rows, 5 + h, :], p_T[:, k, 0:rows], w_pp[:, k, h * HALF:(h + 1) * HALF], start=(k == 0), stop=(k == PLE // P - 1))
                last.then_inc(s_("pp_done"), 1)
                pe.wait_ge(s_("d_hT"), t + 1)
                for h in range(2):
                    for k in range(KC):
                        last = mm(ps[0:rows, 3 + h, :], hT4[:, k, 0:rows], w_pg[:, k, h * HALF:(h + 1) * HALF], start=(k == 0), stop=(k == KC - 1))
                last.then_inc(s_("pg_done"), 1)
                pe.wait_ge(s_("y_ready"), t + 1)
            pairs(ch, 0)(tile_d)


_INS = ["x_prompt", "x_sample", "cache_ckv", "cache_kpe", "state_conv", "page_table", "p_prompt", "p_sample",
        "norm_mix", "w_in", "q_lora_norm", "w_uq", "kv_norm", "w_uk", "w_uv", "q_nope_norm", "k_nope_norm",
        "q_pe_norm", "k_pe_norm", "conv_w", "conv_b", "conv_ln_g", "conv_ln_b", "norm_out_attn", "norm_out_conv",
        "w_out", "norm_ffn", "w_gate", "w_up", "w_down", "norm_ple", "w_ple_gate", "w_ple_proj"]
_OUTS = [(1, SEQ, DM), (NSEQ, TQ, DM), (1, 1, SEQ, KL), (1, 1, SEQ, DR), (1, 1, HIST, CC),
         (1, NSEQ, TQ, KL), (1, NSEQ, TQ, DR), (1, NSEQ, HIST, CC)]


def rope_rows():
    pos = np.concatenate([np.arange(SEQ), np.tile(PAST + np.arange(TQ), NSEQ)]).astype(np.float32)
    inv = (np.float32(1.0) / np.power(np.float32(10000.0), np.arange(0, DR, 2, dtype=np.float32) / np.float32(DR))).astype(np.float32)
    ang = pos[:, None] * inv[None, :]
    return np.concatenate([np.cos(ang), np.sin(ang)], axis=1).astype(np.float32)


def kernel(**inputs):
    import numpy as _np
    import concourse.bacc as _bacc
    from concourse import mybir as _mybir
    from concourse.bass_utils import run_bass_kernel_spmd as _run

    nc = _bacc.Bacc("TRN2", target_bir_lowering=False, num_devices=1)
    arrays, args = {}, {}
    for name in _INS:
        a = _np.ascontiguousarray(inputs[name])
        arrays[f"in_{name}"] = a
        args[name] = nc.dram_tensor(f"in_{name}", a.shape, _mybir.dt.from_np(a.dtype), kind="ExternalInput").ap()
    arrays["in_rope"] = rope_rows()
    args["rope"] = nc.dram_tensor("in_rope", arrays["in_rope"].shape, _mybir.dt.float32, kind="ExternalInput").ap()
    outs = [nc.dram_tensor(f"out_{i}", shape, _mybir.dt.float32, kind="ExternalOutput").ap() for i, shape in enumerate(_OUTS)]
    build(nc, args, outs)
    r = _run(nc, [arrays], core_ids=[0])
    return tuple(r.results[0][f"out_{i}"] for i in range(len(_OUTS)))
```

```python
from contextlib import ExitStack, contextmanager

import numpy as np
import concourse.bass as bass
from concourse import mybir

P = 128
DM = 1024
SEQ = 1024
NSEQ, TQ = 8, 8
NS = NSEQ * TQ
PAST, PAGE = 2048, 128
NPAGE = PAST // PAGE
NH, DN, DR, DV = 8, 64, 32, 64
DQ = DN + DR
QL, KL = 384, 256
CC, CK = 512, 31
HIST = CK - 1
INW = QL + KL + DR + 2 * CC
DFF = 2816
PLE = 256
EPS = 1e-6
SCALE = 1.0 / float(np.sqrt(np.float32(DN + DR)))
NEG = -1e30
TILES = SEQ // P
NT = TILES + 1
NTOK = SEQ + NS
KC = DM // P
LC = KL // P
CCH = CC // P
HALF = 512
GROUPS = DFF // (2 * P)
PAGES_HALF = NPAGE // 2 * 2 * 16
BLOCKS = [(SEQ, NS), (0, 512), (512, 512)]

F32 = mybir.dt.float32
F32R = mybir.dt.float32r
I32 = mybir.dt.int32
ALU = mybir.AluOpType
ACT = mybir.ActivationFunctionType
AXX = mybir.AxisListType.X

COLS = {}
for _n, _k in (("norm_mix", 8), ("norm_out_attn", 4), ("norm_out_conv", 4), ("norm_ffn", 8),
               ("norm_ple", 8), ("conv_b", 4)):
    COLS[_n] = (sum(k for _, k in COLS.values()), _k)
NCOL = sum(k for _, k in COLS.values())


class Chain:

    def __init__(self, eng, sem):
        self.eng, self.sem, self.base, self.n = eng, sem, 0, 0

    def link(self, ins):
        self.n += 1
        ins.then_inc(self.sem, 1)
        self.eng.wait_ge(self.sem, self.base + self.n)

    @contextmanager
    def loop(self, count, per):
        before = self.n
        with self.eng.Fori(0, count) as i:
            self.base, self.n = i * per + before, 0
            yield i
            assert self.n == per, f"a loop's body links {self.n}"
        self.base, self.n = 0, before + count * per


def build(nc, A, O):
    ctx = ExitStack()
    with ctx:
        ctx.enter_context(nc.allow_non_contiguous_dma("weights by slices, gains broadcast"))
        def sb(name, shape, dt=F32):
            return ctx.enter_context(nc.sbuf_tensor(name, shape, dt))

        def sem(name):
            return ctx.enter_context(nc.semaphore(name))

        ident = sb("ident", [P, P])
        causal = sb("causal", [P, P])
        self_mask = sb("self_mask", [NS, NS])
        mhalf = sb("mhalf", [P, 4 * NH])
        inv_n = sb("inv_n", [P, 3 + 3 * NH])
        gcol = sb("gcol", [P, NCOL])
        g_q = sb("g_q", [P, QL])
        g_kv = sb("g_kv", [P, KL])
        g_kpe = sb("g_kpe", [P, DR])
        g_qn = sb("g_qn", [P, DN])
        g_qpe = sb("g_qpe", [P, DR])
        ckv_keep = sb("ckv_keep", [NS, KL])
        rope = sb("rope", [P, NT, DR])
        tapw = sb("tapw", [P, CCH, CK])
        table = sb("table", [1, NSEQ * NPAGE], I32)
        w_uk = sb("w_uk", [P, LC, NH * DN])
        w_uv = sb("w_uv", [P, LC, NH * DV])
        stats = sb("stats", [P, 160])
        glu_s = sb("glu_s", [P, CCH, NSEQ, HIST + TQ])
        qT_s = sb("qT_s", [DQ, NH, NS])
        kT_s = sb("kT_s", [DQ, NH, NS])
        arena_cols = 50500
        with nc.sbuf_tensor("arena", [P, arena_cols], F32) as arena:
            pass

        def window(name, at, shape, dt):
            n = int(np.prod(shape))
            with nc.sbuf_tensor(name + "_before", [P, at], F32):
                with nc.sbuf_tensor(name, [P, n], dt) as w:
                    pass
            v = w[:, :]
            if len(shape) == 2:
                v = v.rearrange("p (a b) -> p a b", b=shape[1])
            if len(shape) == 3:
                v = v.rearrange("p (a b c) -> p a b c", b=shape[1], c=shape[2])
            return v

        class Region:
            def __init__(self, start):
                self.at = start

            def take_window(self, name, *shape):
                at = self.at
                self.take(*shape)
                return window(name, at, shape, F32)

            def take_split(self, name, *shape):
                at = self.at
                self.take(*shape)
                part = window(name, at, shape, F32R)
                return part.bitcast(F32), part

            def take(self, *shape, rows=P):
                n = int(np.prod(shape))
                v = arena[0:rows, self.at:self.at + n]
                self.at += n
                assert self.at <= arena_cols, (self.at, arena_cols)
                if len(shape) == 2:
                    v = v.rearrange("p (a b) -> p a b", b=shape[1])
                if len(shape) == 3:
                    v = v.rearrange("p (a b c) -> p a b c", b=shape[1], c=shape[2])
                if len(shape) == 4:
                    v = v.rearrange("p (a b c d) -> p a b c d", b=shape[1], c=shape[2], d=shape[3])
                return v

        R = Region(0)
        qT = R.take(NH, SEQ, rows=DQ)
        kT = R.take(NH, SEQ, rows=DQ)
        V = R.take(TILES, NH * DV)
        glu_start = R.at
        glu = R.take(CCH, HIST + SEQ)
        shared_end = R.at
        w_in = R.take(KC, INW)
        w_uq = R.take(QL // P, NH * DQ)
        x_in = [R.take(DM), R.take(DM)]
        hT = R.take(KC, P)
        x_scr = R.take(DM)
        sq = R.take(2, QL)
        tap_rows = sq.rearrange("p a n -> p (a n)")[0:CK, 0:CC]
        cqn = R.take(QL)
        hist = x_in[1].rearrange("p (a n) -> p a n", a=2)
        ckvn = R.take(KL)
        kr = R.take(DR)
        kn = R.take(DR)
        rk = R.take(4, DR // 2)
        glu_t = R.take(CC)
        sig = glu_t
        gain_rows = glu_t[0:NCOL, 0:P]
        g_kn = glu_t[:, P:P + DN]
        cT = R.take(5, P)
        qh = R.take(NH, DQ)
        z_scr = x_scr
        kh = R.take(NH, DQ)
        k_scr = kh.rearrange("p a n -> p (a n)")
        rt = k_scr[:, 0:4 * NH * DR // 2].rearrange("p (a b c) -> p a b c", a=4, c=DR // 2)
        R = Region(shared_end)
        mix_tok = R.take(NT, 2 * CC)
        attn_tok, conv_tok = mix_tok[:, :, 0:CC], mix_tok[:, :, CC:2 * CC]
        b_keep_end = R.at
        qTh = [R.take(SEQ, rows=DQ), R.take(SEQ, rows=DQ)]
        prob = [R.take(SEQ), R.take(SEQ)]
        pT = R.take(SEQ)
        b_end = R.at
        R = Region(0)
        pages1, kpe1 = R.take(NPAGE + 1, KL + 1), R.take(NPAGE, DR)
        s_tok = [R.take(NPAGE + 1, NS), R.take(NPAGE + 1, NS)]
        s_low_end = (NT + 2) * DM
        assert R.at <= s_low_end
        R = Region(b_keep_end)
        p_tok = R.take(NPAGE + 1, NS)
        cT_ring = [R.take(LC, P), R.take(LC, P)]
        kpeT_ring = [R.take(P, rows=DR), R.take(P, rows=DR)]
        ksq = [R.take(NH * DN), R.take(NH * DN)]
        ms_k = R.take(NPAGE, NH)
        rstd_k = R.take(NPAGE, NH)
        s_part = R.take(4, NH, TQ)
        m_part = R.take(NS)
        m_row = R.take(P)
        o_lat = R.take(KL)
        oT_lat = R.take(LC, NH, NSEQ, TQ)
        y_c = R.take(SEQ)
        y_s = R.take(NSEQ, TQ)
        assert b_end <= R.at
        w_ukT = R.take(NH, KL, rows=DN)
        q_abs = R.take(LC, NH, NS)
        q_pe = R.take(NH, NS, rows=DR)
        s_self = R.take(NH, NSEQ, TQ)
        pages = [R.take(NPAGE + 1, KL + 1), pages1]
        kpe = [R.take(NPAGE, DR), kpe1]
        R = Region(0)
        x2 = R.take(NT, DM)
        xr = [R.take(DM), R.take(DM)]
        assert R.at <= s_low_end
        R = Region(s_low_end)
        w_out = R.take(KC, DM)
        w_out_end = R.at
        aT_place = R.at
        R = Region(w_out_end + NTOK)
        w_raw = [R.take_window("w_raw0", 2, KC, P), R.take_window("w_raw1", 2, KC, P)]
        assert w_out_end <= glu_start and R.at <= shared_end
        R = Region(shared_end)
        h_hi, h_hi_r = R.take_split("h_hi", TILES, KC, P)
        h_s = R.take(KC, NS)
        assert R.at <= b_keep_end
        R = Region(b_keep_end)
        h_full = R.take_window("h_full", TILES, KC, P)
        _, h_lo_r = Region(b_keep_end).take_split("h_lo", TILES, KC, P)
        h_end = R.at
        mixn = R.take(DM)
        mT = R.take(KC, P)
        conv_n = R.take(CC)
        ln_g = R.take(CC)
        ln_b = R.take(CC)
        xn2 = R.take(DM)
        R = Region(h_end)
        wd_hi, wd_hi_r = R.take_split("wd_hi", 2, DM)
        _, wd_lo_r = R.take_split("wd_lo", 2, DM)
        parts = [R.take_split(f"act{i}", NTOK) for i in range(3)]
        R = Region(aT_place)
        parts.append(R.take_split("act3", NTOK))
        a_hi, a_hi_r = zip(parts[0], parts[1])
        _, a_lo_r = zip(parts[2], parts[3])
        R = Region(s_low_end)
        w_hi, w_hi_r = zip(*(R.take_split(f"w_hi{i}", 2, KC, P) for i in range(2)))
        _, w_lo_r = zip(*(R.take_split(f"w_lo{i}", 2, KC, P) for i in range(2)))
        assert R.at <= w_out_end
        R = Region(NT * DM)
        gate_s = R.take_window("gate_s", NTOK)
        wd_raw = [w[:, :, :].rearrange("p a n -> p (a n)") for w in (w_uk, w_uv)]
        R = Region(shared_end)
        w_pg = R.take(KC, DM)
        assert R.at <= b_keep_end
        R = Region(b_keep_end)
        w_pp = R.take(PLE // P, DM)
        p_in = [R.take(PLE), R.take(PLE)]
        assert R.at <= h_end
        p_T = R.take(PLE // P, P)
        hT4 = R.take(KC, P)
        sg = R.take(DM)
        y_out = [R.take(DM), R.take(DM)]
        xn4 = R.take(DM)
        junk4 = R.take(DM)

        ps = ctx.enter_context(nc.psum_tensor("ps", [P, 8, 512], F32))

        S = {}

        def s_(name):
            if name not in S:
                S[name] = sem(name)
            return S[name]

        win_v = A["w_in"][0].rearrange("(k p) n -> p k n", p=P)
        xp_v = A["x_prompt"][0].rearrange("(t p) n -> t p n", p=P)
        xs_v = A["x_sample"].rearrange("b q n -> (b q) n")
        st = lambda a, n=1: stats[:, a:a + n]
        HD2 = DR // 2

        def tiles(chain, per, tile):
            tile(0, 0, P, 1, P)
            with chain.loop(TILES // 2 - 1, per) as p:
                tile(2 * p + 1, 1, P, p + 1, P)
                tile(2 * p + 2, 0, P, p + 2, P)
            tile(TILES - 1, 1, P, TILES // 2, NS)
            tile(TILES, 0, NS, TILES // 2 + 1, 0)

        def first(t):
            return isinstance(t, int) and t == 0

        def slot_count(t, s, v):
            return v if s == 0 else v + 1

        def nt_act(act, stage, n, src, rows, col, scratch):
            nc.scalar.activation(scratch[0:rows, :], src, ACT.Square,
                                 accum_out=st(col)[0:rows]).then_inc(s_(stage + "_sumsq"), 1)

        def nt_dve_scale(dve, stage, n, src, rows, col, out):
            dve.wait_ge(s_(stage + "_sumsq"), n)
            nc.vector.tensor_scalar(st(col + 1)[0:rows], st(col)[0:rows], 1.0 / DM, EPS, ALU.mult,
                                    ALU.add).then_inc(s_(stage + "_ms"), 1)
            dve.wait_ge(s_(stage + "_rstd"), n)
            nc.vector.tensor_scalar(out[0:rows, :], src, st(col + 2)[0:rows], None,
                                    ALU.mult).then_inc(s_(stage + "_xn"), 1)

        def nt_pool(pool, stage, n, rows, col):
            pool.wait_ge(s_(stage + "_ms"), n)
            nc.gpsimd.tensor_tensor(st(col + 2)[0:rows], st(col + 1)[0:rows], mhalf[0:rows, 0:1],
                                    ALU.pow).then_inc(s_(stage + "_rstd"), 1)

        def nt_pe(pe, stage, n, rows, src, bank):
            pe.wait_ge(s_(stage + "_xn"), n)
            for k in range(KC):
                last = nc.tensor.transpose(ps[:, bank + k // 4, (k % 4) * P:(k % 4) * P + rows],
                                           src[0:rows, k * P:(k + 1) * P], ident[0:rows, 0:rows])
            last.then_inc(s_(stage + "_xT"), 1)

        def nt_dve_gain(dve, stage, n, rows, bank, gain, out):
            dve.wait_ge(s_(stage + "_xT"), n)
            g0 = COLS[gain][0] if isinstance(gain, str) else gain
            for b in range(2):
                src = ps[:, bank + b, :].rearrange("p (k c) -> p k c", c=P)[:, :, 0:rows]
                g = gcol[:, g0 + 4 * b:g0 + 4 * b + 4].unsqueeze(2).to_broadcast([P, 4, rows])
                last = nc.vector.tensor_tensor(out[:, 4 * b:4 * b + 4, :], src, g, ALU.mult)
            last.then_inc(s_(stage + "_hT"), 1)

        T0, T1, Z0, Z1, Z2, Z3, P0, P1 = 0, 1, 2, 3, 4, 5, 6, 7
        c_scr = ps[:, 6:8, :].rearrange("p a n -> p (a n)")
        block = ctx.enter_context(nc.Block())

        @block.sync
        def _(sp):
            lat_w, glu_w = QL + KL + DR, 2 * CC
            sp.dma_start(x_in[0], xp_v[0]).then_inc(s_("x_loaded0"), 16)
            for name in COLS:
                c0, k = COLS[name]
                sp.dma_start(gain_rows[c0:c0 + k, :], A[name][0].rearrange("(k p) -> k p", p=P)).then_inc(s_("consts"), 16)
            sp.dma_start(tap_rows, A["conv_w"][0]).then_inc(s_("consts"), 16)
            sp.dma_start(w_in[:, :, 0:lat_w], win_v[:, :, 0:lat_w]).then_inc(s_("w_lat_loaded"), 16)
            sp.dma_start(x_in[1], xp_v[1]).then_inc(s_("x_loaded1"), 16)
            sp.dma_start(w_in[:, :, lat_w:], win_v[:, :, lat_w:]).then_inc(s_("w_glu_loaded"), 16)
            sp.dma_start(w_uq, A["w_uq"][0].rearrange("(k p) n -> p k n", p=P)).then_inc(s_("w_u_loaded"), 16)
            sp.dma_start(w_uk[:, :, :], A["w_uk"][0].rearrange("(k p) n -> p k n", p=P)).then_inc(s_("w_u_loaded"), 16)
            sp.dma_start(w_uv[:, :, :], A["w_uv"][0].rearrange("(k p) n -> p k n", p=P)).then_inc(s_("w_u_loaded"), 16)

            def load_x(t, s):
                sp.wait_ge(s_("a_xT"), t + 1)
                sp.dma_start(x_in[s], xp_v[bass.ds(t + 2, 1)].rearrange("a p n -> (a p) n")).then_inc(s_(f"x_loaded{s}"), 16)

            def store_a(t, rows):
                out_ckv = O[2][0, 0, bass.ds(t * P, P), :] if rows == P else O[5][0].rearrange("b q n -> (b q) n")
                out_kpe = O[3][0, 0, bass.ds(t * P, P), :] if rows == P else O[6][0].rearrange("b q n -> (b q) n")
                sp.wait_ge(s_("lat_ready"), t + 1)
                sp.dma_start(out_ckv, ckvn[0:rows, :]).then_inc(s_("lat_stored"), 16)
                sp.wait_ge(s_("kpe_ready"), t + 1)
                sp.dma_start(out_kpe, kr[0:rows, :]).then_inc(s_("lat_stored"), 16)
            with sp.Fori(0, TILES // 2 - 1) as p:
                for s in range(2):
                    load_x(2 * p + s, s)
                    store_a(2 * p + s, P)
            sp.wait_ge(s_("a_xT"), TILES - 1)
            sp.dma_start(x_in[0][0:NS, :], xs_v).then_inc(s_("x_loaded0"), 16)
            store_a(TILES - 2, P)
            sp.wait_ge(s_("a_xT"), TILES)
            for a in range(2):
                sp.dma_start(hist[0:120, a, :], A["state_conv"][0, 4 * a:4 * a + 4].rearrange("b n c -> (b n) c")).then_inc(s_("hist_loaded"), 16)
            store_a(TILES - 1, P)
            sp.wait_ge(s_("glu_ready"), TILES)
            sp.dma_start(O[4][0, 0], glu_t[P - HIST:P, :]).then_inc(s_("tail_stored"), 16)
            store_a(TILES, NS)
            sp.wait_ge(s_("glu_ready"), NT)
            for b in range(NSEQ):
                sp.dma_start(O[7][0, b, HIST - TQ:HIST, :], glu_t[b * TQ:(b + 1) * TQ, :]).then_inc(s_("out_stored"), 16)
            sp.dma_start(O[7][0, :, 0:HIST - TQ, :], A["state_conv"][0, :, TQ:HIST, :]).then_inc(s_("out_stored"), 16)

            sp.wait_ge(s_("table_loaded"), 16)

            def load_pages(b, s):
                for g in range(NPAGE):
                    idx = sp.value_load(table[0:1, bass.ds(b * NPAGE + g, 1)], min_val=0, max_val=A["cache_ckv"].shape[1] - 1)
                    sp.dma_start(pages[s][:, g, 0:KL], A["cache_ckv"][0, bass.ds(idx, 1)].rearrange("a p n -> (a p) n")).then_inc(s_(f"pages_loaded{s}{g // 8}"), 16)
                    sp.dma_start(kpe[s][:, g, :], A["cache_kpe"][0, bass.ds(idx, 1)].rearrange("a p n -> (a p) n")).then_inc(s_(f"pages_loaded{s}{g // 8}"), 16)
            sp.wait_ge(s_("b_ones0"), 1)
            load_pages(0, 0)
            sp.wait_ge(s_("o_evac"), TILES * NH)
            sp.wait_ge(s_("b_ones1"), 1)
            load_pages(1, 1)
            sp.dma_start(w_out, A["w_out"][0].rearrange("(k p) n -> p k n", p=P)).then_inc(s_("w_out_loaded"), 16)
            with sp.Fori(0, NSEQ // 2 - 1) as p:
                for s in range(2):
                    sp.wait_ge(s_("pv_s_done"), 2 * p + s + 1)
                    load_pages(2 * p + s + 2, s)

            sp.wait_ge(s_("s_done"), 1)
            for dst, name in ((ln_g, "conv_ln_g"), (ln_b, "conv_ln_b")):
                sp.dma_start(dst, A[name][0].partition_broadcast(P)).then_inc(s_("ln_loaded"), 16)
            for s in range(2):
                sp.dma_start(xr[s], xp_v[s]).then_inc(s_(f"xr_loaded{s}"), 16)
            wg_v = A["w_gate"][0].rearrange("(k p) n -> p k n", p=P)
            wu_v = A["w_up"][0].rearrange("(k p) n -> p k n", p=P)
            wd_v = A["w_down"][0].rearrange("(f p) n -> p f n", p=P)

            def load_gu(f, s):
                sp.dma_start(w_raw[s][:, 0], wg_v[:, :, bass.ds(f * P, P)]).then_inc(s_(f"gu_loaded{s}"), 16)
                sp.dma_start(w_raw[s][:, 1], wu_v[:, :, bass.ds(f * P, P)]).then_inc(s_(f"gu_loaded{s}"), 16)

            def load_wd(g):
                for s in range(2):
                    sp.dma_start(wd_raw[s], wd_v[:, bass.ds(2 * g + s, 1), :].rearrange("p a n -> p (a n)")).then_inc(s_("wd_loaded"), 16)
            for s in range(2):
                load_gu(s, s)
            load_wd(0)
            with sp.Fori(0, TILES // 2 - 1) as p:
                for s in range(2):
                    sp.wait_ge(s_("x2_ready"), 2 * p + s + 1)
                    sp.dma_start(xr[s], xp_v[bass.ds(2 * p + s + 2, 1)].rearrange("a p n -> (a p) n")).then_inc(s_(f"xr_loaded{s}"), 16)
            sp.wait_ge(s_("x2_ready"), TILES - 1)
            sp.dma_start(xr[0][0:NS, :], xs_v).then_inc(s_("xr_loaded0"), 16)

            with sp.Fori(0, GROUPS - 1) as g:
                for s in range(2):
                    sp.wait_ge(s_("up_done"), 6 * g + 3 * s + 2)
                    load_gu(2 * g + s + 2, s)
                    if s == 0:
                        sp.wait_ge(s_("wd_split"), g + 1)
                        load_wd(g + 1)

            pp_v = A["p_prompt"][0, 0].rearrange("(t p) n -> t p n", p=P)
            ps_v = A["p_sample"][0].rearrange("b q n -> (b q) n")
            yp_v = O[0][0].rearrange("(t p) n -> t p n", p=P)
            sp.wait_ge(s_("up_done"), 6 * GROUPS)
            for h in range(2):
                sp.dma_start(w_pg[:, :, h * HALF:(h + 1) * HALF], A["w_ple_gate"][0, :, h * HALF:(h + 1) * HALF].rearrange("(k p) n -> p k n", p=P))\
                    .then_inc(s_(f"w_pg_loaded{h}"), 16)
            sp.dma_start(w_pp, A["w_ple_proj"][0].rearrange("(k p) n -> p k n", p=P)).then_inc(s_("w_pp_loaded"), 16)
            for s in range(2):
                sp.dma_start(p_in[s], pp_v[s]).then_inc(s_(f"p_loaded{s}"), 16)

            def load_p(t, s):
                sp.wait_ge(s_("ppT_done"), t + 1)
                sp.dma_start(p_in[s], pp_v[bass.ds(t + 2, 1)].rearrange("a p n -> (a p) n")).then_inc(s_(f"p_loaded{s}"), 16)

            def store_y(t, s):
                sp.wait_ge(s_("y_ready"), t + 1)
                sp.dma_start(yp_v[bass.ds(t, 1)].rearrange("a p n -> (a p) n"), y_out[s]).then_inc(s_(f"y_stored{s}"), 16)
            with sp.Fori(0, TILES // 2 - 1) as p:
                for s in range(2):
                    load_p(2 * p + s, s)
                    store_y(2 * p + s, s)
            sp.wait_ge(s_("ppT_done"), TILES - 1)
            sp.dma_start(p_in[0][0:NS, :], ps_v).then_inc(s_("p_loaded0"), 16)
            store_y(TILES - 2, 0)
            store_y(TILES - 1, 1)
            sp.wait_ge(s_("y_ready"), NT)
            sp.dma_start(O[1].rearrange("b q n -> (b q) n"), y_out[0][0:NS, :]).then_inc(s_("y_stored0"), 16)
            sp.wait_ge(s_("y_stored0"), 16 * (TILES // 2 + 1))
            sp.wait_ge(s_("y_stored1"), 16 * (TILES // 2))
            sp.wait_ge(s_("lat_stored"), 32 * NT)
            sp.wait_ge(s_("tail_stored"), 16)
            sp.wait_ge(s_("out_stored"), 16 * (NSEQ + 1))

        @block.gpsimd
        def _(pool):
            ch = Chain(pool, s_("pool_own"))
            ch.link(nc.gpsimd.memset(ident[:, :], 0.0))
            nc.gpsimd.affine_select(out=ident[:, :], in_=ident[:, :], compare_op=ALU.not_equal, fill=1.0,
                                    base=0, pattern=[[-1, P]], channel_multiplier=1).then_inc(s_("ident_ready"), 1)
            nc.gpsimd.memset(mhalf[:, :], -0.5)
            for i, n in enumerate((QL, KL, DR)):
                nc.gpsimd.memset(inv_n[:, i:i + 1], 1.0 / n)
            nc.gpsimd.memset(inv_n[:, 3:3 + NH], 1.0 / DN)
            nc.gpsimd.memset(inv_n[:, 3 + NH:3 + 2 * NH], 1.0 / DR)
            ch.link(nc.gpsimd.memset(inv_n[:, 3 + 2 * NH:3 + 3 * NH], 1.0 / DN))
            nc.gpsimd.memset(glu[:, :, 0:HIST], 0.0)
            ch.link(nc.gpsimd.memset(causal[:, :], 0.0))
            nc.gpsimd.affine_select(out=causal[:, :], in_=causal[:, :], compare_op=ALU.is_ge, fill=NEG,
                                    base=0, pattern=[[-1, P]], channel_multiplier=1)
            ch.link(nc.gpsimd.memset(self_mask[:, :], 0.0))
            sm = self_mask[:, :].rearrange("p (b q) -> p b q", q=TQ)
            ch.link(nc.gpsimd.affine_select(out=sm, in_=sm, compare_op=ALU.is_ge, fill=NEG, base=0,
                                            pattern=[[TQ, NSEQ], [1, TQ]], channel_multiplier=-1))
            nc.gpsimd.affine_select(out=sm, in_=sm, compare_op=ALU.is_ge, fill=NEG, base=0,
                                    pattern=[[-TQ, NSEQ], [0, TQ]], channel_multiplier=1).then_inc(s_("pool_consts"), 1)


            def rstd_q(t, rows):
                pool.wait_ge(s_("msq_ready"), t + 1)
                nc.gpsimd.tensor_tensor(st(80, 24)[0:rows], st(50, 24)[0:rows], mhalf[0:rows, 0:24], ALU.pow).then_inc(s_("rstd_q"), 1)

            def tile_a(t, s, rows, v, ahead):
                if not first(t):
                    rstd_q(t - 1, P)
                pool.wait_ge(s_("msz_ready"), t + 1)
                nc.gpsimd.tensor_tensor(st(16, 3)[0:rows], st(12, 3)[0:rows], mhalf[0:rows, 0:3], ALU.pow).then_inc(s_("rstd_z"), 1)
                if ahead:
                    nt_pool(pool, "a", t + 2, ahead, 0)
            nt_pool(pool, "a", 1, P, 0)
            tiles(ch, 0, tile_a)
            rstd_q(TILES, NS)

            pool.wait_ge(s_("ckv_kept"), 1)
            pool.wait_ge(s_("hist_ready"), 1)
            pool.wait_ge(s_("lat_stored"), 32 * NT)
            pool.wait_ge(s_("tail_stored"), 16)
            pool.wait_ge(s_("out_stored"), 16 * (NSEQ + 1))

            def set_page(s):
                ch.link(nc.gpsimd.memset(pages[s][:, :, KL:KL + 1], 1.0))
                ch.link(nc.gpsimd.memset(pages[s][:, NPAGE, 0:KL], 0.0))
                nc.gpsimd.tensor_copy(pages[s][0:NS, NPAGE, 0:KL], ckv_keep[:, :]).then_inc(s_(f"b_ones{s}"), 1)
                pool.wait_ge(s_(f"b_ones{s}"), 1)
            nc.gpsimd.memset(s_self[64:P, :, :, :], NEG).then_inc(s_("self_place"), 1)
            pool.wait_ge(s_("self_place"), 1)
            set_page(0)
            pool.wait_ge(s_("o_evac"), TILES * NH)
            set_page(1)
            with ch.loop(NSEQ, 0) as b:
                for q in range(4):
                    pool.wait_ge(s_("msk_ready"), 4 * b + q + 1)
                    nc.gpsimd.tensor_tensor(rstd_k[:, 4 * q:4 * q + 4, :], ms_k[:, 4 * q:4 * q + 4, :],
                                            mhalf[:, 0:4 * NH].rearrange("p (g h) -> p g h", h=NH), ALU.pow).then_inc(s_("rstdk_ready"), 1)

            def mix_pool(n, rows):
                pool.wait_ge(s_("var_ready"), n)
                nc.gpsimd.tensor_tensor(st(6)[0:rows], st(7)[0:rows], mhalf[0:rows, 0:1], ALU.pow).then_inc(s_("rstd_ln"), 1)
                pool.wait_ge(s_("msm_ready"), n)
                nc.gpsimd.tensor_tensor(st(22, 2)[0:rows], st(20, 2)[0:rows], mhalf[0:rows, 0:2], ALU.pow).then_inc(s_("rstd_m"), 1)

            def tile_c(t, s, rows, v, ahead):
                if not first(t):
                    nt_pool(pool, "c", t, P, 0)
                if ahead:
                    mix_pool(t + 2, ahead)
            mix_pool(1, P)
            tiles(ch, 0, tile_c)
            nt_pool(pool, "c", NT, NS, 0)

            def tile_d(t, s, rows, v, ahead):
                if ahead:
                    nt_pool(pool, "d", t + 2, ahead, 0)
            nt_pool(pool, "d", 1, P, 0)
            tiles(ch, 0, tile_d)

        @block.scalar
        def _(act):
            ch = Chain(act, s_("act_own"))
            for dst, name in ((g_q, "q_lora_norm"), (g_kv, "kv_norm"), (g_kpe, "k_pe_norm"), (g_qn, "q_nope_norm"),
                              (g_kn, "k_nope_norm"), (g_qpe, "q_pe_norm")):
                act.dma_start(dst[0:P], A[name][0].partition_broadcast(P)).then_inc(s_("gains"), 16)
            act.dma_start(rope[:, 0:TILES, :], A["rope"][0:SEQ, :].rearrange("(t p) n -> p t n", p=P)).then_inc(s_("gains"), 16)
            act.dma_start(rope[0:NS, TILES, :], A["rope"][SEQ:NTOK, :]).then_inc(s_("gains"), 16)
            act.dma_start(table[:, :], A["page_table"].rearrange("b g -> (b g)").unsqueeze(0)).then_inc(s_("table_loaded"), 16)
            act.wait_ge(s_("pool_consts"), 1)
            act.wait_ge(s_("colT_done"), 1)

            def qkv_act(t, rows):
                act.wait_ge(s_("q_done"), t + 1)
                nc.scalar.activation(sq[0:rows, :, :], ps[0:rows, P0:P0 + 2, 0:QL], ACT.Square).then_inc(s_("q_sq"), 1)
                act.wait_ge(s_("kv_done"), t + 1)
                nc.scalar.activation(k_scr[0:rows, 0:NH * DN], ps[0:rows, Z2, :], ACT.Square).then_inc(s_("k_sq"), 1)
                if rows == P:
                    nc.scalar.activation(V[:, bass.ds(t, 1), :], ps[:, Z3, :].unsqueeze(1), ACT.Copy).then_inc(s_("v_ready"), 1)

            def qT_copy(t, rows):
                act.wait_ge(s_("qT_done"), t + 1)
                src = ps[0:DQ, T0:T0 + 2, :].rearrange("p a (k c) -> p (a k) c", c=P)[:, :, 0:rows]
                dst = qT[:, :, bass.ds(t * P, P)] if rows == P else qT_s[:, :, :]
                nc.scalar.activation(dst, src, ACT.Copy).then_inc(s_("qT_ready"), 1)

            def tile_a(t, s, rows, v, ahead):
                if not first(t):
                    qkv_act(t - 1, P)
                act.wait_ge(s_("z_lat_done"), t + 1)
                act.wait_ge(s_("a_sumsq"), t + 1)
                nc.scalar.activation(z_scr[0:rows, 0:QL], ps[0:rows, Z0, 0:QL], ACT.Square, accum_out=st(8)[0:rows])
                nc.scalar.activation(z_scr[0:rows, QL:QL + KL], ps[0:rows, Z1, 0:KL], ACT.Square, accum_out=st(9)[0:rows])
                nc.scalar.activation(z_scr[0:rows, QL + KL:QL + KL + DR], ps[0:rows, Z1, KL:KL + DR], ACT.Square,
                                     accum_out=st(10)[0:rows]).then_inc(s_("z_sumsq"), 1)
                if not first(t):
                    qT_copy(t - 1, P)
                if ahead:
                    act.wait_ge(s_("z_sumsq"), t + 1)
                    act.wait_ge(s_(f"x_loaded{1 - s}"), 16 * slot_count(t, s, v))
                    nt_act(act, "a", t + 2, x_in[1 - s][0:ahead, :], ahead, 0, x_scr)
                if rows == NS:
                    act.wait_ge(s_("tail_stored"), 16)
                act.wait_ge(s_("z_glu_done"), t + 1)
                nc.scalar.activation(sig[0:rows, :], ps[0:rows, Z3, :], ACT.Sigmoid).then_inc(s_("sig_ready"), 1)
                act.wait_ge(s_("cT_done"), t + 1)
                nc.scalar.activation(cT[:, 0:4, 0:rows], ps[:, T0, :].rearrange("p (k c) -> p k c", c=P)[:, :, 0:rows], ACT.Copy)
                nc.scalar.activation(cT[:, 4, 0:rows], ps[:, T1, 0:rows], ACT.Copy).then_inc(s_("cT_ready"), 1)
                act.wait_ge(s_("gluT_done"), t + 1)
                src = ps[:, Z0, :].rearrange("p (k c) -> p k c", c=P)[:, :, 0:rows]
                if rows == P:
                    nc.scalar.activation(glu[:, :, bass.ds(HIST + t * P, P)], src, ACT.Copy).then_inc(s_("gluT_ready"), 1)
                else:
                    for c in range(CCH):
                        last = nc.scalar.activation(glu_s[:, c, :, HIST:HIST + TQ], src[:, c, :].rearrange("p (b q) -> p b q", q=TQ), ACT.Copy)
                    last.then_inc(s_("gluT_ready"), 1)
            act.wait_ge(s_("x_loaded0"), 16)
            nt_act(act, "a", 1, x_in[0], P, 0, x_scr)
            tiles(ch, 0, tile_a)
            qkv_act(TILES, NS)
            qT_copy(TILES, NS)
            act.wait_ge(s_("hist_done"), 1)
            for a in range(2):
                last = nc.scalar.activation(glu_s[:, :, 4 * a:4 * a + 4, 0:HIST],
                                            ps[:, Z2 + a, 0:CCH * 120].rearrange("p (c b n) -> p c b n", b=4, n=HIST), ACT.Copy)
            last.then_inc(s_("hist_ready"), 1)

            act.wait_ge(s_("self_place"), 1)
            act.wait_ge(s_("wukT_done"), 1)
            nc.scalar.activation(w_ukT, ps[0:DN, 0:4, :].rearrange("p a (h c) -> p (a h) c", c=KL), ACT.Copy)
            nc.scalar.activation(q_pe, qT_s[DN:DQ, :, :], ACT.Copy).then_inc(s_("wukT_ready"), 1)
            act.wait_ge(s_("qabs_done"), 1)
            nc.scalar.activation(q_abs, ps[:, 4:4 + LC, :].rearrange("p a (h n) -> p a h n", h=NH), ACT.Copy).then_inc(s_("qabs_ready"), 1)

            act.wait_ge(s_("kT_ready"), NT)
            with ch.loop(NH // 2, 0) as c:
                for hp in range(2):
                    nc.scalar.activation(qTh[hp], qT[:, bass.ds(2 * c + hp, 1), :].rearrange("p a n -> p (a n)"), ACT.Copy)\
                        .then_inc(s_("qTh_ready"), 1)

                def expo(m):
                    n = (m % 8 + 1) * P
                    act.wait_ge(s_("nmax_ready"), 16 * c + m + 1)
                    nc.scalar.activation(prob[m % 2][:, 0:n], ps[:, 2 * (m % 2):2 * (m % 2) + 2, :].rearrange("p a n -> p (a n)")[:, 0:n],
                                         ACT.Exp, bias=st(120 + m), accum_out=st(136 + m)).then_inc(s_("prob_ready"), 1)
                expo(0)
                expo(1)
                for m in range(16):
                    i = m % 8
                    act.wait_ge(s_("ptA_done"), 16 * c + m + 1)
                    n = min(i + 1, 4) * P
                    nc.scalar.activation(pT[:, 0:n], ps[:, 4, 0:n], ACT.Copy).then_inc(s_("ptA_ready"), 1)
                    if i >= 4:
                        act.wait_ge(s_("ptB_done"), 8 * c + 4 * (m // 8) + i - 3)
                        nc.scalar.activation(pT[:, 512:(i + 1) * P], ps[:, 5, 0:(i - 3) * P], ACT.Copy).then_inc(s_("ptB_ready"), 1)
                    if m < 14:
                        expo(m + 2)

            def soft_exp(b, s):
                act.wait_ge(s_("s_shift"), b + 1)
                nc.scalar.activation(p_tok, s_tok[s], ACT.Exp).then_inc(s_("ptok_ready"), 1)

            def page_copy(n, r):
                act.wait_ge(s_("ctr_done"), n)
                nc.scalar.activation(cT_ring[r], ps[:, r, 0:LC * P].rearrange("p (k c) -> p k c", c=P), ACT.Copy)
                nc.scalar.activation(kpeT_ring[r], ps[0:DR, r, LC * P:LC * P + P], ACT.Copy).then_inc(s_("ctr_ready"), 1)

            def seq_act(b, s, prev, last):
                for g in range(NPAGE):
                    r = g % 2
                    if g < NPAGE - 1 or not last:
                        page_copy(NPAGE * b + g + 2, 1 - r)
                    act.wait_ge(s_("k_done"), NPAGE * b + g + 1)
                    if g >= 2 or prev:
                        act.wait_ge(s_("ksum_done"), NPAGE * b + g - 1)
                    nc.scalar.activation(ksq[r], ps[:, 2 + r, :], ACT.Square).then_inc(s_("ksq_ready"), 1)
                    if g == 6 and prev:
                        soft_exp(b - 1, 1 - s)

            def chunk_copy(c):
                act.wait_ge(s_("yT_done"), c + 1)
                nc.scalar.activation(conv_tok[:, 0:TILES, bass.ds(c * P, P)],
                                     ps[:, 2:4, :].rearrange("p a (k c) -> p (a k) c", c=P), ACT.Copy)
                nc.scalar.activation(conv_tok[0:NS, TILES, bass.ds(c * P, P)], ps[0:NS, 6, 384:384 + P], ACT.Copy).then_inc(s_("yT_ready"), 1)
            page_copy(1, 0)
            seq_act(0, 0, False, False)
            seq_act(1, 1, True, False)
            chunk_copy(0)
            with ch.loop(NSEQ // 2 - 2, 0) as p:
                seq_act(2 * p + 2, 0, True, False)
                seq_act(2 * p + 3, 1, True, False)
                chunk_copy(p + 1)
            seq_act(NSEQ - 2, 0, True, False)
            seq_act(NSEQ - 1, 1, True, True)
            chunk_copy(CCH - 1)
            soft_exp(NSEQ - 1, 1)
            act.wait_ge(s_("ov_done"), 1)
            nc.scalar.activation(attn_tok[0:NS, TILES, :], ps[0:NS, 0, :], ACT.Copy).then_inc(s_("s_done"), 1)

            def x2_square(t, rows):
                act.wait_ge(s_("x2_ready"), t + 1)
                nt_act(act, "c", t + 1, x2[0:rows, bass.ds(t, 1), :].rearrange("p a n -> p (a n)"), rows, 0, c_scr)

            def mix_act(t, rows):
                act.wait_ge(s_("centred"), t + 1)
                nc.scalar.activation(c_scr[0:rows, CC:2 * CC], conv_n[0:rows, :], ACT.Square, accum_out=st(24)[0:rows]).then_inc(s_("var_sumsq"), 1)
                nc.scalar.activation(c_scr[0:rows, 0:CC], attn_tok[0:rows, bass.ds(t, 1), :].rearrange("p a n -> p (a n)"),
                                     ACT.Square, accum_out=st(16)[0:rows])
                act.wait_ge(s_("ln_ready"), t + 1)
                ch.link(nc.scalar.activation(conv_n[0:rows, :], conv_n[0:rows, :], ACT.Silu))
                nc.scalar.activation(c_scr[0:rows, CC:2 * CC], conv_n[0:rows, :], ACT.Square,
                                     accum_out=st(17)[0:rows]).then_inc(s_("mix_sumsq"), 1)

            def tile_c(t, s, rows, v, ahead):
                if not first(t):
                    x2_square(t - 1, P)
                if ahead:
                    mix_act(t + 1, ahead)
            act.wait_ge(s_("s_done"), 1)
            mix_act(0, P)
            tiles(ch, 2, tile_c)
            x2_square(TILES, NS)

            def split_high(s, loads, used):
                act.wait_ge(s_(f"gu_loaded{s}"), 32 * loads)
                if used is not None:
                    act.wait_ge(s_("up_done"), used)
                nc.scalar.activation(w_hi_r[s], w_raw[s], ACT.Copy).then_inc(s_("w_hi_ready"), 1)

            def ffn_act(g, start, end):
                for s in range(2):
                    if not (end and s == 1):
                        split_high(1 - s, g + 1 + s, None if start and s == 0 else 6 * g + 3 * s)
                    if s == 0:
                        act.wait_ge(s_("wd_loaded"), 32 * (g + 1))
                        if not start:
                            act.wait_ge(s_("dn_done"), 2 * NT * g)
                        for a in range(2):
                            last = nc.scalar.activation(wd_hi_r[:, a, :], wd_raw[a], ACT.Copy)
                        last.then_inc(s_("wd_hi_ready"), 1)
                    for b, (at, n) in enumerate(BLOCKS):
                        act.wait_ge(s_("gate_done"), 6 * g + 3 * s + b + 1)
                        nc.scalar.activation(gate_s[:, at:at + n], ps[:, 2 * b, 0:n], ACT.Silu).then_inc(s_("silu_ready"), 1)
            act.wait_ge(s_("c_wout_done"), NT)
            split_high(0, 1, None)
            act.wait_ge(s_("c_hT"), NT)
            ffn_act(0, True, False)
            with act.Fori(1, GROUPS - 1) as g:
                ffn_act(g, False, False)
            ffn_act(GROUPS - 1, False, True)

            act.wait_ge(s_("dn_evac"), 2 * NT * GROUPS)

            def pT_copy(n, rows):
                act.wait_ge(s_("ppT_done"), n)
                nc.scalar.activation(p_T[:, :, 0:rows], ps[:, 2, 0:2 * P].rearrange("p (k c) -> p k c", c=P)[:, :, 0:rows], ACT.Copy)\
                    .then_inc(s_("ppT_ready"), 1)

            def tile_d(t, s, rows, v, ahead):
                if ahead:
                    act.wait_ge(s_("d_ms"), t + 1)
                    nt_act(act, "d", t + 2, x2[0:ahead, bass.ds(t + 1, 1), :].rearrange("p a n -> p (a n)"), ahead, 0, junk4)
                act.wait_ge(s_("pg_done"), t + 1)
                if not first(t):
                    act.wait_ge(s_("y_ready"), t)
                nc.scalar.activation(sg[0:rows, :], ps[0:rows, 3:5, :].rearrange("p a n -> p (a n)"), ACT.Sigmoid).then_inc(s_("sg_ready"), 1)
                if ahead:
                    pT_copy(t + 2, ahead)
            nt_act(act, "d", 1, x2[:, 0, :], P, 0, junk4)
            pT_copy(1, P)
            tiles(ch, 0, tile_d)

        @block.vector
        def _(dve):
            ch = Chain(dve, s_("dve_own"))
            dve.wait_ge(s_("gains"), 16 * 8)
            dve.wait_ge(s_("pool_consts"), 1)
            ch.link(nc.vector.tensor_tensor(g_qn[:, :], g_qn[:, :], g_kn[:, :], ALU.mult))
            ch.link(nc.vector.tensor_scalar(g_qn[:, :], g_qn[:, :], SCALE, None, ALU.mult))
            ch.link(nc.vector.tensor_scalar(g_qpe[:, :], g_qpe[:, :], SCALE, None, ALU.mult))
            dve.wait_ge(s_("colT_done"), 1)
            nc.vector.tensor_copy(gcol[:, :], ps[:, P0, 0:NCOL])
            ch.link(nc.vector.tensor_copy(tapw[:, :, :], ps[:, P1, 0:CCH * CK].rearrange("p (c k) -> p c k", k=CK)))

            def rotate(out1, out2, x1, x2_, cos, sin, a, b, c, d):
                nc.vector.tensor_tensor(a, x1, cos, ALU.mult)
                nc.vector.tensor_tensor(b, x2_, sin, ALU.mult)
                nc.vector.tensor_tensor(c, x2_, cos, ALU.mult)
                ch.link(nc.vector.tensor_tensor(d, x1, sin, ALU.mult))
                nc.vector.tensor_tensor(out1, a, b, ALU.subtract)
                return nc.vector.tensor_tensor(out2, c, d, ALU.add)

            def lat_dve(t, rows):
                r = slice(0, rows)
                if not first(t):
                    dve.wait_ge(s_("lat_stored"), 32 * t)
                dve.wait_ge(s_("z_sumsq"), t + 1)
                ch.link(nc.vector.tensor_tensor(st(12, 3)[r], st(8, 3)[r], inv_n[r, 0:3], ALU.mult))
                nc.vector.tensor_scalar(st(12, 3)[r], st(12, 3)[r], EPS, None, ALU.add).then_inc(s_("msz_ready"), 1)
                dve.wait_ge(s_("rstd_z"), t + 1)
                nc.vector.scalar_tensor_tensor(cqn[r, :], ps[r, Z0, 0:QL], st(16)[r], g_q[r, :], ALU.mult, ALU.mult)
                ch.link(nc.vector.scalar_tensor_tensor(kn[r, :], ps[r, Z1, KL:KL + DR], st(18)[r], g_kpe[r, :], ALU.mult, ALU.mult))
                nc.vector.scalar_tensor_tensor(ckvn[r, :], ps[r, Z1, 0:KL], st(17)[r], g_kv[r, :], ALU.mult, ALU.mult).then_inc(s_("lat_ready"), 1)
                cos = rope[r, bass.ds(t, 1), 0:HD2].rearrange("p a n -> p (a n)")
                sin = rope[r, bass.ds(t, 1), HD2:DR].rearrange("p a n -> p (a n)")
                rotate(kr[r, 0:HD2], kr[r, HD2:DR], kn[r, 0:HD2], kn[r, HD2:DR], cos, sin,
                       *(rk[r, j, :] for j in range(4))).then_inc(s_("kpe_ready"), 1)

            def glu_dve(t, rows):
                dve.wait_ge(s_("sig_ready"), t + 1)
                nc.vector.tensor_tensor(glu_t[0:rows, :], ps[0:rows, Z2, :], sig[0:rows, :], ALU.mult).then_inc(s_("glu_ready"), 1)

            def qk_dve(t, rows):
                r = slice(0, rows)
                dve.wait_ge(s_("q_sq"), t + 1)
                sqh = sq[r, :, :].rearrange("p a (h d) -> p (a h) d", d=DQ)
                nc.vector.reduce_sum(st(20, NH)[r], sqh[:, :, 0:DN], AXX)
                nc.vector.reduce_sum(st(28, NH)[r], sqh[:, :, DN:DQ], AXX)
                dve.wait_ge(s_("k_sq"), t + 1)
                ch.link(nc.vector.reduce_sum(st(36, NH)[r], k_scr[r, 0:NH * DN].rearrange("p (h d) -> p h d", d=DN), AXX))
                ch.link(nc.vector.tensor_tensor(st(50, 24)[r], st(20, 24)[r], inv_n[r, 3:27], ALU.mult))
                nc.vector.tensor_scalar(st(50, 24)[r], st(50, 24)[r], EPS, None, ALU.add).then_inc(s_("msq_ready"), 1)
                dve.wait_ge(s_("rstd_q"), t + 1)
                qv = ps[r, P0:P0 + 2, 0:QL].rearrange("p a (h d) -> p a h d", d=DQ)
                qh4 = qh[r, :, :].rearrange("p (a h) d -> p a h d", a=2)
                rq = st(80, NH)[r].rearrange("p (a h) -> p a h", a=2)
                rp = st(88, NH)[r].rearrange("p (a h) -> p a h", a=2)
                nc.vector.tensor_tensor(qh4[:, :, :, 0:DN], qv[:, :, :, 0:DN], rq.unsqueeze(3).to_broadcast([rows, 2, 4, DN]), ALU.mult)
                ch.link(nc.vector.tensor_tensor(qh4[:, :, :, DN:DQ], qv[:, :, :, DN:DQ], rp.unsqueeze(3).to_broadcast([rows, 2, 4, DR]), ALU.mult))
                nc.vector.tensor_tensor(qh[r, :, 0:DN], qh[r, :, 0:DN], g_qn[r, :].unsqueeze(1).to_broadcast([rows, NH, DN]), ALU.mult)
                ch.link(nc.vector.tensor_tensor(qh[r, :, DN:DQ], qh[r, :, DN:DQ], g_qpe[r, :].unsqueeze(1).to_broadcast([rows, NH, DR]), ALU.mult))
                cosb = rope[r, bass.ds(t, 1), 0:HD2].to_broadcast([rows, NH, HD2])
                sinb = rope[r, bass.ds(t, 1), HD2:DR].to_broadcast([rows, NH, HD2])
                rotate(qh[r, :, DN:DN + HD2], qh[r, :, DN + HD2:DQ], qh[r, :, DN:DN + HD2], qh[r, :, DN + HD2:DQ],
                       cosb, sinb, *(rt[r, j, :, :] for j in range(4))).then_inc(s_("qh_ready"), 1)
                dve.wait_ge(s_("qh_ready"), t + 1)
                nc.vector.tensor_tensor(kh[r, :, 0:DN], ps[r, Z2, :].rearrange("p (h d) -> p h d", d=DN),
                                        st(96, NH)[r].unsqueeze(2).to_broadcast([rows, NH, DN]), ALU.mult)
                dve.wait_ge(s_("kpe_ready"), t + 1)
                nc.vector.tensor_copy(kh[r, :, DN:DQ], kr[r, :].unsqueeze(1).to_broadcast([rows, NH, DR])).then_inc(s_("kh_ready"), 1)

            def kT_dve(t, rows):
                dve.wait_ge(s_("kT_done"), t + 1)
                src = ps[0:DQ, P0:P0 + 2, :].rearrange("p a (k c) -> p (a k) c", c=P)[:, :, 0:rows]
                dst = kT[:, :, bass.ds(t * P, P)] if rows == P else kT_s[:, :, :]
                nc.vector.tensor_copy(dst, src).then_inc(s_("kT_ready"), 1)

            def tile_a(t, s, rows, v, ahead):
                if not first(t):
                    qk_dve(t - 1, P)
                    kT_dve(t - 1, P)
                lat_dve(t, rows)
                if ahead:
                    nt_dve_scale(dve, "a", t + 2, x_in[1 - s][0:ahead, :], ahead, 0, x_in[1 - s])
                glu_dve(t, rows)
                if ahead:
                    nt_dve_gain(dve, "a", t + 2, ahead, T0, "norm_mix", hT[:, :, 0:ahead])
            nt_dve_scale(dve, "a", 1, x_in[0], P, 0, x_in[0])
            nt_dve_gain(dve, "a", 1, P, T0, "norm_mix", hT)
            tiles(ch, 16, tile_a)
            qk_dve(TILES, NS)
            kT_dve(TILES, NS)
            nc.vector.tensor_copy(ckv_keep[:, :], ckvn[0:NS, :]).then_inc(s_("ckv_kept"), 1)
            dve.wait_ge(s_("hist_ready"), 1)
            dve.wait_ge(s_("out_stored"), 16 * (NSEQ + 1))

            dve.wait_ge(s_("self_place"), 1)
            dve.wait_ge(s_("self_done"), 1)
            nc.vector.tensor_tensor(s_self[0:NS, :, :, :].rearrange("p h b q -> p h (b q)"),
                                    ps[0:NS, 7, :].rearrange("p (h n) -> p h n", h=NH),
                                    self_mask[:, :].unsqueeze(1).to_broadcast([NS, NH, NS]), ALU.add).then_inc(s_("self_ready"), 1)
            dve.wait_ge(s_("self_ready"), 1)

            with ch.loop(NH // 2, 32) as c:
                def s_view(m):
                    return ps[:, 2 * (m % 2):2 * (m % 2) + 2, :].rearrange("p a n -> p (a n)")

                def row_max(m):
                    i = m % 8
                    dve.wait_ge(s_("scores_done"), 16 * c + m + 1)
                    d = s_view(m)[:, i * P:(i + 1) * P]
                    ch.link(nc.vector.tensor_tensor(d, d, causal[:, :], ALU.add))
                    nc.vector.tensor_reduce(st(120 + m), s_view(m)[:, 0:(i + 1) * P], AXX, ALU.max, negate=True).then_inc(s_("nmax_ready"), 1)

                def out_rows(m):
                    i = m % 8
                    dve.wait_ge(s_("pv_done"), 16 * c + m + 1)
                    ch.link(nc.vector.reciprocal(st(136 + m), st(136 + m)))
                    nc.vector.tensor_scalar(attn_tok[:, i, bass.ds((2 * c + m // 8) * DV, DV)], ps[:, 6 + m % 2, 0:DV],
                                            st(136 + m), None, ALU.mult).then_inc(s_("o_evac"), 1)

                row_max(0)
                row_max(1)
                for m in range(16):
                    if m < 14:
                        row_max(m + 2)
                    out_rows(m)
            def w_(c, k):
                return tapw[:, bass.ds(c, 1), k:k + 1].rearrange("p a n -> p (a n)")

            def tap(c, k):
                src = glu[:, bass.ds(c, 1), k:k + SEQ].rearrange("p a n -> p (a n)")
                src_s = glu_s[:, bass.ds(c, 1), :, k:k + TQ].rearrange("p a b n -> p (a b) n")
                if k == 0:
                    bias = gcol[:, bass.ds(c + COLS["conv_b"][0], 1)]
                    nc.vector.tensor_scalar(y_c, src, w_(c, k), bias, ALU.mult, ALU.add)
                    ch.link(nc.vector.tensor_scalar(y_s, src_s, w_(c, k), bias, ALU.mult, ALU.add))
                else:
                    nc.vector.scalar_tensor_tensor(y_c, src, w_(c, k), y_c, ALU.mult, ALU.add)
                    ins = nc.vector.scalar_tensor_tensor(y_s, src_s, w_(c, k), y_s, ALU.mult, ALU.add)
                    if k == CK - 1:
                        ins.then_inc(s_("y_ready_c"), 1)
                    else:
                        ch.link(ins)
            def col_max(b, s):
                nc.vector.tensor_reduce(m_part, s_tok[s].rearrange("p g n -> p n g"), AXX, ALU.max).then_inc(s_("mpart_ready"), 1)

            def row_of_max(b, s):
                dve.wait_ge(s_("mT_done"), b + 1)
                ch.link(nc.vector.reduce_max(st(107)[0:NS], ps[0:NS, 6, 0:P], AXX))
                nc.vector.tensor_copy(m_row[0:NS, :], st(107)[0:NS].to_broadcast([NS, P])).then_inc(s_("mrow_ready"), 1)

            def shift(b, s):
                dve.wait_ge(s_("mB_done"), b + 1)
                nc.vector.tensor_tensor(s_tok[s], s_tok[s], ps[:, 6, P:P + NS].unsqueeze(1).to_broadcast([P, NPAGE + 1, NS]),
                                        ALU.subtract).then_inc(s_("s_shift"), 1)

            def out_lat(b, s):
                dve.wait_ge(s_("pv_s_done"), b + 1)
                ch.link(nc.vector.reciprocal(st(105)[0:NS], ps[0:NS, 7, KL:KL + 1]))
                nc.vector.tensor_scalar(o_lat[0:NS, :], ps[0:NS, 7, 0:KL], st(105)[0:NS], None, ALU.mult).then_inc(s_("olat_ready"), 1)

            def out_latT(b, s):
                dve.wait_ge(s_("olT_done"), b + 1)
                for c in range(LC):
                    last = nc.vector.tensor_copy(oT_lat[:, c, :, bass.ds(b, 1), :].rearrange("p h a q -> p (h a) q"),
                                                 ps[:, 6, 256 + c * NS:256 + (c + 1) * NS].rearrange("p (h q) -> p h q", q=TQ))
                last.then_inc(s_("olT_ready"), 1)

            def quad(b, s, q):
                dve.wait_ge(s_("rstdk_ready"), 4 * b + q + 1)
                dve.wait_ge(s_("sc_done"), 4 * b + q + 1)
                sc = ps[:, 4 + q % 2, :].rearrange("p (g k n) -> p g k n", g=4, k=2)
                ch.link(nc.vector.tensor_tensor(s_part, sc[:, :, 0, :].rearrange("p g (h q) -> p g h q", q=TQ),
                                                rstd_k[:, 4 * q:4 * q + 4, :].unsqueeze(3).to_broadcast([P, 4, NH, TQ]), ALU.mult))
                nc.vector.tensor_tensor(s_tok[s][:, 4 * q:4 * q + 4, :], s_part.rearrange("p g h q -> p g (h q)"),
                                        sc[:, :, 1, :], ALU.add).then_inc(s_("sc_used"), 1)

            def last_quad(b, s):
                quad(b, s, 3)
                ch.link(nc.vector.tensor_copy(s_tok[s][:, NPAGE, :].rearrange("p (h q) -> p h q", q=TQ),
                                              s_self[:, :, bass.ds(b, 1), :].rearrange("p h a q -> p (h a) q")))
                dve.wait_ge(s_("sc_used"), 4 * b + 4)
                col_max(b, s)

            def seq_dve(b, s, prev, c):
                for g in range(NPAGE):
                    q = g // 4
                    dve.wait_ge(s_("ksq_ready"), NPAGE * b + g + 1)
                    nc.vector.reduce_sum(ms_k[:, g, :], ksq[g % 2].rearrange("p (h d) -> p h d", d=DN), AXX)\
                        .then_inc(s_("ksum_done"), 1)
                    if NPAGE * s + g < CK:
                        tap(c, NPAGE * s + g)
                    if g % 4 == 3:
                        dve.wait_ge(s_("ksum_done"), NPAGE * b + g + 1)
                        nc.vector.tensor_scalar(ms_k[:, 4 * q:4 * q + 4, :], ms_k[:, 4 * q:4 * q + 4, :], 1.0 / DN, EPS,
                                                ALU.mult, ALU.add).then_inc(s_("msk_ready"), 1)
                    if g in (5, 9, 13):
                        quad(b, s, (g - 5) // 4)
                    if prev and g == 1:
                        last_quad(b - 1, 1 - s)
                    if prev and g == 3:
                        row_of_max(b - 1, 1 - s)
                    if prev and g == 4:
                        shift(b - 1, 1 - s)
                    if prev and g == 11:
                        out_lat(b - 1, 1 - s)
                    if prev and g == 14:
                        out_latT(b - 1, 1 - s)
                if s == 1:
                    dve.wait_ge(s_("yT_done"), c + 1)
            seq_dve(0, 0, False, 0)
            seq_dve(1, 1, True, 0)
            with ch.loop(NSEQ // 2 - 1, 44) as p:
                for s in range(2):
                    seq_dve(2 * p + s + 2, s, True, p + 1)
            last_quad(NSEQ - 1, 1)
            row_of_max(NSEQ - 1, 1)
            shift(NSEQ - 1, 1)
            out_lat(NSEQ - 1, 1)
            out_latT(NSEQ - 1, 1)

            dve.wait_ge(s_("s_done"), 1)

            def mix_dve(t, rows):
                r = slice(0, rows)
                cv = conv_tok[r, bass.ds(t, 1), :].rearrange("p a n -> p (a n)")
                ch.link(nc.vector.reduce_sum(st(4)[r], cv, AXX))
                ch.link(nc.vector.tensor_scalar(st(5)[r], st(4)[r], 1.0 / CC, None, ALU.mult))
                nc.vector.tensor_scalar(conv_n[r, :], cv, st(5)[r], None, ALU.subtract).then_inc(s_("centred"), 1)
                dve.wait_ge(s_("var_sumsq"), t + 1)
                nc.vector.tensor_scalar(st(7)[r], st(24)[r], 1.0 / CC, EPS, ALU.mult, ALU.add).then_inc(s_("var_ready"), 1)
                dve.wait_ge(s_("ln_loaded"), 32)
                dve.wait_ge(s_("rstd_ln"), t + 1)
                ch.link(nc.vector.scalar_tensor_tensor(conv_n[r, :], conv_n[r, :], st(6)[r], ln_g[r, :], ALU.mult, ALU.mult))
                nc.vector.tensor_tensor(conv_n[r, :], conv_n[r, :], ln_b[r, :], ALU.add).then_inc(s_("ln_ready"), 1)
                dve.wait_ge(s_("mix_sumsq"), t + 1)
                nc.vector.tensor_scalar(st(20, 2)[r], st(16, 2)[r], 1.0 / CC, EPS, ALU.mult, ALU.add).then_inc(s_("msm_ready"), 1)
                dve.wait_ge(s_("rstd_m"), t + 1)
                nc.vector.tensor_scalar(mixn[r, 0:CC], attn_tok[r, bass.ds(t, 1), :].rearrange("p a n -> p (a n)"), st(22)[r], None, ALU.mult)
                nc.vector.tensor_scalar(mixn[r, CC:2 * CC], conv_n[r, :], st(23)[r], None, ALU.mult).then_inc(s_("m_xn"), 1)

            def x2_dve(t, s, v, rows):
                r = slice(0, rows)
                xv = x2[r, bass.ds(t, 1), :].rearrange("p a n -> p (a n)")
                dve.wait_ge(s_(f"xr_loaded{s}"), 16 * v)
                dve.wait_ge(s_("c_wout_done"), t + 1)
                nc.vector.tensor_tensor(xv, ps[r, 2:4, :].rearrange("p a n -> p (a n)"), xr[s][r, :], ALU.add).then_inc(s_("x2_ready"), 1)
                nt_dve_scale(dve, "c", t + 1, xv, rows, 0, xn2)

            def tile_c(t, s, rows, v, ahead):
                if not first(t):
                    x2_dve(t - 1, 1 - s, v if s == 1 else v - 1, P)
                if ahead:
                    mix_dve(t + 1, ahead)
                    nt_dve_gain(dve, "m", t + 2, ahead, 0, "norm_out_attn", mT[:, :, 0:ahead])
                if not first(t):
                    one = lambda v: v[:, bass.ds(t - 1, 1)].rearrange("p a k c -> p (a k) c")
                    nt_dve_gain(dve, "c", t, P, 4, "norm_ffn", one(h_full))
                    dve.wait_ge(s_("c_hT"), t)
                    ch.link(nc.vector.tensor_copy(one(h_hi_r), one(h_full)))
                    nc.vector.tensor_tensor(one(h_lo_r), one(h_full), one(h_hi), ALU.subtract).then_inc(s_("h_split"), 1)
            mix_dve(0, P)
            nt_dve_gain(dve, "m", 1, P, 0, "norm_out_attn", mT)
            tiles(ch, 8, tile_c)
            x2_dve(TILES, 0, TILES // 2 + 1, NS)
            nt_dve_gain(dve, "c", NT, NS, 4, "norm_ffn", h_s)

            def split_low(s, n):
                dve.wait_ge(s_("w_hi_ready"), n)
                nc.vector.tensor_tensor(w_lo_r[s], w_raw[s], w_hi[s], ALU.subtract).then_inc(s_("w_split"), 1)

            def ffn_dve(g, end):
                for s in range(2):
                    if not (end and s == 1):
                        split_low(1 - s, 2 * g + s + 2)
                    if s == 0:
                        dve.wait_ge(s_("wd_hi_ready"), g + 1)
                        for a in range(2):
                            last = nc.vector.tensor_tensor(wd_lo_r[:, a, :], wd_raw[a], wd_hi[:, a, :], ALU.subtract)
                        last.then_inc(s_("wd_split"), 1)
                    for b, (at, n) in enumerate(BLOCKS):
                        c = slice(at, at + n)
                        dve.wait_ge(s_("silu_ready"), 6 * g + 3 * s + b + 1)
                        dve.wait_ge(s_("up_done"), 6 * g + 3 * s + b + 1)
                        ch.link(nc.vector.tensor_tensor(gate_s[:, c], gate_s[:, c], ps[:, 2 * b + 1, 0:n], ALU.mult))
                        ch.link(nc.vector.tensor_copy(a_hi_r[s][:, c], gate_s[:, c]))
                        nc.vector.tensor_tensor(a_lo_r[s][:, c], gate_s[:, c], a_hi[s][:, c], ALU.subtract).then_inc(s_("aT_ready"), 1)
                for t in range(NT):
                    rows = P if t < TILES else NS
                    for h in range(2):
                        dve.wait_ge(s_("dn_done"), 2 * NT * g + 2 * t + h + 1)
                        d = x2[0:rows, t, h * HALF:(h + 1) * HALF]
                        nc.vector.tensor_tensor(d, d, ps[0:rows, 6 + h, :], ALU.add).then_inc(s_("dn_evac"), 1)
            split_low(0, 1)
            with ch.loop(GROUPS - 1, 12) as g:
                ffn_dve(g, False)
            ffn_dve(GROUPS - 1, True)

            dve.wait_ge(s_("dn_evac"), 2 * NT * GROUPS)

            def scale_d(t, rows):
                nt_dve_scale(dve, "d", t + 1, x2[0:rows, bass.ds(t, 1), :].rearrange("p a n -> p (a n)"), rows, 0, xn4)

            def tile_d(t, s, rows, v, ahead):
                r = slice(0, rows)
                if ahead:
                    scale_d(t + 1, ahead)
                    nt_dve_gain(dve, "d", t + 2, ahead, 0, "norm_ple", hT4[:, :, 0:ahead])
                dve.wait_ge(s_("sg_ready"), t + 1)
                dve.wait_ge(s_("pp_done"), t + 1)
                ch.link(nc.vector.tensor_tensor(sg[r, :], sg[r, :], ps[r, 5:7, :].rearrange("p a n -> p (a n)"), ALU.mult))
                nc.vector.tensor_tensor(y_out[s][r, :], sg[r, :], x2[r, bass.ds(t, 1), :].rearrange("p a n -> p (a n)"),
                                        ALU.add).then_inc(s_("y_ready"), 1)
                if not first(t):
                    dve.wait_ge(s_(f"y_stored{1 - s}"), 16 * (v if s == 1 else v - 1))
            scale_d(0, P)
            nt_dve_gain(dve, "d", 1, P, 0, "norm_ple", hT4)
            tiles(ch, 2, tile_d)

        @block.tensor
        def _(pe):
            ch = Chain(pe, s_("pe_own"))
            mm, tr = nc.tensor.matmul, nc.tensor.transpose
            pe.wait_ge(s_("ident_ready"), 1)
            pe.wait_ge(s_("consts"), 16 * (len(COLS) + 1))
            tr(ps[:, P0, 0:NCOL], gain_rows, ident[0:NCOL, 0:NCOL])
            for c in range(CCH):
                last = tr(ps[:, P1, c * CK:(c + 1) * CK], tap_rows[:, c * P:(c + 1) * P], ident[0:CK, 0:CK])
            last.then_inc(s_("colT_done"), 1)

            def qk_T(t, rows):
                pe.wait_ge(s_("qh_ready"), t + 1)
                for h in range(NH):
                    last = tr(ps[0:DQ, T0 + h // 4, (h % 4) * P:(h % 4) * P + rows], qh[0:rows, h, :], ident[0:rows, 0:rows])
                last.then_inc(s_("qT_done"), 1)
                pe.wait_ge(s_("kh_ready"), t + 1)
                for h in range(NH):
                    last = tr(ps[0:DQ, P0 + h // 4, (h % 4) * P:(h % 4) * P + rows], kh[0:rows, h, :], ident[0:rows, 0:rows])
                last.then_inc(s_("kT_done"), 1)

            def tile_a(t, s, rows, v, ahead):
                pe.wait_ge(s_("a_hT"), t + 1)
                if first(t):
                    pe.wait_ge(s_("w_lat_loaded"), 16)
                else:
                    pe.wait_ge(s_("gluT_ready"), t)
                for bank, c0, n in ((Z0, 0, QL), (Z1, QL, KL + DR)):
                    for k in range(KC):
                        last = mm(ps[0:rows, bank, 0:n], hT[:, k, 0:rows], w_in[:, k, c0:c0 + n], start=(k == 0), stop=(k == KC - 1))
                last.then_inc(s_("z_lat_done"), 1)
                if first(t):
                    pe.wait_ge(s_("w_glu_loaded"), 16)
                else:
                    qk_T(t - 1, P)
                    pe.wait_ge(s_("v_ready"), t)
                for bank, c0 in ((Z3, QL + KL + DR + CC), (Z2, QL + KL + DR)):
                    for k in range(KC):
                        last = mm(ps[0:rows, bank, :], hT[:, k, 0:rows], w_in[:, k, c0:c0 + CC], start=(k == 0), stop=(k == KC - 1))
                last.then_inc(s_("z_glu_done"), 1)
                if not first(t):
                    pe.wait_ge(s_("qT_ready"), t)
                if ahead:
                    nt_pe(pe, "a", t + 2, ahead, x_in[1 - s], T0)
                    pe.wait_ge(s_("a_hT"), t + 2)
                pe.wait_ge(s_("lat_ready"), t + 1)
                for k in range(5):
                    src = cqn[0:rows, k * P:(k + 1) * P] if k < 3 else ckvn[0:rows, (k - 3) * P:(k - 2) * P]
                    last = tr(ps[:, T0 + k // 4, (k % 4) * P:(k % 4) * P + rows], src, ident[0:rows, 0:rows])
                last.then_inc(s_("cT_done"), 1)
                pe.wait_ge(s_("glu_ready"), t + 1)
                for k in range(CCH):
                    last = tr(ps[:, Z0, k * P:k * P + rows], glu_t[0:rows, k * P:(k + 1) * P], ident[0:rows, 0:rows])
                last.then_inc(s_("gluT_done"), 1)
                if first(t):
                    pe.wait_ge(s_("w_u_loaded"), 48)
                else:
                    pe.wait_ge(s_("kT_ready"), t)
                pe.wait_ge(s_("cT_ready"), t + 1)
                for a in range(2):
                    for k in range(QL // P):
                        last = mm(ps[0:rows, P0 + a, 0:QL], cT[:, k, 0:rows], w_uq[:, k, a * QL:(a + 1) * QL], start=(k == 0), stop=(k == QL // P - 1))
                last.then_inc(s_("q_done"), 1)
                for bank, w in ((Z2, w_uk), (Z3, w_uv)):
                    for k in range(LC):
                        last = mm(ps[0:rows, bank, :], cT[:, 3 + k, 0:rows], w[:, k, :], start=(k == 0), stop=(k == LC - 1))
                last.then_inc(s_("kv_done"), 1)
            nt_pe(pe, "a", 1, P, x_in[0], T0)
            tiles(ch, 0, tile_a)
            qk_T(TILES, NS)
            pe.wait_ge(s_("hist_loaded"), 32)
            for a in range(2):
                for c in range(CCH):
                    last = tr(ps[:, Z2 + a, c * 120:(c + 1) * 120], hist[0:120, a, c * P:(c + 1) * P], ident[0:120, 0:120])
            last.then_inc(s_("hist_done"), 1)

            pe.wait_ge(s_("kT_ready"), NT)
            pe.wait_ge(s_("hist_ready"), 1)
            for h in range(NH):
                for k in range(LC):
                    last = tr(ps[0:DN, h // 2, (h % 2) * KL + k * P:(h % 2) * KL + (k + 1) * P], w_uk[:, k, h * DN:(h + 1) * DN], ident[:, :])
            last.then_inc(s_("wukT_done"), 1)
            for h in range(NH):
                last = mm(ps[0:NS, 7, h * NS:(h + 1) * NS], kT_s[:, h, :], qT_s[:, h, :], start=True, stop=True)
            last.then_inc(s_("self_done"), 1)
            pe.wait_ge(s_("wukT_ready"), 1)
            for h in range(NH):
                for k in range(LC):
                    last = mm(ps[:, 4 + k, h * NS:(h + 1) * NS], w_ukT[:, h, k * P:(k + 1) * P], qT_s[0:DN, h, :], start=True, stop=True)
            last.then_inc(s_("qabs_done"), 1)
            pe.wait_ge(s_("qabs_ready"), 1)
            pe.wait_ge(s_("self_ready"), 1)
            with ch.loop(NH // 2, 0) as c:
                def scores(m):
                    hp, i = m // 8, m % 8
                    if i == 0:
                        pe.wait_ge(s_("qTh_ready"), 2 * c + hp + 1)
                    n = (i + 1) * P
                    for a in range(0, n, 512):
                        w = min(512, n - a)
                        last = mm(ps[:, 2 * (m % 2) + a // 512, 0:w], qTh[hp][:, i * P:(i + 1) * P],
                                  kT[:, bass.ds(2 * c + hp, 1), a:a + w].rearrange("p a n -> p (a n)"), start=True, stop=True)
                    last.then_inc(s_("scores_done"), 1)
                scores(0)
                scores(1)
                for m in range(16):
                    hp, i = m // 8, m % 8
                    pe.wait_ge(s_("prob_ready"), 16 * c + m + 1)
                    for j in range(i + 1):
                        last = tr(ps[:, 4 + j // 4, (j % 4) * P:(j % 4 + 1) * P], prob[m % 2][:, j * P:(j + 1) * P], ident[:, :])
                        if j == min(i, 3):
                            last.then_inc(s_("ptA_done"), 1)
                    if i >= 4:
                        last.then_inc(s_("ptB_done"), 1)
                    if m < 14:
                        scores(m + 2)
                    if m >= 2:
                        pe.wait_ge(s_("o_evac"), 16 * c + m - 1)
                    pe.wait_ge(s_("ptA_ready"), 16 * c + m + 1)
                    for j in range(i + 1):
                        if j == 4:
                            pe.wait_ge(s_("ptB_ready"), 8 * c + 4 * hp + i - 3)
                        last = mm(ps[:, 6 + m % 2, 0:DV], pT[:, j * P:(j + 1) * P],
                                  V[:, j, bass.ds((2 * c + hp) * DV, DV)], start=(j == 0), stop=(j == i))
                    last.then_inc(s_("pv_done"), 1)
                pe.wait_ge(s_("o_evac"), 16 * c + 16)
            def page_T(s, g):
                r = g % 2
                for k in range(LC):
                    tr(ps[:, r, k * P:(k + 1) * P], pages[s][:, g, k * P:(k + 1) * P], ident[:, :])
                tr(ps[0:DR, r, LC * P:(LC + 1) * P], kpe[s][:, g, :], ident[:, :]).then_inc(s_("ctr_done"), 1)

            def seq_pe(b, s, prev, loads, next_loads):
                for g in range(NPAGE):
                    r, q = g % 2, g // 4
                    if g < NPAGE - 1:
                        if g == NPAGE // 2 - 1:
                            pe.wait_ge(s_(f"pages_loaded{s}1"), PAGES_HALF * loads)
                        page_T(s, g + 1)
                    elif next_loads is not None:
                        pe.wait_ge(s_(f"pages_loaded{1 - s}0"), PAGES_HALF * next_loads)
                        page_T(1 - s, 0)
                    pe.wait_ge(s_("ctr_ready"), NPAGE * b + g + 1)
                    if g >= 2 or prev:
                        pe.wait_ge(s_("ksq_ready"), NPAGE * b + g - 1)
                    for k in range(LC):
                        last = mm(ps[:, 2 + r, :], cT_ring[r][:, k, :], w_uk[:, k, :], start=(k == 0), stop=(k == LC - 1))
                    last.then_inc(s_("k_done"), 1)
                    if g % 4 == 0 and (q >= 2 or prev):
                        pe.wait_ge(s_("sc_used"), 4 * b + q - 1)
                    o = (g % 4) * P
                    for k in range(LC):
                        mm(ps[:, 4 + q % 2, o:o + NS], cT_ring[r][:, k, :], q_abs[:, k, :, bass.ds(b * TQ, TQ)], start=(k == 0), stop=(k == LC - 1))
                    last = mm(ps[:, 4 + q % 2, o + NS:o + 2 * NS], kpeT_ring[r], q_pe[:, :, bass.ds(b * TQ, TQ)], start=True, stop=True)
                    if g % 4 == 3:
                        last.then_inc(s_("sc_done"), 1)
                    if prev and g == 2:
                        max_T(b - 1)
                    if prev and g == 4:
                        max_B(b - 1)
                    if prev and g == 8:
                        pv(b - 1, 1 - s)
                    if prev and g == 13:
                        lat_T(b - 1)

            def chunk_T(b, c):
                pe.wait_ge(s_("ksq_ready"), NPAGE * b + NPAGE)
                pe.wait_ge(s_("olT_ready"), b)
                pe.wait_ge(s_("y_ready_c"), c + 1)
                for t in range(TILES):
                    tr(ps[:, 2 + t // 4, (t % 4) * P:(t % 4 + 1) * P], y_c[:, t * P:(t + 1) * P], ident[:, :])
                tr(ps[0:NS, 6, 384:384 + P], y_s.rearrange("p b q -> p (b q)"), ident[:, :]).then_inc(s_("yT_done"), 1)
                pe.wait_ge(s_("yT_ready"), c + 1)

            def max_T(b):
                pe.wait_ge(s_("mpart_ready"), b + 1)
                mm(ps[0:NS, 6, 0:P], m_part, ident[:, :], start=True, stop=True).then_inc(s_("mT_done"), 1)

            def max_B(b):
                pe.wait_ge(s_("mrow_ready"), b + 1)
                mm(ps[:, 6, P:P + NS], m_row[0:NS, :], ident[0:NS, 0:NS], start=True, stop=True).then_inc(s_("mB_done"), 1)

            def pv(b, s):
                pe.wait_ge(s_("ptok_ready"), b + 1)
                for g in range(NPAGE + 1):
                    last = mm(ps[0:NS, 7, 0:KL + 1], p_tok[:, g, :], pages[s][:, g, :], start=(g == 0), stop=(g == NPAGE))
                last.then_inc(s_("pv_s_done"), 1)

            def lat_T(b):
                pe.wait_ge(s_("olat_ready"), b + 1)
                for k in range(LC):
                    last = mm(ps[:, 6, 256 + k * NS:256 + (k + 1) * NS], o_lat[0:NS, k * P:(k + 1) * P], ident[0:NS, 0:NS], start=True, stop=True)
                last.then_inc(s_("olT_done"), 1)
            pe.wait_ge(s_("pages_loaded00"), PAGES_HALF)
            page_T(0, 0)
            seq_pe(0, 0, False, 1, 1)
            seq_pe(1, 1, True, 1, 2)
            chunk_T(1, 0)
            with ch.loop(NSEQ // 2 - 2, 0) as p:
                seq_pe(2 * p + 2, 0, True, p + 2, p + 2)
                seq_pe(2 * p + 3, 1, True, p + 2, p + 3)
                chunk_T(2 * p + 3, p + 1)
            seq_pe(NSEQ - 2, 0, True, NSEQ // 2, NSEQ // 2)
            seq_pe(NSEQ - 1, 1, True, NSEQ // 2, None)
            chunk_T(NSEQ - 1, CCH - 1)
            max_T(NSEQ - 1)
            max_B(NSEQ - 1)
            pv(NSEQ - 1, 1)
            lat_T(NSEQ - 1)
            pe.wait_ge(s_("olT_ready"), NSEQ)
            for h in range(NH):
                for k in range(LC):
                    last = mm(ps[0:NS, 0, h * DV:(h + 1) * DV], oT_lat[:, k, h, :, :].rearrange("p b q -> p (b q)"),
                              w_uv[:, k, h * DV:(h + 1) * DV], start=(k == 0), stop=(k == LC - 1))
            last.then_inc(s_("ov_done"), 1)
            pe.wait_ge(s_("s_done"), 1)

            pe.wait_ge(s_("w_out_loaded"), 16)

            def tile_c(t, s, rows, v, ahead):
                pe.wait_ge(s_("m_hT"), t + 1)
                if not first(t):
                    pe.wait_ge(s_("x2_ready"), t)
                for h in range(2):
                    for k in range(KC):
                        last = mm(ps[0:rows, 2 + h, :], mT[:, k, 0:rows], w_out[:, k, h * HALF:(h + 1) * HALF], start=(k == 0), stop=(k == KC - 1))
                last.then_inc(s_("c_wout_done"), 1)
                if ahead:
                    nt_pe(pe, "m", t + 2, ahead, mixn, 0)
                if not first(t):
                    nt_pe(pe, "c", t, P, xn2, 4)
            nt_pe(pe, "m", 1, P, mixn, 0)
            tiles(ch, 0, tile_c)
            nt_pe(pe, "c", NT, NS, xn2, 4)

            pe.wait_ge(s_("c_hT"), NT)

            def split_mm(out, left, right, start, stop):
                mm(out, left[0], right[0], start=start, stop=False)
                mm(out, left[0], right[1], start=False, stop=False)
                return mm(out, left[1], right[0], start=False, stop=stop)

            def group(g, start):
                for s in range(2):
                    for b, (at, n) in enumerate(BLOCKS):
                        if b == 0:
                            pe.wait_ge(s_(f"gu_loaded{s}"), 32 * (g + 1))
                        if b == 1:
                            pe.wait_ge(s_("w_split"), 2 * g + s + 1)
                            if start:
                                pe.wait_ge(s_("h_split"), TILES)
                        if not (start and s == 0):
                            pe.wait_ge(s_("aT_ready"), 6 * g + 3 * (s - 1) + b + 1)
                        for u, done in enumerate(("gate_done", "up_done")):
                            out = ps[:, 2 * b + u, 0:n]
                            for k in range(KC):
                                ends = dict(start=(k == 0), stop=(k == KC - 1))
                                if b == 0:
                                    last = mm(out, w_raw[s][:, u, k, :], h_s[:, k, :], **ends)
                                else:
                                    tt = slice(at // P, (at + n) // P)
                                    last = split_mm(out.rearrange("p (t c) -> p t c", c=P),
                                                    (w_hi_r[s][:, u, k, :], w_lo_r[s][:, u, k, :]),
                                                    (h_hi_r[:, tt, k, :], h_lo_r[:, tt, k, :]), **ends)
                            last.then_inc(s_(done), 1)
                pe.wait_ge(s_("wd_split"), g + 1)
                for t in range(NT):
                    rows = P if t < TILES else NS
                    b = [i for i, (at, n) in enumerate(BLOCKS) if at <= t * P < at + n][0]
                    pe.wait_ge(s_("aT_ready"), 6 * g + 3 + b + 1)
                    c = slice(t * P, t * P + rows)
                    for h in range(2):
                        if not (start and t == 0):
                            pe.wait_ge(s_("dn_evac"), 2 * NT * g + 2 * (t - 1) + h + 1)
                        e = slice(h * HALF, (h + 1) * HALF)
                        for s in range(2):
                            last = split_mm(ps[0:rows, 6 + h, :], (a_hi_r[s][:, c], a_lo_r[s][:, c]),
                                            (wd_hi_r[:, s, e], wd_lo_r[:, s, e]), start=(s == 0), stop=(s == 1))
                        last.then_inc(s_("dn_done"), 1)
            group(0, True)
            with pe.Fori(1, GROUPS) as g:
                group(g, False)

            pe.wait_ge(s_("dn_evac"), 2 * NT * GROUPS)

            def p_T_pe(n, s, count, rows):
                pe.wait_ge(s_(f"p_loaded{s}"), 16 * count)
                for k in range(PLE // P):
                    last = tr(ps[:, 2, k * P:k * P + rows], p_in[s][0:rows, k * P:(k + 1) * P], ident[0:rows, 0:rows])
                last.then_inc(s_("ppT_done"), 1)

            def tile_d(t, s, rows, v, ahead):
                pe.wait_ge(s_("d_hT"), t + 1)
                if not first(t):
                    pe.wait_ge(s_("sg_ready"), t)
                for h in range(2):
                    if first(t):
                        pe.wait_ge(s_(f"w_pg_loaded{h}"), 16)
                    for k in range(KC):
                        last = mm(ps[0:rows, 3 + h, :], hT4[:, k, 0:rows], w_pg[:, k, h * HALF:(h + 1) * HALF], start=(k == 0), stop=(k == KC - 1))
                last.then_inc(s_("pg_done"), 1)
                if ahead:
                    nt_pe(pe, "d", t + 2, ahead, xn4, 0)
                pe.wait_ge(s_("ppT_ready"), t + 1)
                if first(t):
                    pe.wait_ge(s_("w_pp_loaded"), 16)
                if not first(t):
                    pe.wait_ge(s_("y_ready"), t)
                for h in range(2):
                    for k in range(PLE // P):
                        last = mm(ps[0:rows, 5 + h, :], p_T[:, k, 0:rows], w_pp[:, k, h * HALF:(h + 1) * HALF], start=(k == 0), stop=(k == PLE // P - 1))
                last.then_inc(s_("pp_done"), 1)
                if ahead:
                    p_T_pe(t + 2, 1 - s, slot_count(t, s, v), ahead)
            p_T_pe(1, 0, 1, P)
            nt_pe(pe, "d", 1, P, xn4, 0)
            tiles(ch, 0, tile_d)


_INS = ["x_prompt", "x_sample", "cache_ckv", "cache_kpe", "state_conv", "page_table", "p_prompt", "p_sample",
        "norm_mix", "w_in", "q_lora_norm", "w_uq", "kv_norm", "w_uk", "w_uv", "q_nope_norm", "k_nope_norm",
        "q_pe_norm", "k_pe_norm", "conv_w", "conv_b", "conv_ln_g", "conv_ln_b", "norm_out_attn", "norm_out_conv",
        "w_out", "norm_ffn", "w_gate", "w_up", "w_down", "norm_ple", "w_ple_gate", "w_ple_proj"]
_OUTS = [(1, SEQ, DM), (NSEQ, TQ, DM), (1, 1, SEQ, KL), (1, 1, SEQ, DR), (1, 1, HIST, CC),
         (1, NSEQ, TQ, KL), (1, NSEQ, TQ, DR), (1, NSEQ, HIST, CC)]


def rope_rows():
    pos = np.concatenate([np.arange(SEQ), np.tile(PAST + np.arange(TQ), NSEQ)]).astype(np.float32)
    inv = (np.float32(1.0) / np.power(np.float32(10000.0), np.arange(0, DR, 2, dtype=np.float32) / np.float32(DR))).astype(np.float32)
    ang = pos[:, None] * inv[None, :]
    return np.concatenate([np.cos(ang), np.sin(ang)], axis=1).astype(np.float32)


def kernel(**inputs):
    import numpy as _np
    import concourse.bacc as _bacc
    from concourse import mybir as _mybir
    from concourse.bass_utils import run_bass_kernel_spmd as _run

    nc = _bacc.Bacc("TRN2", target_bir_lowering=False, num_devices=1, dynamic_dma_scratch_size=1024)
    arrays, args = {}, {}
    for name in _INS:
        a = _np.ascontiguousarray(inputs[name])
        arrays[f"in_{name}"] = a
        args[name] = nc.dram_tensor(f"in_{name}", a.shape, _mybir.dt.from_np(a.dtype), kind="ExternalInput").ap()
    arrays["in_rope"] = rope_rows()
    args["rope"] = nc.dram_tensor("in_rope", arrays["in_rope"].shape, _mybir.dt.float32, kind="ExternalInput").ap()
    outs = [nc.dram_tensor(f"out_{i}", shape, _mybir.dt.float32, kind="ExternalOutput").ap() for i, shape in enumerate(_OUTS)]
    build(nc, args, outs)
    r = _run(nc, [arrays], core_ids=[0])
    return tuple(r.results[0][f"out_{i}"] for i in range(len(_OUTS)))
```

```python
from contextlib import ExitStack, contextmanager

import numpy as np
import concourse.bass as bass
from concourse import mybir

P = 128
DM = 1024
SEQ = 1024
NSEQ, TQ = 8, 8
NS = NSEQ * TQ
PAST, PAGE = 2048, 128
NPAGE = PAST // PAGE
NH, DN, DR, DV = 8, 64, 32, 64
DQ = DN + DR
QL, KL = 384, 256
CC, CK = 512, 31
HIST = CK - 1
INW = QL + KL + DR + 2 * CC
DFF = 2816
PLE = 256
EPS = 1e-6
SCALE = 1.0 / float(np.sqrt(np.float32(DN + DR)))
NEG = -1e30
TILES = SEQ // P
NT = TILES + 1
NTOK = SEQ + NS
KC = DM // P
LC = KL // P
CCH = CC // P
HALF = 512
GROUPS = DFF // (2 * P)
PAIR = 2 * TILES
ORDER = [(hp, i) for hp in range(2) for i in range(TILES)]
PAGES_HALF = NPAGE // 2 * 2 * 16
BLOCKS = [(SEQ, NS), (0, 512), (512, 512)]

F32 = mybir.dt.float32
F32R = mybir.dt.float32r
I32 = mybir.dt.int32
ALU = mybir.AluOpType
ACT = mybir.ActivationFunctionType
AXX = mybir.AxisListType.X

COLS = {}
for _n, _k in (("norm_mix", 8), ("norm_out_attn", 4), ("norm_out_conv", 4), ("norm_ffn", 8),
               ("norm_ple", 8), ("conv_b", 4)):
    COLS[_n] = (sum(k for _, k in COLS.values()), _k)
NCOL = sum(k for _, k in COLS.values())


class Chain:

    def __init__(self, eng, sem):
        self.eng, self.sem, self.base, self.n = eng, sem, 0, 0

    def link(self, ins):
        self.n += 1
        ins.then_inc(self.sem, 1)
        self.eng.wait_ge(self.sem, self.base + self.n)

    @contextmanager
    def loop(self, count, per):
        before = self.n
        with self.eng.Fori(0, count) as i:
            self.base, self.n = i * per + before, 0
            yield i
            assert self.n == per, f"a loop's body links {self.n}"
        self.base, self.n = 0, before + count * per


def build(nc, A, O):
    ctx = ExitStack()
    with ctx:
        ctx.enter_context(nc.allow_non_contiguous_dma("weights by slices, gains broadcast"))
        def sb(name, shape, dt=F32):
            return ctx.enter_context(nc.sbuf_tensor(name, shape, dt))

        def sem(name):
            return ctx.enter_context(nc.semaphore(name))

        ident = sb("ident", [P, P])
        causal = sb("causal", [P, P])
        self_mask = sb("self_mask", [NS, NS])
        mhalf = sb("mhalf", [P, 4 * NH])
        inv_n = sb("inv_n", [P, 3 + 3 * NH])
        gcol = sb("gcol", [P, NCOL])
        g_q = sb("g_q", [P, QL])
        g_kv = sb("g_kv", [P, KL])
        g_kpe = sb("g_kpe", [P, DR])
        g_qn = sb("g_qn", [P, DN])
        g_qpe = sb("g_qpe", [P, DR])
        ckv_keep = sb("ckv_keep", [NS, KL])
        rope = sb("rope", [P, NT, DR])
        tapw = sb("tapw", [P, CCH, CK])
        table = sb("table", [1, NSEQ * NPAGE], I32)
        w_uk = sb("w_uk", [P, LC, NH * DN])
        w_uv = sb("w_uv", [P, LC, NH * DV])
        stats = sb("stats", [P, 160])
        glu_s = sb("glu_s", [P, CCH, NSEQ, HIST + TQ])
        qT_s = sb("qT_s", [DQ, NH, NS])
        kT_s = sb("kT_s", [DQ, NH, NS])
        arena_cols = 50500
        with nc.sbuf_tensor("arena", [P, arena_cols], F32) as arena:
            pass

        def window(name, at, shape, dt):
            n = int(np.prod(shape))
            with nc.sbuf_tensor(name + "_before", [P, at], F32):
                with nc.sbuf_tensor(name, [P, n], dt) as w:
                    pass
            v = w[:, :]
            if len(shape) == 2:
                v = v.rearrange("p (a b) -> p a b", b=shape[1])
            if len(shape) == 3:
                v = v.rearrange("p (a b c) -> p a b c", b=shape[1], c=shape[2])
            return v

        class Region:
            def __init__(self, start):
                self.at = start

            def take_window(self, name, *shape):
                at = self.at
                self.take(*shape)
                return window(name, at, shape, F32)

            def take_split(self, name, *shape):
                at = self.at
                self.take(*shape)
                part = window(name, at, shape, F32R)
                return part.bitcast(F32), part

            def take(self, *shape, rows=P):
                n = int(np.prod(shape))
                v = arena[0:rows, self.at:self.at + n]
                self.at += n
                assert self.at <= arena_cols, (self.at, arena_cols)
                if len(shape) == 2:
                    v = v.rearrange("p (a b) -> p a b", b=shape[1])
                if len(shape) == 3:
                    v = v.rearrange("p (a b c) -> p a b c", b=shape[1], c=shape[2])
                if len(shape) == 4:
                    v = v.rearrange("p (a b c d) -> p a b c d", b=shape[1], c=shape[2], d=shape[3])
                return v

        R = Region(0)
        qT = R.take(NH, SEQ, rows=DQ)
        kT = R.take(NH, SEQ, rows=DQ)
        V = R.take(TILES, NH * DV)
        glu_start = R.at
        glu = R.take(CCH, HIST + SEQ)
        shared_end = R.at
        w_in = R.take(KC, INW)
        w_uq = R.take(QL // P, NH * DQ)
        x_in = [R.take(DM), R.take(DM)]
        hT = R.take(KC, P)
        x_scr = R.take(DM)
        sq = R.take(2, QL)
        tap_rows = sq.rearrange("p a n -> p (a n)")[0:CK, 0:CC]
        cqn = R.take(QL)
        hist = x_in[1].rearrange("p (a n) -> p a n", a=2)
        ckvn = R.take(KL)
        kr = R.take(DR)
        kn = R.take(DR)
        rk = R.take(4, DR // 2)
        glu_t = R.take(CC)
        sig = glu_t
        gain_rows = glu_t[0:NCOL, 0:P]
        g_kn = R.take(DN)
        cT = R.take(5, P)
        qh = R.take(NH, DQ)
        z_scr = x_scr
        kh = R.take(NH, DQ)
        k_scr = kh.rearrange("p a n -> p (a n)")
        rt = k_scr[:, 0:4 * NH * DR // 2].rearrange("p (a b c) -> p a b c", a=4, c=DR // 2)
        R = Region(shared_end)
        mix_tok = R.take(NT, 2 * CC)
        attn_tok, conv_tok = mix_tok[:, :, 0:CC], mix_tok[:, :, CC:2 * CC]
        b_keep_end = R.at
        qTh = [R.take(SEQ, rows=DQ), R.take(SEQ, rows=DQ)]
        prob = [R.take(SEQ), R.take(SEQ)]
        pT = R.take(SEQ)
        b_end = R.at
        R = Region(0)
        pages1, kpe1 = R.take(NPAGE + 1, KL + 1), R.take(NPAGE, DR)
        s_tok = [R.take(NPAGE + 1, NS), R.take(NPAGE + 1, NS)]
        s_low_end = (NT + 2) * DM
        assert R.at <= s_low_end
        R = Region(b_keep_end)
        p_tok = R.take(NPAGE + 1, NS)
        cT_ring = [R.take(LC, P), R.take(LC, P)]
        kpeT_ring = [R.take(P, rows=DR), R.take(P, rows=DR)]
        ksq = [R.take(NH * DN), R.take(NH * DN)]
        ms_k = R.take(NPAGE, NH)
        rstd_k = R.take(NPAGE, NH)
        s_part = R.take(4, NH, TQ)
        m_part = R.take(NS)
        m_row = R.take(P)
        o_lat = R.take(KL)
        oT_lat = R.take(LC, NH, NSEQ, TQ)
        y_c = R.take(SEQ)
        y_s = R.take(NSEQ, TQ)
        assert b_end <= R.at
        w_ukT = R.take(NH, KL, rows=DN)
        q_abs = R.take(LC, NH, NS)
        q_pe = R.take(NH, NS, rows=DR)
        s_self = R.take(NH, NSEQ, TQ)
        s_self_end = R.at
        pages = [R.take(NPAGE + 1, KL + 1), pages1]
        kpe = [R.take(NPAGE, DR), kpe1]
        R = Region(0)
        x2 = R.take(NT, DM)
        xr = [R.take(DM), R.take(DM)]
        assert R.at <= s_low_end
        R = Region(s_low_end)
        w_out = R.take(KC, DM)
        w_out_end = R.at
        aT_place = R.at
        R = Region(w_out_end + NTOK)
        w_raw = [R.take_window("w_raw0", 2, KC, P), R.take_window("w_raw1", 2, KC, P)]
        assert w_out_end <= glu_start and R.at <= shared_end
        R = Region(shared_end)
        h_hi, h_hi_r = R.take_split("h_hi", TILES, KC, P)
        h_s = R.take(KC, NS)
        assert R.at <= b_keep_end
        R = Region(b_keep_end)
        h_full = R.take_window("h_full", TILES, KC, P)
        _, h_lo_r = Region(b_keep_end).take_split("h_lo", TILES, KC, P)
        h_end = R.at
        xn2 = R.take(DM)
        x_scr2 = R.take(DM)
        assert R.at >= s_self_end
        mixn = R.take(DM)
        mT = R.take(KC, P)
        conv_n = R.take(CC)
        ln_g = R.take(CC)
        ln_b = R.take(CC)
        c_scr = R.take(DM)
        R = Region(h_end)
        wd_hi, wd_hi_r = R.take_split("wd_hi", 2, DM)
        _, wd_lo_r = R.take_split("wd_lo", 2, DM)
        parts = [R.take_split(f"act{i}", NTOK) for i in range(3)]
        R = Region(aT_place)
        parts.append(R.take_split("act3", NTOK))
        a_hi, a_hi_r = zip(parts[0], parts[1])
        _, a_lo_r = zip(parts[2], parts[3])
        R = Region(s_low_end)
        w_hi, w_hi_r = zip(*(R.take_split(f"w_hi{i}", 2, KC, P) for i in range(2)))
        _, w_lo_r = zip(*(R.take_split(f"w_lo{i}", 2, KC, P) for i in range(2)))
        assert R.at <= w_out_end
        R = Region(NT * DM)
        gate_s = R.take_window("gate_s", NTOK)
        wd_raw = [w[:, :, :].rearrange("p a n -> p (a n)") for w in (w_uk, w_uv)]
        R = Region(shared_end)
        w_pg = R.take_window("w_pg", KC, DM)
        assert R.at <= b_keep_end
        _, w_pg_lo_r = Region(shared_end).take_split("w_pg_lo", KC, DM)
        w_pg_hi, w_pg_hi_r = Region(s_low_end).take_split("w_pg_hi", KC, DM)
        R = Region(b_keep_end)
        w_pp = R.take(PLE // P, DM)
        p_in = [R.take(PLE), R.take(PLE)]
        assert R.at <= h_end
        p_T = R.take(PLE // P, P)
        h4_at = R.at
        h4_full = R.take_window("h4_full", KC, P)
        _, h4_lo_r = Region(h4_at).take_split("h4_lo", KC, P)
        h4_hi, h4_hi_r = R.take_split("h4_hi", KC, P)
        sg = R.take(DM)
        y_out = [R.take(DM), R.take(DM)]
        xn4 = R.take(DM)
        junk4 = R.take(DM)

        ps = ctx.enter_context(nc.psum_tensor("ps", [P, 8, 512], F32))

        S = {}

        def s_(name):
            if name not in S:
                S[name] = sem(name)
            return S[name]

        win_v = A["w_in"][0].rearrange("(k p) n -> p k n", p=P)
        xp_v = A["x_prompt"][0].rearrange("(t p) n -> t p n", p=P)
        xs_v = A["x_sample"].rearrange("b q n -> (b q) n")
        st = lambda a, n=1: stats[:, a:a + n]
        HD2 = DR // 2

        def tiles(chain, per, tile):
            tile(0, 0, P, 1, P)
            with chain.loop(TILES // 2 - 1, per) as p:
                tile(2 * p + 1, 1, P, p + 1, P)
                tile(2 * p + 2, 0, P, p + 2, P)
            tile(TILES - 1, 1, P, TILES // 2, NS)
            tile(TILES, 0, NS, TILES // 2 + 1, 0)

        def long_blocks(m):
            return sum(i >= 4 for _, i in ORDER[:m + 1])

        def first(t):
            return isinstance(t, int) and t == 0

        def slot_count(t, s, v):
            return v if s == 0 else v + 1

        def nt_act(act, stage, n, src, rows, col, scratch):
            nc.scalar.activation(scratch[0:rows, :], src, ACT.Square,
                                 accum_out=st(col)[0:rows]).then_inc(s_(stage + "_sumsq"), 1)

        def nt_dve_mean(dve, stage, n, rows, col):
            dve.wait_ge(s_(stage + "_sumsq"), n)
            nc.vector.tensor_scalar(st(col + 1)[0:rows], st(col)[0:rows], 1.0 / DM, EPS, ALU.mult,
                                    ALU.add).then_inc(s_(stage + "_ms"), 1)

        def nt_dve_scale(dve, stage, n, src, rows, col, out):
            dve.wait_ge(s_(stage + "_rstd"), n)
            nc.vector.tensor_scalar(out[0:rows, :], src, st(col + 2)[0:rows], None,
                                    ALU.mult).then_inc(s_(stage + "_xn"), 1)

        def nt_pool(pool, stage, n, rows, col):
            pool.wait_ge(s_(stage + "_ms"), n)
            nc.gpsimd.tensor_tensor(st(col + 2)[0:rows], st(col + 1)[0:rows], mhalf[0:rows, 0:1],
                                    ALU.pow).then_inc(s_(stage + "_rstd"), 1)

        def nt_pe(pe, stage, n, rows, src, bank):
            pe.wait_ge(s_(stage + "_xn"), n)
            for k in range(KC):
                last = nc.tensor.transpose(ps[:, bank + k // 4, (k % 4) * P:(k % 4) * P + rows],
                                           src[0:rows, k * P:(k + 1) * P], ident[0:rows, 0:rows])
            last.then_inc(s_(stage + "_xT"), 1)

        def nt_dve_gain(dve, stage, n, rows, bank, gain, out):
            dve.wait_ge(s_(stage + "_xT"), n)
            g0 = COLS[gain][0] if isinstance(gain, str) else gain
            for b in range(2):
                src = ps[:, bank + b, :].rearrange("p (k c) -> p k c", c=P)[:, :, 0:rows]
                g = gcol[:, g0 + 4 * b:g0 + 4 * b + 4].unsqueeze(2).to_broadcast([P, 4, rows])
                last = nc.vector.tensor_tensor(out[:, 4 * b:4 * b + 4, :], src, g, ALU.mult)
            last.then_inc(s_(stage + "_hT"), 1)

        OUT = (2, 6)
        T0, T1, Z0, Z1, Z2, Z3, P0, P1 = 0, 1, 2, 3, 4, 5, 6, 7
        block = ctx.enter_context(nc.Block())

        @block.sync
        def _(sp):
            lat_w, glu_w = QL + KL + DR, 2 * CC
            sp.dma_start(x_in[0], xp_v[0]).then_inc(s_("x_loaded0"), 16)
            for name in COLS:
                c0, k = COLS[name]
                sp.dma_start(gain_rows[c0:c0 + k, :], A[name][0].rearrange("(k p) -> k p", p=P)).then_inc(s_("consts"), 16)
            sp.dma_start(tap_rows, A["conv_w"][0]).then_inc(s_("consts"), 16)
            sp.dma_start(w_in[:, :, 0:lat_w], win_v[:, :, 0:lat_w]).then_inc(s_("w_lat_loaded"), 16)
            sp.dma_start(x_in[1], xp_v[1]).then_inc(s_("x_loaded1"), 16)
            sp.dma_start(w_in[:, :, lat_w:], win_v[:, :, lat_w:]).then_inc(s_("w_glu_loaded"), 16)
            sp.dma_start(w_uq, A["w_uq"][0].rearrange("(k p) n -> p k n", p=P)).then_inc(s_("w_u_loaded"), 16)
            sp.dma_start(w_uk[:, :, :], A["w_uk"][0].rearrange("(k p) n -> p k n", p=P)).then_inc(s_("w_u_loaded"), 16)
            sp.dma_start(w_uv[:, :, :], A["w_uv"][0].rearrange("(k p) n -> p k n", p=P)).then_inc(s_("w_u_loaded"), 16)

            def load_x(t, s):
                sp.wait_ge(s_("a_xT"), t + 1)
                sp.dma_start(x_in[s], xp_v[bass.ds(t + 2, 1)].rearrange("a p n -> (a p) n")).then_inc(s_(f"x_loaded{s}"), 16)

            def store_a(t, rows):
                out_ckv = O[2][0, 0, bass.ds(t * P, P), :] if rows == P else O[5][0].rearrange("b q n -> (b q) n")
                out_kpe = O[3][0, 0, bass.ds(t * P, P), :] if rows == P else O[6][0].rearrange("b q n -> (b q) n")
                sp.wait_ge(s_("lat_ready"), t + 1)
                sp.dma_start(out_ckv, ckvn[0:rows, :]).then_inc(s_("lat_stored"), 16)
                sp.wait_ge(s_("kpe_ready"), t + 1)
                sp.dma_start(out_kpe, kr[0:rows, :]).then_inc(s_("lat_stored"), 16)
            with sp.Fori(0, TILES // 2 - 1) as p:
                for s in range(2):
                    load_x(2 * p + s, s)
                    store_a(2 * p + s, P)
            sp.wait_ge(s_("a_xT"), TILES - 1)
            sp.dma_start(x_in[0][0:NS, :], xs_v).then_inc(s_("x_loaded0"), 16)
            store_a(TILES - 2, P)
            sp.wait_ge(s_("a_xT"), TILES)
            for a in range(2):
                sp.dma_start(hist[0:120, a, :], A["state_conv"][0, 4 * a:4 * a + 4].rearrange("b n c -> (b n) c")).then_inc(s_("hist_loaded"), 16)
            store_a(TILES - 1, P)
            sp.wait_ge(s_("glu_ready"), TILES)
            sp.dma_start(O[4][0, 0], glu_t[P - HIST:P, :]).then_inc(s_("out_stored"), 16)
            store_a(TILES, NS)
            sp.wait_ge(s_("glu_ready"), NT)
            for b in range(NSEQ):
                sp.dma_start(O[7][0, b, HIST - TQ:HIST, :], glu_t[b * TQ:(b + 1) * TQ, :]).then_inc(s_("out_stored"), 16)
            sp.dma_start(O[7][0, :, 0:HIST - TQ, :], A["state_conv"][0, :, TQ:HIST, :]).then_inc(s_("out_stored"), 16)

            sp.wait_ge(s_("table_loaded"), 16)

            def load_pages(b, s):
                for g in range(NPAGE):
                    idx = sp.value_load(table[0:1, bass.ds(b * NPAGE + g, 1)], min_val=0, max_val=A["cache_ckv"].shape[1] - 1)
                    sp.dma_start(pages[s][:, g, 0:KL], A["cache_ckv"][0, bass.ds(idx, 1)].rearrange("a p n -> (a p) n")).then_inc(s_(f"pages_loaded{s}{g // 8}"), 16)
                    sp.dma_start(kpe[s][:, g, :], A["cache_kpe"][0, bass.ds(idx, 1)].rearrange("a p n -> (a p) n")).then_inc(s_(f"pages_loaded{s}{g // 8}"), 16)
            sp.wait_ge(s_("page_set"), 1)
            load_pages(0, 0)
            sp.wait_ge(s_("o_evac"), TILES * NH)
            sp.wait_ge(s_("page_set"), 2)
            load_pages(1, 1)
            sp.dma_start(w_out, A["w_out"][0].rearrange("(k p) n -> p k n", p=P)).then_inc(s_("w_out_loaded"), 16)
            with sp.Fori(0, NSEQ // 2 - 1) as p:
                for s in range(2):
                    sp.wait_ge(s_("pv_s_done"), 2 * p + s + 1)
                    load_pages(2 * p + s + 2, s)

            sp.wait_ge(s_("pv_s_done"), NSEQ - 1)
            for dst, name in ((ln_g, "conv_ln_g"), (ln_b, "conv_ln_b")):
                sp.dma_start(dst, A[name][0].partition_broadcast(P)).then_inc(s_("ln_loaded"), 16)
            for s in range(2):
                sp.dma_start(xr[s], xp_v[s]).then_inc(s_(f"xr_loaded{s}"), 16)
            wg_v = A["w_gate"][0].rearrange("(k p) n -> p k n", p=P)
            wu_v = A["w_up"][0].rearrange("(k p) n -> p k n", p=P)
            wd_v = A["w_down"][0].rearrange("(f p) n -> p f n", p=P)

            def load_gu(f, s):
                sp.dma_start(w_raw[s][:, 0], wg_v[:, :, bass.ds(f * P, P)]).then_inc(s_(f"gu_loaded{s}"), 16)
                sp.dma_start(w_raw[s][:, 1], wu_v[:, :, bass.ds(f * P, P)]).then_inc(s_(f"gu_loaded{s}"), 16)

            def load_wd(g):
                for s in range(2):
                    sp.dma_start(wd_raw[s], wd_v[:, bass.ds(2 * g + s, 1), :].rearrange("p a n -> p (a n)")).then_inc(s_("wd_loaded"), 16)
            sp.wait_ge(s_("y_ready_c"), CCH)
            for s in range(2):
                load_gu(s, s)
            sp.wait_ge(s_("ov_done"), 1)
            load_wd(0)
            with sp.Fori(0, TILES // 2 - 1) as p:
                for s in range(2):
                    sp.wait_ge(s_("x2_ready"), 2 * p + s + 1)
                    sp.dma_start(xr[s], xp_v[bass.ds(2 * p + s + 2, 1)].rearrange("a p n -> (a p) n")).then_inc(s_(f"xr_loaded{s}"), 16)
            sp.wait_ge(s_("x2_ready"), TILES - 1)
            sp.dma_start(xr[0][0:NS, :], xs_v).then_inc(s_("xr_loaded0"), 16)

            with sp.Fori(0, GROUPS - 1) as g:
                for s in range(2):
                    sp.wait_ge(s_("up_done"), 6 * g + 3 * s + 2)
                    load_gu(2 * g + s + 2, s)
                    if s == 0:
                        sp.wait_ge(s_("wd_split"), g + 1)
                        load_wd(g + 1)

            pp_v = A["p_prompt"][0, 0].rearrange("(t p) n -> t p n", p=P)
            ps_v = A["p_sample"][0].rearrange("b q n -> (b q) n")
            yp_v = O[0][0].rearrange("(t p) n -> t p n", p=P)
            sp.wait_ge(s_("up_done"), 6 * GROUPS)
            for h in range(2):
                sp.dma_start(w_pg[:, :, h * HALF:(h + 1) * HALF], A["w_ple_gate"][0, :, h * HALF:(h + 1) * HALF].rearrange("(k p) n -> p k n", p=P))\
                    .then_inc(s_(f"w_pg_loaded{h}"), 16)
            sp.dma_start(w_pp, A["w_ple_proj"][0].rearrange("(k p) n -> p k n", p=P)).then_inc(s_("w_pp_loaded"), 16)
            for s in range(2):
                sp.dma_start(p_in[s], pp_v[s]).then_inc(s_(f"p_loaded{s}"), 16)

            def load_p(t, s):
                sp.wait_ge(s_("ppT_done"), t + 1)
                sp.dma_start(p_in[s], pp_v[bass.ds(t + 2, 1)].rearrange("a p n -> (a p) n")).then_inc(s_(f"p_loaded{s}"), 16)

            def store_y(t, s):
                sp.wait_ge(s_("y_ready"), t + 1)
                sp.dma_start(yp_v[bass.ds(t, 1)].rearrange("a p n -> (a p) n"), y_out[s]).then_inc(s_(f"y_stored{s}"), 16)
            with sp.Fori(0, TILES // 2 - 1) as p:
                for s in range(2):
                    load_p(2 * p + s, s)
                    store_y(2 * p + s, s)
            sp.wait_ge(s_("ppT_done"), TILES - 1)
            sp.dma_start(p_in[0][0:NS, :], ps_v).then_inc(s_("p_loaded0"), 16)
            store_y(TILES - 2, 0)
            store_y(TILES - 1, 1)
            sp.wait_ge(s_("y_ready"), NT)
            sp.dma_start(O[1].rearrange("b q n -> (b q) n"), y_out[0][0:NS, :]).then_inc(s_("y_stored0"), 16)
            sp.wait_ge(s_("y_stored0"), 16 * (TILES // 2 + 1))
            sp.wait_ge(s_("y_stored1"), 16 * (TILES // 2))
            sp.wait_ge(s_("lat_stored"), 32 * NT)
            sp.wait_ge(s_("out_stored"), 16 * (NSEQ + 2))

        @block.gpsimd
        def _(pool):
            ch = Chain(pool, s_("pool_own"))
            ch.link(nc.gpsimd.memset(ident[:, :], 0.0))
            nc.gpsimd.affine_select(out=ident[:, :], in_=ident[:, :], compare_op=ALU.not_equal, fill=1.0,
                                    base=0, pattern=[[-1, P]], channel_multiplier=1).then_inc(s_("ident_ready"), 1)
            nc.gpsimd.memset(mhalf[:, :], -0.5)
            for i, n in enumerate((QL, KL, DR)):
                nc.gpsimd.memset(inv_n[:, i:i + 1], 1.0 / n)
            nc.gpsimd.memset(inv_n[:, 3:3 + NH], 1.0 / DN)
            nc.gpsimd.memset(inv_n[:, 3 + NH:3 + 2 * NH], 1.0 / DR)
            ch.link(nc.gpsimd.memset(inv_n[:, 3 + 2 * NH:3 + 3 * NH], 1.0 / DN))
            nc.gpsimd.memset(glu[:, :, 0:HIST], 0.0)
            ch.link(nc.gpsimd.memset(causal[:, :], 0.0))
            nc.gpsimd.affine_select(out=causal[:, :], in_=causal[:, :], compare_op=ALU.is_ge, fill=NEG,
                                    base=0, pattern=[[-1, P]], channel_multiplier=1)
            ch.link(nc.gpsimd.memset(self_mask[:, :], 0.0))
            sm = self_mask[:, :].rearrange("p (b q) -> p b q", q=TQ)
            ch.link(nc.gpsimd.affine_select(out=sm, in_=sm, compare_op=ALU.is_ge, fill=NEG, base=0,
                                            pattern=[[TQ, NSEQ], [1, TQ]], channel_multiplier=-1))
            nc.gpsimd.affine_select(out=sm, in_=sm, compare_op=ALU.is_ge, fill=NEG, base=0,
                                    pattern=[[-TQ, NSEQ], [0, TQ]], channel_multiplier=1).then_inc(s_("pool_consts"), 1)


            def rstd_q(t, rows):
                pool.wait_ge(s_("msq_ready"), t + 1)
                nc.gpsimd.tensor_tensor(st(80, 24)[0:rows], st(50, 24)[0:rows], mhalf[0:rows, 0:24], ALU.pow).then_inc(s_("rstd_q"), 1)

            def tile_a(t, s, rows, v, ahead):
                if not first(t):
                    rstd_q(t - 1, P)
                pool.wait_ge(s_("msz_ready"), t + 1)
                nc.gpsimd.tensor_tensor(st(16, 3)[0:rows], st(12, 3)[0:rows], mhalf[0:rows, 0:3], ALU.pow).then_inc(s_("rstd_z"), 1)
                if ahead:
                    nt_pool(pool, "a", t + 2, ahead, 0)
            nt_pool(pool, "a", 1, P, 0)
            tiles(ch, 0, tile_a)
            rstd_q(TILES, NS)

            pool.wait_ge(s_("ckv_kept"), 1)
            pool.wait_ge(s_("hist_ready"), 1)
            pool.wait_ge(s_("lat_stored"), 32 * NT)
            pool.wait_ge(s_("out_stored"), 16 * (NSEQ + 2))

            def set_page(s):
                ch.link(nc.gpsimd.memset(pages[s][:, :, KL:KL + 1], 1.0))
                ch.link(nc.gpsimd.memset(pages[s][:, NPAGE, 0:KL], 0.0))
                nc.gpsimd.tensor_copy(pages[s][0:NS, NPAGE, 0:KL], ckv_keep[:, :]).then_inc(s_("page_set"), 1)
                pool.wait_ge(s_("page_set"), s + 1)
            nc.gpsimd.memset(s_self[64:P, :, :, :], NEG).then_inc(s_("self_place"), 1)
            pool.wait_ge(s_("self_place"), 1)
            set_page(0)
            pool.wait_ge(s_("o_evac"), TILES * NH)
            set_page(1)
            with ch.loop(NSEQ, 0) as b:
                for q in range(4):
                    pool.wait_ge(s_("msk_ready"), 4 * b + q + 1)
                    nc.gpsimd.tensor_tensor(rstd_k[:, 4 * q:4 * q + 4, :], ms_k[:, 4 * q:4 * q + 4, :],
                                            mhalf[:, 0:4 * NH].rearrange("p (g h) -> p g h", h=NH), ALU.pow).then_inc(s_("rstdk_ready"), 1)

            def ln_pool(n, rows):
                pool.wait_ge(s_("var_ready"), n)
                nc.gpsimd.tensor_tensor(st(6)[0:rows], st(7)[0:rows], mhalf[0:rows, 0:1], ALU.pow).then_inc(s_("rstd_ln"), 1)

            def mix_pool(n, rows):
                pool.wait_ge(s_("msm_ready"), n)
                nc.gpsimd.tensor_tensor(st(22, 2)[0:rows], st(20, 2)[0:rows], mhalf[0:rows, 0:2], ALU.pow).then_inc(s_("rstd_m"), 1)

            def tile_c(t, s, rows, v, ahead):
                if ahead:
                    ln_pool(t + 2, ahead)
                if not first(t):
                    nt_pool(pool, "c", t, P, 0)
                if ahead:
                    mix_pool(t + 2, ahead)
            ln_pool(1, P)
            mix_pool(1, P)
            tiles(ch, 0, tile_c)
            nt_pool(pool, "c", NT, NS, 0)

            def tile_d(t, s, rows, v, ahead):
                if ahead:
                    nt_pool(pool, "d", t + 2, ahead, 0)
            def w_pg_low(h):
                pool.wait_ge(s_("w_pg_hi"), h + 1)
                e = slice(h * HALF, (h + 1) * HALF)
                nc.gpsimd.tensor_tensor(w_pg_lo_r[:, :, e], w_pg[:, :, e], w_pg_hi[:, :, e], ALU.subtract).then_inc(s_("w_pg_split"), 1)
            w_pg_low(0)
            nt_pool(pool, "d", 1, P, 0)
            w_pg_low(1)
            tiles(ch, 0, tile_d)

        @block.scalar
        def _(act):
            ch = Chain(act, s_("act_own"))
            act.wait_ge(s_("x_loaded0"), 16)
            nt_act(act, "a", 1, x_in[0], P, 0, x_scr)
            for dst, name in ((g_q, "q_lora_norm"), (g_kv, "kv_norm"), (g_kpe, "k_pe_norm"), (g_qn, "q_nope_norm"),
                              (g_kn, "k_nope_norm"), (g_qpe, "q_pe_norm")):
                act.dma_start(dst[0:P], A[name][0].partition_broadcast(P)).then_inc(s_("gains"), 16)
            act.dma_start(rope[:, 0:TILES, :], A["rope"][0:SEQ, :].rearrange("(t p) n -> p t n", p=P)).then_inc(s_("gains"), 16)
            act.dma_start(rope[0:NS, TILES, :], A["rope"][SEQ:NTOK, :]).then_inc(s_("gains"), 16)
            act.dma_start(table[:, :], A["page_table"].rearrange("b g -> (b g)").unsqueeze(0)).then_inc(s_("table_loaded"), 16)

            def qkv_act(t, rows):
                act.wait_ge(s_("q_done"), t + 1)
                nc.scalar.activation(sq[0:rows, :, :], ps[0:rows, P0:P0 + 2, 0:QL], ACT.Square).then_inc(s_("q_sq"), 1)
                act.wait_ge(s_("kv_done"), t + 1)
                nc.scalar.activation(k_scr[0:rows, 0:NH * DN], ps[0:rows, Z2, :], ACT.Square).then_inc(s_("k_sq"), 1)
                if rows == P:
                    nc.scalar.activation(V[:, bass.ds(t, 1), :], ps[:, Z3, :].unsqueeze(1), ACT.Copy).then_inc(s_("v_ready"), 1)

            def qT_copy(t, rows):
                act.wait_ge(s_("qT_done"), t + 1)
                src = ps[0:DQ, T0:T0 + 2, :].rearrange("p a (k c) -> p (a k) c", c=P)[:, :, 0:rows]
                dst = qT[:, :, bass.ds(t * P, P)] if rows == P else qT_s[:, :, :]
                nc.scalar.activation(dst, src, ACT.Copy).then_inc(s_("qT_ready"), 1)

            def tile_a(t, s, rows, v, ahead):
                if not first(t):
                    qkv_act(t - 1, P)
                act.wait_ge(s_("z_lat_done"), t + 1)
                act.wait_ge(s_("a_sumsq"), t + 1)
                nc.scalar.activation(z_scr[0:rows, 0:QL], ps[0:rows, Z0, 0:QL], ACT.Square, accum_out=st(8)[0:rows])
                nc.scalar.activation(z_scr[0:rows, QL:QL + KL], ps[0:rows, Z1, 0:KL], ACT.Square, accum_out=st(9)[0:rows])
                nc.scalar.activation(z_scr[0:rows, QL + KL:QL + KL + DR], ps[0:rows, Z1, KL:KL + DR], ACT.Square,
                                     accum_out=st(10)[0:rows]).then_inc(s_("z_sumsq"), 1)
                if not first(t):
                    qT_copy(t - 1, P)
                if ahead:
                    act.wait_ge(s_("z_sumsq"), t + 1)
                    act.wait_ge(s_(f"x_loaded{1 - s}"), 16 * slot_count(t, s, v))
                    nt_act(act, "a", t + 2, x_in[1 - s][0:ahead, :], ahead, 0, x_scr)
                if rows == NS:
                    act.wait_ge(s_("out_stored"), 16)
                act.wait_ge(s_("z_glu_done"), t + 1)
                nc.scalar.activation(sig[0:rows, :], ps[0:rows, Z3, :], ACT.Sigmoid).then_inc(s_("sig_ready"), 1)
                act.wait_ge(s_("cT_done"), t + 1)
                nc.scalar.activation(cT[:, 0:4, 0:rows], ps[:, T0, :].rearrange("p (k c) -> p k c", c=P)[:, :, 0:rows], ACT.Copy)
                nc.scalar.activation(cT[:, 4, 0:rows], ps[:, T1, 0:rows], ACT.Copy).then_inc(s_("cT_ready"), 1)
                act.wait_ge(s_("gluT_done"), t + 1)
                src = ps[:, Z0, :].rearrange("p (k c) -> p k c", c=P)[:, :, 0:rows]
                if rows == P:
                    nc.scalar.activation(glu[:, :, bass.ds(HIST + t * P, P)], src, ACT.Copy).then_inc(s_("gluT_ready"), 1)
                else:
                    for c in range(CCH):
                        last = nc.scalar.activation(glu_s[:, c, :, HIST:HIST + TQ], src[:, c, :].rearrange("p (b q) -> p b q", q=TQ), ACT.Copy)
                    last.then_inc(s_("gluT_ready"), 1)
            act.wait_ge(s_("pool_consts"), 1)
            act.wait_ge(s_("colT_done"), 1)
            tiles(ch, 0, tile_a)
            qkv_act(TILES, NS)
            act.wait_ge(s_("hist_done"), 1)
            for a in range(2):
                last = nc.scalar.activation(glu_s[:, :, 4 * a:4 * a + 4, 0:HIST],
                                            ps[:, Z0 + a, 0:CCH * 120].rearrange("p (c b n) -> p c b n", b=4, n=HIST), ACT.Copy)
            last.then_inc(s_("hist_ready"), 1)
            qT_copy(TILES, NS)

            act.wait_ge(s_("self_place"), 1)
            act.wait_ge(s_("wukT_done"), 1)
            nc.scalar.activation(w_ukT, ps[0:DN, 0:4, :].rearrange("p a (h c) -> p (a h) c", c=KL), ACT.Copy)
            nc.scalar.activation(q_pe, qT_s[DN:DQ, :, :], ACT.Copy).then_inc(s_("wukT_ready"), 1)
            act.wait_ge(s_("qabs_done"), 1)
            nc.scalar.activation(q_abs, ps[:, 4:4 + LC, :].rearrange("p a (h n) -> p a h n", h=NH), ACT.Copy).then_inc(s_("qabs_ready"), 1)

            act.wait_ge(s_("kT_ready"), NT)
            def head_qT(c, hp):
                nc.scalar.activation(qTh[hp], qT[:, bass.ds(2 * c + hp, 1), :].rearrange("p a n -> p (a n)"), ACT.Copy)\
                    .then_inc(s_("qTh_ready"), 1)

            def expo(c, m):
                n, j = (ORDER[m % PAIR][1] + 1) * P, m % PAIR
                act.wait_ge(s_("nmax_ready"), PAIR * c + m + 1)
                nc.scalar.activation(prob[m % 2][:, 0:n], ps[:, 2 * (m % 2):2 * (m % 2) + 2, :].rearrange("p a n -> p (a n)")[:, 0:n],
                                     ACT.Exp, bias=st(120 + j), accum_out=st(136 + j)).then_inc(s_("prob_ready"), 1)

            def pair_act(c, end):
                for m in range(PAIR):
                    i = ORDER[m][1]
                    if i >= 4:
                        act.wait_ge(s_("ptB_done"), TILES * c + long_blocks(m))
                        nc.scalar.activation(pT[:, 512:(i + 1) * P], ps[:, 5, 0:(i - 3) * P], ACT.Copy).then_inc(s_("ptB_ready"), 1)
                    if m < PAIR - 2 or not end:
                        expo(c, m + 2)
                    if m == TILES and not end:
                        act.wait_ge(s_("scores_done"), PAIR * c + TILES)
                        head_qT(c + 1, 0)
                    if m == PAIR - 1 and not end:
                        act.wait_ge(s_("scores_done"), PAIR * (c + 1))
                        head_qT(c + 1, 1)
            head_qT(0, 0)
            head_qT(0, 1)
            expo(0, 0)
            expo(0, 1)
            with ch.loop(NH // 2 - 1, 0) as c:
                pair_act(c, False)
            pair_act(NH // 2 - 1, True)

            def soft_exp(b, s):
                act.wait_ge(s_("s_shift"), b + 1)
                nc.scalar.activation(p_tok, s_tok[s], ACT.Exp).then_inc(s_("ptok_ready"), 1)

            def page_copy(n, r):
                act.wait_ge(s_("ctr_done"), n)
                nc.scalar.activation(cT_ring[r], ps[:, r, 0:LC * P].rearrange("p (k c) -> p k c", c=P), ACT.Copy)
                nc.scalar.activation(kpeT_ring[r], ps[0:DR, r, LC * P:LC * P + P], ACT.Copy).then_inc(s_("ctr_ready"), 1)

            def seq_act(b, s, prev, last):
                for g in range(NPAGE):
                    r = g % 2
                    if g < NPAGE - 1 or not last:
                        page_copy(NPAGE * b + g + 2, 1 - r)
                    act.wait_ge(s_("k_done"), NPAGE * b + g + 1)
                    if g >= 2 or prev:
                        act.wait_ge(s_("ksum_done"), NPAGE * b + g - 1)
                    nc.scalar.activation(ksq[r], ps[:, 2 + r, :], ACT.Square).then_inc(s_("ksq_ready"), 1)
                    if g == 7 and prev:
                        soft_exp(b - 1, 1 - s)

            def chunk_copy(c):
                act.wait_ge(s_("yT_done"), c + 1)
                nc.scalar.activation(conv_tok[:, 0:TILES, bass.ds(c * P, P)],
                                     ps[:, 2:4, :].rearrange("p a (k c) -> p (a k) c", c=P), ACT.Copy)
                nc.scalar.activation(conv_tok[0:NS, TILES, bass.ds(c * P, P)], ps[0:NS, 6, 384:384 + P], ACT.Copy).then_inc(s_("yT_ready"), 1)
            page_copy(1, 0)
            seq_act(0, 0, False, False)
            seq_act(1, 1, True, False)
            chunk_copy(0)
            with ch.loop(NSEQ // 2 - 2, 0) as p:
                seq_act(2 * p + 2, 0, True, False)
                seq_act(2 * p + 3, 1, True, False)
                chunk_copy(p + 1)
            seq_act(NSEQ - 2, 0, True, False)
            seq_act(NSEQ - 1, 1, True, True)
            chunk_copy(CCH - 1)
            def centred_square(t, rows):
                act.wait_ge(s_("centred"), t + 1)
                if not first(t):
                    act.wait_ge(s_("mix_sumsq"), t)
                nc.scalar.activation(c_scr[0:rows, CC:2 * CC], conv_n[0:rows, :], ACT.Square, accum_out=st(24)[0:rows]).then_inc(s_("var_sumsq"), 1)
                nc.scalar.activation(c_scr[0:rows, 0:CC], attn_tok[0:rows, bass.ds(t, 1), :].rearrange("p a n -> p (a n)"),
                                     ACT.Square, accum_out=st(16)[0:rows])

            def x2_square(t, rows):
                act.wait_ge(s_("x2_ready"), t + 1)
                if not first(t):
                    act.wait_ge(s_("c_sumsq"), t)
                nt_act(act, "c", t + 1, x2[0:rows, bass.ds(t, 1), :].rearrange("p a n -> p (a n)"), rows, 0, x_scr2)

            def conv_silu(t, rows):
                act.wait_ge(s_("ln_ready"), t + 1)
                ch.link(nc.scalar.activation(conv_n[0:rows, :], conv_n[0:rows, :], ACT.Silu))
                nc.scalar.activation(c_scr[0:rows, CC:2 * CC], conv_n[0:rows, :], ACT.Square,
                                     accum_out=st(17)[0:rows]).then_inc(s_("mix_sumsq"), 1)

            def tile_c(t, s, rows, v, ahead):
                if ahead:
                    centred_square(t + 1, ahead)
                if not first(t):
                    x2_square(t - 1, P)
                if ahead:
                    conv_silu(t + 1, ahead)
            act.wait_ge(s_("yT_ready"), CCH)
            centred_square(0, P)
            conv_silu(0, P)
            soft_exp(NSEQ - 1, 1)
            act.wait_ge(s_("ov_done"), 1)
            nc.scalar.activation(attn_tok[0:NS, TILES, :], ps[0:NS, 4, :], ACT.Copy).then_inc(s_("s_done"), 1)
            act.wait_ge(s_("s_done"), 1)
            tiles(ch, 2, tile_c)
            x2_square(TILES, NS)

            def split_high(s, loads, used):
                act.wait_ge(s_(f"gu_loaded{s}"), 32 * loads)
                if used is not None:
                    act.wait_ge(s_("up_done"), used)
                nc.scalar.activation(w_hi_r[s], w_raw[s], ACT.Copy).then_inc(s_("w_hi_ready"), 1)

            def ffn_act(g, start, end):
                for s in range(2):
                    if not (end and s == 1):
                        split_high(1 - s, g + 1 + s, None if start and s == 0 else 6 * g + 3 * s)
                    if s == 0:
                        act.wait_ge(s_("wd_loaded"), 32 * (g + 1))
                        if not start:
                            act.wait_ge(s_("dn_done"), 2 * NT * g)
                        for a in range(2):
                            last = nc.scalar.activation(wd_hi_r[:, a, :], wd_raw[a], ACT.Copy)
                        last.then_inc(s_("wd_hi_ready"), 1)
                    for b, (at, n) in enumerate(BLOCKS):
                        act.wait_ge(s_("gate_done"), 6 * g + 3 * s + b + 1)
                        nc.scalar.activation(gate_s[:, at:at + n], ps[:, 2 * b, 0:n], ACT.Silu).then_inc(s_("silu_ready"), 1)
            act.wait_ge(s_("c_wout_done"), NT)
            split_high(0, 1, None)
            act.wait_ge(s_("c_hT"), NT)
            ffn_act(0, True, False)
            with act.Fori(1, GROUPS - 1) as g:
                ffn_act(g, False, False)
            ffn_act(GROUPS - 1, False, True)

            for h in range(2):
                act.wait_ge(s_(f"w_pg_loaded{h}"), 16)
                e = slice(h * HALF, (h + 1) * HALF)
                nc.scalar.activation(w_pg_hi_r[:, :, e], w_pg[:, :, e], ACT.Copy).then_inc(s_("w_pg_hi"), 1)
            act.wait_ge(s_("dn_evac"), 2 * NT * GROUPS)

            def pT_copy(n, rows):
                act.wait_ge(s_("ppT_done"), n)
                nc.scalar.activation(p_T[:, :, 0:rows], ps[:, 2, 0:2 * P].rearrange("p (k c) -> p k c", c=P)[:, :, 0:rows], ACT.Copy)\
                    .then_inc(s_("ppT_ready"), 1)

            def tile_d(t, s, rows, v, ahead):
                if ahead:
                    act.wait_ge(s_("d_ms"), t + 1)
                    nt_act(act, "d", t + 2, x2[0:ahead, bass.ds(t + 1, 1), :].rearrange("p a n -> p (a n)"), ahead, 0, junk4)
                act.wait_ge(s_("pg_done"), t + 1)
                if not first(t):
                    act.wait_ge(s_("y_ready"), t)
                nc.scalar.activation(sg[0:rows, :], ps[0:rows, 3:5, :].rearrange("p a n -> p (a n)"), ACT.Sigmoid).then_inc(s_("sg_ready"), 1)
                if ahead:
                    pT_copy(t + 2, ahead)
            nt_act(act, "d", 1, x2[:, 0, :], P, 0, junk4)
            pT_copy(1, P)
            tiles(ch, 0, tile_d)

        @block.vector
        def _(dve):
            ch = Chain(dve, s_("dve_own"))
            nt_dve_mean(dve, "a", 1, P, 0)
            nt_dve_scale(dve, "a", 1, x_in[0], P, 0, x_in[0])
            dve.wait_ge(s_("colT_done"), 1)
            nc.vector.tensor_copy(gcol[:, :], ps[:, P0, 0:NCOL])
            ch.link(nc.vector.tensor_copy(tapw[:, :, :], ps[:, P1, 0:CCH * CK].rearrange("p (c k) -> p c k", k=CK)))
            nt_dve_gain(dve, "a", 1, P, T0, "norm_mix", hT)
            dve.wait_ge(s_("gains"), 16 * 8)
            dve.wait_ge(s_("pool_consts"), 1)
            ch.link(nc.vector.tensor_tensor(g_qn[:, :], g_qn[:, :], g_kn[:, :], ALU.mult))
            ch.link(nc.vector.tensor_scalar(g_qn[:, :], g_qn[:, :], SCALE, None, ALU.mult))
            ch.link(nc.vector.tensor_scalar(g_qpe[:, :], g_qpe[:, :], SCALE, None, ALU.mult))

            def rotate(out1, out2, x1, x2_, cos, sin, a, b, c, d):
                nc.vector.tensor_tensor(a, x1, cos, ALU.mult)
                nc.vector.tensor_tensor(b, x2_, sin, ALU.mult)
                nc.vector.tensor_tensor(c, x2_, cos, ALU.mult)
                ch.link(nc.vector.tensor_tensor(d, x1, sin, ALU.mult))
                nc.vector.tensor_tensor(out1, a, b, ALU.subtract)
                return nc.vector.tensor_tensor(out2, c, d, ALU.add)

            def lat_dve(t, rows):
                r = slice(0, rows)
                if not first(t):
                    dve.wait_ge(s_("lat_stored"), 32 * t)
                dve.wait_ge(s_("z_sumsq"), t + 1)
                ch.link(nc.vector.tensor_tensor(st(12, 3)[r], st(8, 3)[r], inv_n[r, 0:3], ALU.mult))
                nc.vector.tensor_scalar(st(12, 3)[r], st(12, 3)[r], EPS, None, ALU.add).then_inc(s_("msz_ready"), 1)
                dve.wait_ge(s_("rstd_z"), t + 1)
                nc.vector.scalar_tensor_tensor(cqn[r, :], ps[r, Z0, 0:QL], st(16)[r], g_q[r, :], ALU.mult, ALU.mult)
                ch.link(nc.vector.scalar_tensor_tensor(kn[r, :], ps[r, Z1, KL:KL + DR], st(18)[r], g_kpe[r, :], ALU.mult, ALU.mult))
                nc.vector.scalar_tensor_tensor(ckvn[r, :], ps[r, Z1, 0:KL], st(17)[r], g_kv[r, :], ALU.mult, ALU.mult).then_inc(s_("lat_ready"), 1)
                cos = rope[r, bass.ds(t, 1), 0:HD2].rearrange("p a n -> p (a n)")
                sin = rope[r, bass.ds(t, 1), HD2:DR].rearrange("p a n -> p (a n)")
                rotate(kr[r, 0:HD2], kr[r, HD2:DR], kn[r, 0:HD2], kn[r, HD2:DR], cos, sin,
                       *(rk[r, j, :] for j in range(4))).then_inc(s_("kpe_ready"), 1)

            def glu_dve(t, rows):
                dve.wait_ge(s_("sig_ready"), t + 1)
                nc.vector.tensor_tensor(glu_t[0:rows, :], ps[0:rows, Z2, :], sig[0:rows, :], ALU.mult).then_inc(s_("glu_ready"), 1)

            def qk_dve(t, rows):
                r = slice(0, rows)
                dve.wait_ge(s_("q_sq"), t + 1)
                sqh = sq[r, :, :].rearrange("p a (h d) -> p (a h) d", d=DQ)
                nc.vector.reduce_sum(st(20, NH)[r], sqh[:, :, 0:DN], AXX)
                nc.vector.reduce_sum(st(28, NH)[r], sqh[:, :, DN:DQ], AXX)
                dve.wait_ge(s_("k_sq"), t + 1)
                ch.link(nc.vector.reduce_sum(st(36, NH)[r], k_scr[r, 0:NH * DN].rearrange("p (h d) -> p h d", d=DN), AXX))
                ch.link(nc.vector.tensor_tensor(st(50, 24)[r], st(20, 24)[r], inv_n[r, 3:27], ALU.mult))
                nc.vector.tensor_scalar(st(50, 24)[r], st(50, 24)[r], EPS, None, ALU.add).then_inc(s_("msq_ready"), 1)
                dve.wait_ge(s_("rstd_q"), t + 1)
                qv = ps[r, P0:P0 + 2, 0:QL].rearrange("p a (h d) -> p a h d", d=DQ)
                qh4 = qh[r, :, :].rearrange("p (a h) d -> p a h d", a=2)
                rq = st(80, NH)[r].rearrange("p (a h) -> p a h", a=2)
                rp = st(88, NH)[r].rearrange("p (a h) -> p a h", a=2)
                nc.vector.tensor_tensor(qh4[:, :, :, 0:DN], qv[:, :, :, 0:DN], rq.unsqueeze(3).to_broadcast([rows, 2, 4, DN]), ALU.mult)
                ch.link(nc.vector.tensor_tensor(qh4[:, :, :, DN:DQ], qv[:, :, :, DN:DQ], rp.unsqueeze(3).to_broadcast([rows, 2, 4, DR]), ALU.mult))
                nc.vector.tensor_tensor(qh[r, :, 0:DN], qh[r, :, 0:DN], g_qn[r, :].unsqueeze(1).to_broadcast([rows, NH, DN]), ALU.mult)
                ch.link(nc.vector.tensor_tensor(qh[r, :, DN:DQ], qh[r, :, DN:DQ], g_qpe[r, :].unsqueeze(1).to_broadcast([rows, NH, DR]), ALU.mult))
                cosb = rope[r, bass.ds(t, 1), 0:HD2].to_broadcast([rows, NH, HD2])
                sinb = rope[r, bass.ds(t, 1), HD2:DR].to_broadcast([rows, NH, HD2])
                rotate(qh[r, :, DN:DN + HD2], qh[r, :, DN + HD2:DQ], qh[r, :, DN:DN + HD2], qh[r, :, DN + HD2:DQ],
                       cosb, sinb, *(rt[r, j, :, :] for j in range(4))).then_inc(s_("qh_ready"), 1)
                dve.wait_ge(s_("qh_ready"), t + 1)
                nc.vector.tensor_tensor(kh[r, :, 0:DN], ps[r, Z2, :].rearrange("p (h d) -> p h d", d=DN),
                                        st(96, NH)[r].unsqueeze(2).to_broadcast([rows, NH, DN]), ALU.mult)
                dve.wait_ge(s_("kpe_ready"), t + 1)
                nc.vector.tensor_copy(kh[r, :, DN:DQ], kr[r, :].unsqueeze(1).to_broadcast([rows, NH, DR])).then_inc(s_("kh_ready"), 1)

            def kT_dve(t, rows):
                dve.wait_ge(s_("kT_done"), t + 1)
                src = ps[0:DQ, P0:P0 + 2, :].rearrange("p a (k c) -> p (a k) c", c=P)[:, :, 0:rows]
                dst = kT[:, :, bass.ds(t * P, P)] if rows == P else kT_s[:, :, :]
                nc.vector.tensor_copy(dst, src).then_inc(s_("kT_ready"), 1)

            def tile_a(t, s, rows, v, ahead):
                if not first(t):
                    qk_dve(t - 1, P)
                    kT_dve(t - 1, P)
                lat_dve(t, rows)
                if ahead:
                    nt_dve_mean(dve, "a", t + 2, ahead, 0)
                    nt_dve_scale(dve, "a", t + 2, x_in[1 - s][0:ahead, :], ahead, 0, x_in[1 - s])
                glu_dve(t, rows)
                if ahead:
                    nt_dve_gain(dve, "a", t + 2, ahead, T0, "norm_mix", hT[:, :, 0:ahead])
            tiles(ch, 16, tile_a)
            qk_dve(TILES, NS)
            kT_dve(TILES, NS)
            nc.vector.tensor_copy(ckv_keep[:, :], ckvn[0:NS, :]).then_inc(s_("ckv_kept"), 1)
            dve.wait_ge(s_("hist_ready"), 1)
            dve.wait_ge(s_("out_stored"), 16 * (NSEQ + 2))

            dve.wait_ge(s_("self_place"), 1)
            dve.wait_ge(s_("self_done"), 1)
            nc.vector.tensor_tensor(s_self[0:NS, :, :, :].rearrange("p h b q -> p h (b q)"),
                                    ps[0:NS, 7, :].rearrange("p (h n) -> p h n", h=NH),
                                    self_mask[:, :].unsqueeze(1).to_broadcast([NS, NH, NS]), ALU.add).then_inc(s_("self_ready"), 1)
            dve.wait_ge(s_("self_ready"), 1)

            def s_view(m):
                return ps[:, 2 * (m % 2):2 * (m % 2) + 2, :].rearrange("p a n -> p (a n)")

            def row_max(c, m):
                i = ORDER[m % PAIR][1]
                dve.wait_ge(s_("scores_done"), PAIR * c + m + 1)
                d = s_view(m)[:, i * P:(i + 1) * P]
                ch.link(nc.vector.tensor_tensor(d, d, causal[:, :], ALU.add))
                nc.vector.tensor_reduce(st(120 + m % PAIR), s_view(m)[:, 0:(i + 1) * P], AXX, ALU.max, negate=True).then_inc(s_("nmax_ready"), 1)

            def out_rows(c, m):
                hp, i = ORDER[m]
                dve.wait_ge(s_("pv_done"), PAIR * c + m + 1)
                ch.link(nc.vector.reciprocal(st(136 + m), st(136 + m)))
                nc.vector.tensor_scalar(attn_tok[:, i, bass.ds((2 * c + hp) * DV, DV)], ps[:, 6 + m % 2, 0:DV],
                                        st(136 + m), None, ALU.mult).then_inc(s_("o_evac"), 1)

            def pair_dve(c, end):
                for m in range(PAIR):
                    n = min(ORDER[m][1] + 1, 4) * P
                    dve.wait_ge(s_("ptA_done"), PAIR * c + m + 1)
                    nc.vector.tensor_copy(pT[:, 0:n], ps[:, 4, 0:n]).then_inc(s_("ptA_ready"), 1)
                    if m >= 1:
                        out_rows(c, m - 1)
                    if m < PAIR - 2 or not end:
                        row_max(c, m + 2)
                out_rows(c, PAIR - 1)
            row_max(0, 0)
            row_max(0, 1)
            with ch.loop(NH // 2 - 1, 2 * PAIR) as c:
                pair_dve(c, False)
            pair_dve(NH // 2 - 1, True)

            def w_(c, k):
                return tapw[:, bass.ds(c, 1), k:k + 1].rearrange("p a n -> p (a n)")

            def tap(c, k):
                src = glu[:, bass.ds(c, 1), k:k + SEQ].rearrange("p a n -> p (a n)")
                src_s = glu_s[:, bass.ds(c, 1), :, k:k + TQ].rearrange("p a b n -> p (a b) n")
                if k == 0:
                    bias = gcol[:, bass.ds(c + COLS["conv_b"][0], 1)]
                    nc.vector.tensor_scalar(y_c, src, w_(c, k), bias, ALU.mult, ALU.add)
                    ch.link(nc.vector.tensor_scalar(y_s, src_s, w_(c, k), bias, ALU.mult, ALU.add))
                else:
                    nc.vector.scalar_tensor_tensor(y_c, src, w_(c, k), y_c, ALU.mult, ALU.add)
                    ins = nc.vector.scalar_tensor_tensor(y_s, src_s, w_(c, k), y_s, ALU.mult, ALU.add)
                    if k == CK - 1:
                        ins.then_inc(s_("y_ready_c"), 1)
                    else:
                        ch.link(ins)
            def col_max(b, s):
                nc.vector.tensor_reduce(m_part, s_tok[s].rearrange("p g n -> p n g"), AXX, ALU.max).then_inc(s_("mpart_ready"), 1)

            def row_of_max(b, s):
                dve.wait_ge(s_("mT_done"), b + 1)
                ch.link(nc.vector.reduce_max(st(107)[0:NS], ps[0:NS, 6, 0:P], AXX))
                nc.vector.tensor_copy(m_row[0:NS, :], st(107)[0:NS].to_broadcast([NS, P])).then_inc(s_("mrow_ready"), 1)

            def shift(b, s):
                dve.wait_ge(s_("mB_done"), b + 1)
                nc.vector.tensor_tensor(s_tok[s], s_tok[s], ps[:, 6, P:P + NS].unsqueeze(1).to_broadcast([P, NPAGE + 1, NS]),
                                        ALU.subtract).then_inc(s_("s_shift"), 1)

            def out_lat(b, s):
                dve.wait_ge(s_("pv_s_done"), b + 1)
                ch.link(nc.vector.reciprocal(st(105)[0:NS], ps[0:NS, 7, KL:KL + 1]))
                nc.vector.tensor_scalar(o_lat[0:NS, :], ps[0:NS, 7, 0:KL], st(105)[0:NS], None, ALU.mult).then_inc(s_("olat_ready"), 1)

            def out_latT(b, s):
                dve.wait_ge(s_("olT_done"), b + 1)
                for c in range(LC):
                    last = nc.vector.tensor_copy(oT_lat[:, c, :, bass.ds(b, 1), :].rearrange("p h a q -> p (h a) q"),
                                                 ps[:, 6, 256 + c * NS:256 + (c + 1) * NS].rearrange("p (h q) -> p h q", q=TQ))
                last.then_inc(s_("olT_ready"), 1)

            def quad(b, s, q):
                dve.wait_ge(s_("rstdk_ready"), 4 * b + q + 1)
                dve.wait_ge(s_("sc_done"), 4 * b + q + 1)
                sc = ps[:, 4 + q % 2, :].rearrange("p (g k n) -> p g k n", g=4, k=2)
                ch.link(nc.vector.tensor_tensor(s_part, sc[:, :, 0, :].rearrange("p g (h q) -> p g h q", q=TQ),
                                                rstd_k[:, 4 * q:4 * q + 4, :].unsqueeze(3).to_broadcast([P, 4, NH, TQ]), ALU.mult))
                nc.vector.tensor_tensor(s_tok[s][:, 4 * q:4 * q + 4, :], s_part.rearrange("p g h q -> p g (h q)"),
                                        sc[:, :, 1, :], ALU.add).then_inc(s_("sc_used"), 1)

            def last_quad(b, s):
                quad(b, s, 3)
                ch.link(nc.vector.tensor_copy(s_tok[s][:, NPAGE, :].rearrange("p (h q) -> p h q", q=TQ),
                                              s_self[:, :, bass.ds(b, 1), :].rearrange("p h a q -> p (h a) q")))
                dve.wait_ge(s_("sc_used"), 4 * b + 4)
                col_max(b, s)

            def seq_dve(b, s, prev, c):
                for g in range(NPAGE):
                    q = g // 4
                    dve.wait_ge(s_("ksq_ready"), NPAGE * b + g + 1)
                    nc.vector.reduce_sum(ms_k[:, g, :], ksq[g % 2].rearrange("p (h d) -> p h d", d=DN), AXX)\
                        .then_inc(s_("ksum_done"), 1)
                    if prev and g == 4:
                        row_of_max(b - 1, 1 - s)
                    if NPAGE * s + g < CK:
                        tap(c, NPAGE * s + g)
                    if g % 4 == 3:
                        dve.wait_ge(s_("ksum_done"), NPAGE * b + g + 1)
                        nc.vector.tensor_scalar(ms_k[:, 4 * q:4 * q + 4, :], ms_k[:, 4 * q:4 * q + 4, :], 1.0 / DN, EPS,
                                                ALU.mult, ALU.add).then_inc(s_("msk_ready"), 1)
                    if g in (5, 9, 13):
                        quad(b, s, (g - 5) // 4)
                    if prev and g == 2:
                        last_quad(b - 1, 1 - s)
                    if prev and g == 5:
                        shift(b - 1, 1 - s)
                    if prev and g == 11:
                        out_lat(b - 1, 1 - s)
                    if prev and g == 14:
                        out_latT(b - 1, 1 - s)
                if s == 1:
                    dve.wait_ge(s_("yT_done"), c + 1)
            seq_dve(0, 0, False, 0)
            seq_dve(1, 1, True, 0)
            with ch.loop(NSEQ // 2 - 1, 44) as p:
                for s in range(2):
                    seq_dve(2 * p + s + 2, s, True, p + 1)


            def centre(t, rows):
                r = slice(0, rows)
                cv = conv_tok[r, bass.ds(t, 1), :].rearrange("p a n -> p (a n)")
                ch.link(nc.vector.reduce_sum(st(4)[r], cv, AXX))
                ch.link(nc.vector.tensor_scalar(st(5)[r], st(4)[r], 1.0 / CC, None, ALU.mult))
                nc.vector.tensor_scalar(conv_n[r, :], cv, st(5)[r], None, ALU.subtract).then_inc(s_("centred"), 1)

            def variance(t, rows):
                r = slice(0, rows)
                dve.wait_ge(s_("var_sumsq"), t + 1)
                nc.vector.tensor_scalar(st(7)[r], st(24)[r], 1.0 / CC, EPS, ALU.mult, ALU.add).then_inc(s_("var_ready"), 1)

            def layer_norm(t, rows):
                r = slice(0, rows)
                dve.wait_ge(s_("rstd_ln"), t + 1)
                ch.link(nc.vector.scalar_tensor_tensor(conv_n[r, :], conv_n[r, :], st(6)[r], ln_g[r, :], ALU.mult, ALU.mult))
                nc.vector.tensor_tensor(conv_n[r, :], conv_n[r, :], ln_b[r, :], ALU.add).then_inc(s_("ln_ready"), 1)

            def mix_scale(t, rows):
                r = slice(0, rows)
                dve.wait_ge(s_("mix_sumsq"), t + 1)
                nc.vector.tensor_scalar(st(20, 2)[r], st(16, 2)[r], 1.0 / CC, EPS, ALU.mult, ALU.add).then_inc(s_("msm_ready"), 1)
                dve.wait_ge(s_("rstd_m"), t + 1)
                nc.vector.tensor_scalar(mixn[r, 0:CC], attn_tok[r, bass.ds(t, 1), :].rearrange("p a n -> p (a n)"), st(22)[r], None, ALU.mult)
                nc.vector.tensor_scalar(mixn[r, CC:2 * CC], conv_n[r, :], st(23)[r], None, ALU.mult).then_inc(s_("m_xn"), 1)

            def x2_view(t, r):
                return x2[r, bass.ds(t, 1), :].rearrange("p a n -> p (a n)")

            def residual(t, s, v, rows):
                r = slice(0, rows)
                dve.wait_ge(s_(f"xr_loaded{s}"), 16 * v)
                dve.wait_ge(s_("c_wout_done"), t + 1)
                nc.vector.tensor_tensor(x2_view(t, r), ps[r, OUT[s]:OUT[s] + 2, :].rearrange("p a n -> p (a n)"), xr[s][r, :],
                                        ALU.add).then_inc(s_("x2_ready"), 1)

            def split_h(t):
                one = lambda v: v[:, bass.ds(t, 1)].rearrange("p a k c -> p (a k) c")
                nt_dve_gain(dve, "c", t + 1, P, 4, "norm_ffn", one(h_full))
                dve.wait_ge(s_("c_hT"), t + 1)
                ch.link(nc.vector.tensor_copy(one(h_hi_r), one(h_full)))
                nc.vector.tensor_tensor(one(h_lo_r), one(h_full), one(h_hi), ALU.subtract).then_inc(s_("h_split"), 1)

            def tile_c(t, s, rows, v, ahead):
                if ahead:
                    centre(t + 1, ahead)
                if not first(t):
                    residual(t - 1, 1 - s, v if s == 1 else v - 1, P)
                if ahead:
                    variance(t + 1, ahead)
                if not first(t):
                    nt_dve_mean(dve, "c", t, P, 0)
                if ahead:
                    layer_norm(t + 1, ahead)
                if not first(t):
                    nt_dve_scale(dve, "c", t, x2_view(t - 1, slice(0, P)), P, 0, xn2)
                if ahead:
                    mix_scale(t + 1, ahead)
                    nt_dve_gain(dve, "m", t + 2, ahead, 0, "norm_out_attn", mT[:, :, 0:ahead])
                if not first(t):
                    split_h(t - 1)
            dve.wait_ge(s_("yT_ready"), CCH)
            dve.wait_ge(s_("ln_loaded"), 32)
            centre(0, P)
            variance(0, P)
            last_quad(NSEQ - 1, 1)
            layer_norm(0, P)
            row_of_max(NSEQ - 1, 1)
            shift(NSEQ - 1, 1)
            mix_scale(0, P)
            nt_dve_gain(dve, "m", 1, P, 0, "norm_out_attn", mT)
            out_lat(NSEQ - 1, 1)
            out_latT(NSEQ - 1, 1)
            tiles(ch, 8, tile_c)
            residual(TILES, 0, TILES // 2 + 1, NS)
            nt_dve_mean(dve, "c", NT, NS, 0)
            nt_dve_scale(dve, "c", NT, x2_view(TILES, slice(0, NS)), NS, 0, xn2)
            nt_dve_gain(dve, "c", NT, NS, 4, "norm_ffn", h_s)

            def split_low(s, n):
                dve.wait_ge(s_("w_hi_ready"), n)
                nc.vector.tensor_tensor(w_lo_r[s], w_raw[s], w_hi[s], ALU.subtract).then_inc(s_("w_split"), 1)

            def ffn_dve(g, end):
                for s in range(2):
                    if not (end and s == 1):
                        split_low(1 - s, 2 * g + s + 2)
                    if s == 0:
                        dve.wait_ge(s_("wd_hi_ready"), g + 1)
                        for a in range(2):
                            last = nc.vector.tensor_tensor(wd_lo_r[:, a, :], wd_raw[a], wd_hi[:, a, :], ALU.subtract)
                        last.then_inc(s_("wd_split"), 1)
                    for b, (at, n) in enumerate(BLOCKS):
                        c = slice(at, at + n)
                        dve.wait_ge(s_("silu_ready"), 6 * g + 3 * s + b + 1)
                        dve.wait_ge(s_("up_done"), 6 * g + 3 * s + b + 1)
                        ch.link(nc.vector.tensor_tensor(gate_s[:, c], gate_s[:, c], ps[:, 2 * b + 1, 0:n], ALU.mult))
                        ch.link(nc.vector.tensor_copy(a_hi_r[s][:, c], gate_s[:, c]))
                        nc.vector.tensor_tensor(a_lo_r[s][:, c], gate_s[:, c], a_hi[s][:, c], ALU.subtract).then_inc(s_("aT_ready"), 1)
                for t in range(NT):
                    rows = P if t < TILES else NS
                    for h in range(2):
                        dve.wait_ge(s_("dn_done"), 2 * NT * g + 2 * t + h + 1)
                        d = x2[0:rows, t, h * HALF:(h + 1) * HALF]
                        nc.vector.tensor_tensor(d, d, ps[0:rows, 6 + h, :], ALU.add).then_inc(s_("dn_evac"), 1)
            split_low(0, 1)
            with ch.loop(GROUPS - 1, 12) as g:
                ffn_dve(g, False)
            ffn_dve(GROUPS - 1, True)

            dve.wait_ge(s_("dn_evac"), 2 * NT * GROUPS)

            def scale_d(t, rows):
                nt_dve_mean(dve, "d", t + 1, rows, 0)
                nt_dve_scale(dve, "d", t + 1, x2[0:rows, bass.ds(t, 1), :].rearrange("p a n -> p (a n)"), rows, 0, xn4)

            def gain_split(n, rows):
                c = slice(0, rows)
                nt_dve_gain(dve, "d", n, rows, 0, "norm_ple", h4_full[:, :, c])
                dve.wait_ge(s_("d_hT"), n)
                ch.link(nc.vector.tensor_copy(h4_hi_r[:, :, c], h4_full[:, :, c]))
                nc.vector.tensor_tensor(h4_lo_r[:, :, c], h4_full[:, :, c], h4_hi[:, :, c], ALU.subtract).then_inc(s_("h4_split"), 1)

            def tile_d(t, s, rows, v, ahead):
                r = slice(0, rows)
                if ahead:
                    scale_d(t + 1, ahead)
                    gain_split(t + 2, ahead)
                dve.wait_ge(s_("sg_ready"), t + 1)
                dve.wait_ge(s_("pp_done"), t + 1)
                ch.link(nc.vector.tensor_tensor(sg[r, :], sg[r, :], ps[r, 5:7, :].rearrange("p a n -> p (a n)"), ALU.mult))
                nc.vector.tensor_tensor(y_out[s][r, :], sg[r, :], x2[r, bass.ds(t, 1), :].rearrange("p a n -> p (a n)"),
                                        ALU.add).then_inc(s_("y_ready"), 1)
                if not first(t):
                    dve.wait_ge(s_(f"y_stored{1 - s}"), 16 * (v if s == 1 else v - 1))
            scale_d(0, P)
            gain_split(1, P)
            tiles(ch, 4, tile_d)

        @block.tensor
        def _(pe):
            ch = Chain(pe, None)
            mm, tr = nc.tensor.matmul, nc.tensor.transpose
            pe.wait_ge(s_("ident_ready"), 1)
            nt_pe(pe, "a", 1, P, x_in[0], T0)
            pe.wait_ge(s_("consts"), 16 * (len(COLS) + 1))
            tr(ps[:, P0, 0:NCOL], gain_rows, ident[0:NCOL, 0:NCOL])
            for c in range(CCH):
                last = tr(ps[:, P1, c * CK:(c + 1) * CK], tap_rows[:, c * P:(c + 1) * P], ident[0:CK, 0:CK])
            last.then_inc(s_("colT_done"), 1)

            def qk_T(t, rows):
                pe.wait_ge(s_("qh_ready"), t + 1)
                for h in range(NH):
                    last = tr(ps[0:DQ, T0 + h // 4, (h % 4) * P:(h % 4) * P + rows], qh[0:rows, h, :], ident[0:rows, 0:rows])
                last.then_inc(s_("qT_done"), 1)
                pe.wait_ge(s_("kh_ready"), t + 1)
                for h in range(NH):
                    last = tr(ps[0:DQ, P0 + h // 4, (h % 4) * P:(h % 4) * P + rows], kh[0:rows, h, :], ident[0:rows, 0:rows])
                last.then_inc(s_("kT_done"), 1)

            def tile_a(t, s, rows, v, ahead):
                pe.wait_ge(s_("a_hT"), t + 1)
                if first(t):
                    pe.wait_ge(s_("w_lat_loaded"), 16)
                else:
                    pe.wait_ge(s_("gluT_ready"), t)
                for bank, c0, n in ((Z0, 0, QL), (Z1, QL, KL + DR)):
                    for k in range(KC):
                        last = mm(ps[0:rows, bank, 0:n], hT[:, k, 0:rows], w_in[:, k, c0:c0 + n], start=(k == 0), stop=(k == KC - 1))
                last.then_inc(s_("z_lat_done"), 1)
                if first(t):
                    pe.wait_ge(s_("w_glu_loaded"), 16)
                else:
                    qk_T(t - 1, P)
                    pe.wait_ge(s_("v_ready"), t)
                for bank, c0 in ((Z3, QL + KL + DR + CC), (Z2, QL + KL + DR)):
                    for k in range(KC):
                        last = mm(ps[0:rows, bank, :], hT[:, k, 0:rows], w_in[:, k, c0:c0 + CC], start=(k == 0), stop=(k == KC - 1))
                last.then_inc(s_("z_glu_done"), 1)
                if not first(t):
                    pe.wait_ge(s_("qT_ready"), t)
                if ahead:
                    nt_pe(pe, "a", t + 2, ahead, x_in[1 - s], T0)
                    pe.wait_ge(s_("a_hT"), t + 2)
                pe.wait_ge(s_("lat_ready"), t + 1)
                for k in range(5):
                    src = cqn[0:rows, k * P:(k + 1) * P] if k < 3 else ckvn[0:rows, (k - 3) * P:(k - 2) * P]
                    last = tr(ps[:, T0 + k // 4, (k % 4) * P:(k % 4) * P + rows], src, ident[0:rows, 0:rows])
                last.then_inc(s_("cT_done"), 1)
                pe.wait_ge(s_("glu_ready"), t + 1)
                for k in range(CCH):
                    last = tr(ps[:, Z0, k * P:k * P + rows], glu_t[0:rows, k * P:(k + 1) * P], ident[0:rows, 0:rows])
                last.then_inc(s_("gluT_done"), 1)
                if first(t):
                    pe.wait_ge(s_("w_u_loaded"), 48)
                else:
                    pe.wait_ge(s_("kT_ready"), t)
                pe.wait_ge(s_("cT_ready"), t + 1)
                for a in range(2):
                    for k in range(QL // P):
                        last = mm(ps[0:rows, P0 + a, 0:QL], cT[:, k, 0:rows], w_uq[:, k, a * QL:(a + 1) * QL], start=(k == 0), stop=(k == QL // P - 1))
                last.then_inc(s_("q_done"), 1)
                for bank, w in ((Z2, w_uk), (Z3, w_uv)):
                    for k in range(LC):
                        last = mm(ps[0:rows, bank, :], cT[:, 3 + k, 0:rows], w[:, k, :], start=(k == 0), stop=(k == LC - 1))
                last.then_inc(s_("kv_done"), 1)
            tiles(ch, 0, tile_a)
            pe.wait_ge(s_("hist_loaded"), 32)
            pe.wait_ge(s_("gluT_ready"), NT)
            pe.wait_ge(s_("lat_ready"), NT)
            for a in range(2):
                for c in range(CCH):
                    last = tr(ps[:, Z0 + a, c * 120:(c + 1) * 120], hist[0:120, a, c * P:(c + 1) * P], ident[0:120, 0:120])
            last.then_inc(s_("hist_done"), 1)
            qk_T(TILES, NS)

            pe.wait_ge(s_("kT_ready"), NT)
            pe.wait_ge(s_("qT_ready"), NT)
            for h in range(NH):
                for k in range(LC):
                    last = tr(ps[0:DN, h // 2, (h % 2) * KL + k * P:(h % 2) * KL + (k + 1) * P], w_uk[:, k, h * DN:(h + 1) * DN], ident[:, :])
            last.then_inc(s_("wukT_done"), 1)
            for h in range(NH):
                last = mm(ps[0:NS, 7, h * NS:(h + 1) * NS], kT_s[:, h, :], qT_s[:, h, :], start=True, stop=True)
            last.then_inc(s_("self_done"), 1)
            pe.wait_ge(s_("wukT_ready"), 1)
            for h in range(NH):
                for k in range(LC):
                    last = mm(ps[:, 4 + k, h * NS:(h + 1) * NS], w_ukT[:, h, k * P:(k + 1) * P], qT_s[0:DN, h, :], start=True, stop=True)
            last.then_inc(s_("qabs_done"), 1)
            pe.wait_ge(s_("qabs_ready"), 1)
            pe.wait_ge(s_("self_ready"), 1)
            def scores(c, m):
                hp, i = ORDER[m % PAIR]
                if i == 0:
                    pe.wait_ge(s_("qTh_ready"), 2 * c + 2 * (m // PAIR) + hp + 1)
                n = (i + 1) * P
                for a in range(0, n, 512):
                    w = min(512, n - a)
                    last = mm(ps[:, 2 * (m % 2) + a // 512, 0:w], qTh[hp][:, i * P:(i + 1) * P],
                              kT[:, bass.ds(2 * c + 2 * (m // PAIR) + hp, 1), a:a + w].rearrange("p a n -> p (a n)"), start=True, stop=True)
                last.then_inc(s_("scores_done"), 1)

            def pair_pe(c, start, end):
                for m in range(PAIR):
                    hp, i = ORDER[m]
                    pe.wait_ge(s_("prob_ready"), PAIR * c + m + 1)
                    for j in range(i + 1):
                        last = tr(ps[:, 4 + j // 4, (j % 4) * P:(j % 4 + 1) * P], prob[m % 2][:, j * P:(j + 1) * P], ident[:, :])
                        if j == min(i, 3):
                            last.then_inc(s_("ptA_done"), 1)
                    if i >= 4:
                        last.then_inc(s_("ptB_done"), 1)
                    if m < PAIR - 2 or not end:
                        scores(c, m + 2)
                    if m >= 2 or not start:
                        pe.wait_ge(s_("o_evac"), PAIR * c + m - 1)
                    pe.wait_ge(s_("ptA_ready"), PAIR * c + m + 1)
                    for j in range(i + 1):
                        if j == 4:
                            pe.wait_ge(s_("ptB_ready"), TILES * c + long_blocks(m))
                        last = mm(ps[:, 6 + m % 2, 0:DV], pT[:, j * P:(j + 1) * P],
                                  V[:, j, bass.ds((2 * c + hp) * DV, DV)], start=(j == 0), stop=(j == i))
                    last.then_inc(s_("pv_done"), 1)
            scores(0, 0)
            scores(0, 1)
            pair_pe(0, True, False)
            with pe.Fori(1, NH // 2 - 1) as c:
                pair_pe(c, False, False)
            pair_pe(NH // 2 - 1, False, True)
            pe.wait_ge(s_("o_evac"), PAIR * NH // 2)
            def page_T(s, g):
                r = g % 2
                for k in range(LC):
                    tr(ps[:, r, k * P:(k + 1) * P], pages[s][:, g, k * P:(k + 1) * P], ident[:, :])
                tr(ps[0:DR, r, LC * P:(LC + 1) * P], kpe[s][:, g, :], ident[:, :]).then_inc(s_("ctr_done"), 1)

            def seq_pe(b, s, prev, loads, next_loads):
                for g in range(NPAGE):
                    r, q = g % 2, g // 4
                    if g < NPAGE - 1:
                        if g == NPAGE // 2 - 1:
                            pe.wait_ge(s_(f"pages_loaded{s}1"), PAGES_HALF * loads)
                        page_T(s, g + 1)
                    elif next_loads is not None:
                        pe.wait_ge(s_(f"pages_loaded{1 - s}0"), PAGES_HALF * next_loads)
                        page_T(1 - s, 0)
                    pe.wait_ge(s_("ctr_ready"), NPAGE * b + g + 1)
                    if g >= 2 or prev:
                        pe.wait_ge(s_("ksq_ready"), NPAGE * b + g - 1)
                    for k in range(LC):
                        last = mm(ps[:, 2 + r, :], cT_ring[r][:, k, :], w_uk[:, k, :], start=(k == 0), stop=(k == LC - 1))
                    last.then_inc(s_("k_done"), 1)
                    if g % 4 == 0 and (q >= 2 or prev):
                        pe.wait_ge(s_("sc_used"), 4 * b + q - 1)
                    o = (g % 4) * P
                    for k in range(LC):
                        mm(ps[:, 4 + q % 2, o:o + NS], cT_ring[r][:, k, :], q_abs[:, k, :, bass.ds(b * TQ, TQ)], start=(k == 0), stop=(k == LC - 1))
                    last = mm(ps[:, 4 + q % 2, o + NS:o + 2 * NS], kpeT_ring[r], q_pe[:, :, bass.ds(b * TQ, TQ)], start=True, stop=True)
                    if g % 4 == 3:
                        last.then_inc(s_("sc_done"), 1)
                    if prev and g == 4:
                        max_T(b - 1)
                    if prev and g == 5:
                        max_B(b - 1)
                    if prev and g == 8:
                        pv(b - 1, 1 - s)
                    if prev and g == 13:
                        lat_T(b - 1)

            def chunk_T(b, c):
                pe.wait_ge(s_("ksq_ready"), NPAGE * b + NPAGE)
                pe.wait_ge(s_("olT_ready"), b)
                pe.wait_ge(s_("y_ready_c"), c + 1)
                for t in range(TILES):
                    tr(ps[:, 2 + t // 4, (t % 4) * P:(t % 4 + 1) * P], y_c[:, t * P:(t + 1) * P], ident[:, :])
                tr(ps[0:NS, 6, 384:384 + P], y_s.rearrange("p b q -> p (b q)"), ident[:, :]).then_inc(s_("yT_done"), 1)
                pe.wait_ge(s_("yT_ready"), c + 1)

            def max_T(b):
                pe.wait_ge(s_("mpart_ready"), b + 1)
                mm(ps[0:NS, 6, 0:P], m_part, ident[:, :], start=True, stop=True).then_inc(s_("mT_done"), 1)

            def max_B(b):
                pe.wait_ge(s_("mrow_ready"), b + 1)
                mm(ps[:, 6, P:P + NS], m_row[0:NS, :], ident[0:NS, 0:NS], start=True, stop=True).then_inc(s_("mB_done"), 1)

            def pv(b, s):
                pe.wait_ge(s_("ptok_ready"), b + 1)
                for g in range(NPAGE + 1):
                    last = mm(ps[0:NS, 7, 0:KL + 1], p_tok[:, g, :], pages[s][:, g, :], start=(g == 0), stop=(g == NPAGE))
                last.then_inc(s_("pv_s_done"), 1)

            def lat_T(b):
                pe.wait_ge(s_("olat_ready"), b + 1)
                for k in range(LC):
                    last = mm(ps[:, 6, 256 + k * NS:256 + (k + 1) * NS], o_lat[0:NS, k * P:(k + 1) * P], ident[0:NS, 0:NS], start=True, stop=True)
                last.then_inc(s_("olT_done"), 1)
            pe.wait_ge(s_("pages_loaded00"), PAGES_HALF)
            page_T(0, 0)
            seq_pe(0, 0, False, 1, 1)
            seq_pe(1, 1, True, 1, 2)
            chunk_T(1, 0)
            with ch.loop(NSEQ // 2 - 2, 0) as p:
                seq_pe(2 * p + 2, 0, True, p + 2, p + 2)
                seq_pe(2 * p + 3, 1, True, p + 2, p + 3)
                chunk_T(2 * p + 3, p + 1)
            seq_pe(NSEQ - 2, 0, True, NSEQ // 2, NSEQ // 2)
            seq_pe(NSEQ - 1, 1, True, NSEQ // 2, None)
            chunk_T(NSEQ - 1, CCH - 1)
            max_T(NSEQ - 1)
            max_B(NSEQ - 1)
            nt_pe(pe, "m", 1, P, mixn, 0)
            pv(NSEQ - 1, 1)
            lat_T(NSEQ - 1)
            pe.wait_ge(s_("olT_ready"), NSEQ)
            for h in range(NH):
                for k in range(LC):
                    last = mm(ps[0:NS, 4, h * DV:(h + 1) * DV], oT_lat[:, k, h, :, :].rearrange("p b q -> p (b q)"),
                              w_uv[:, k, h * DV:(h + 1) * DV], start=(k == 0), stop=(k == LC - 1))
            last.then_inc(s_("ov_done"), 1)
            pe.wait_ge(s_("w_out_loaded"), 16)

            def tile_c(t, s, rows, v, ahead):
                pe.wait_ge(s_("m_hT"), t + 1)
                for h in range(2):
                    for k in range(KC):
                        last = mm(ps[0:rows, OUT[s] + h, :], mT[:, k, 0:rows], w_out[:, k, h * HALF:(h + 1) * HALF], start=(k == 0), stop=(k == KC - 1))
                last.then_inc(s_("c_wout_done"), 1)
                if ahead:
                    nt_pe(pe, "m", t + 2, ahead, mixn, 0)
                if not first(t):
                    nt_pe(pe, "c", t, P, xn2, 4)
            tiles(ch, 0, tile_c)
            nt_pe(pe, "c", NT, NS, xn2, 4)

            pe.wait_ge(s_("c_hT"), NT)

            def split_mm(out, left, right, start, stop):
                mm(out, left[0], right[0], start=start, stop=False)
                mm(out, left[0], right[1], start=False, stop=False)
                return mm(out, left[1], right[0], start=False, stop=stop)

            def group(g, start):
                for s in range(2):
                    for b, (at, n) in enumerate(BLOCKS):
                        if b == 0:
                            pe.wait_ge(s_(f"gu_loaded{s}"), 32 * (g + 1))
                        if b == 1:
                            pe.wait_ge(s_("w_split"), 2 * g + s + 1)
                            if start:
                                pe.wait_ge(s_("h_split"), TILES)
                        if not (start and s == 0):
                            pe.wait_ge(s_("aT_ready"), 6 * g + 3 * (s - 1) + b + 1)
                        for u, done in enumerate(("gate_done", "up_done")):
                            out = ps[:, 2 * b + u, 0:n]
                            for k in range(KC):
                                ends = dict(start=(k == 0), stop=(k == KC - 1))
                                if b == 0:
                                    last = mm(out, w_raw[s][:, u, k, :], h_s[:, k, :], **ends)
                                else:
                                    tt = slice(at // P, (at + n) // P)
                                    last = split_mm(out.rearrange("p (t c) -> p t c", c=P),
                                                    (w_hi_r[s][:, u, k, :], w_lo_r[s][:, u, k, :]),
                                                    (h_hi_r[:, tt, k, :], h_lo_r[:, tt, k, :]), **ends)
                            last.then_inc(s_(done), 1)
                pe.wait_ge(s_("wd_split"), g + 1)
                for t in range(NT):
                    rows = P if t < TILES else NS
                    b = [i for i, (at, n) in enumerate(BLOCKS) if at <= t * P < at + n][0]
                    pe.wait_ge(s_("aT_ready"), 6 * g + 3 + b + 1)
                    c = slice(t * P, t * P + rows)
                    for h in range(2):
                        if not (start and t == 0):
                            pe.wait_ge(s_("dn_evac"), 2 * NT * g + 2 * (t - 1) + h + 1)
                        e = slice(h * HALF, (h + 1) * HALF)
                        for s in range(2):
                            last = split_mm(ps[0:rows, 6 + h, :], (a_hi_r[s][:, c], a_lo_r[s][:, c]),
                                            (wd_hi_r[:, s, e], wd_lo_r[:, s, e]), start=(s == 0), stop=(s == 1))
                        last.then_inc(s_("dn_done"), 1)
            group(0, True)
            with pe.Fori(1, GROUPS) as g:
                group(g, False)

            pe.wait_ge(s_("dn_evac"), 2 * NT * GROUPS)

            def p_T_pe(n, s, count, rows):
                pe.wait_ge(s_(f"p_loaded{s}"), 16 * count)
                for k in range(PLE // P):
                    last = tr(ps[:, 2, k * P:k * P + rows], p_in[s][0:rows, k * P:(k + 1) * P], ident[0:rows, 0:rows])
                last.then_inc(s_("ppT_done"), 1)

            def tile_d(t, s, rows, v, ahead):
                pe.wait_ge(s_("h4_split"), t + 1)
                if not first(t):
                    pe.wait_ge(s_("sg_ready"), t)
                for h in range(2):
                    if first(t):
                        pe.wait_ge(s_("w_pg_split"), h + 1)
                    for k in range(KC):
                        e = slice(h * HALF, (h + 1) * HALF)
                        last = split_mm(ps[0:rows, 3 + h, :], (h4_hi_r[:, k, 0:rows], h4_lo_r[:, k, 0:rows]),
                                        (w_pg_hi_r[:, k, e], w_pg_lo_r[:, k, e]), start=(k == 0), stop=(k == KC - 1))
                last.then_inc(s_("pg_done"), 1)
                if ahead:
                    nt_pe(pe, "d", t + 2, ahead, xn4, 0)
                pe.wait_ge(s_("ppT_ready"), t + 1)
                if first(t):
                    pe.wait_ge(s_("w_pp_loaded"), 16)
                if not first(t):
                    pe.wait_ge(s_("y_ready"), t)
                for h in range(2):
                    for k in range(PLE // P):
                        last = mm(ps[0:rows, 5 + h, :], p_T[:, k, 0:rows], w_pp[:, k, h * HALF:(h + 1) * HALF], start=(k == 0), stop=(k == PLE // P - 1))
                last.then_inc(s_("pp_done"), 1)
                if ahead:
                    p_T_pe(t + 2, 1 - s, slot_count(t, s, v), ahead)
            p_T_pe(1, 0, 1, P)
            nt_pe(pe, "d", 1, P, xn4, 0)
            tiles(ch, 0, tile_d)


_INS = ["x_prompt", "x_sample", "cache_ckv", "cache_kpe", "state_conv", "page_table", "p_prompt", "p_sample",
        "norm_mix", "w_in", "q_lora_norm", "w_uq", "kv_norm", "w_uk", "w_uv", "q_nope_norm", "k_nope_norm",
        "q_pe_norm", "k_pe_norm", "conv_w", "conv_b", "conv_ln_g", "conv_ln_b", "norm_out_attn", "norm_out_conv",
        "w_out", "norm_ffn", "w_gate", "w_up", "w_down", "norm_ple", "w_ple_gate", "w_ple_proj"]
_OUTS = [(1, SEQ, DM), (NSEQ, TQ, DM), (1, 1, SEQ, KL), (1, 1, SEQ, DR), (1, 1, HIST, CC),
         (1, NSEQ, TQ, KL), (1, NSEQ, TQ, DR), (1, NSEQ, HIST, CC)]


def rope_rows():
    pos = np.concatenate([np.arange(SEQ), np.tile(PAST + np.arange(TQ), NSEQ)]).astype(np.float32)
    inv = (np.float32(1.0) / np.power(np.float32(10000.0), np.arange(0, DR, 2, dtype=np.float32) / np.float32(DR))).astype(np.float32)
    ang = pos[:, None] * inv[None, :]
    return np.concatenate([np.cos(ang), np.sin(ang)], axis=1).astype(np.float32)


def kernel(**inputs):
    import numpy as _np
    import concourse.bacc as _bacc
    from concourse import mybir as _mybir
    from concourse.bass_utils import run_bass_kernel_spmd as _run

    nc = _bacc.Bacc("TRN2", target_bir_lowering=False, num_devices=1, dynamic_dma_scratch_size=1024)
    arrays, args = {}, {}
    for name in _INS:
        a = _np.ascontiguousarray(inputs[name])
        arrays[f"in_{name}"] = a
        args[name] = nc.dram_tensor(f"in_{name}", a.shape, _mybir.dt.from_np(a.dtype), kind="ExternalInput").ap()
    arrays["in_rope"] = rope_rows()
    args["rope"] = nc.dram_tensor("in_rope", arrays["in_rope"].shape, _mybir.dt.float32, kind="ExternalInput").ap()
    outs = [nc.dram_tensor(f"out_{i}", shape, _mybir.dt.float32, kind="ExternalOutput").ap() for i, shape in enumerate(_OUTS)]
    build(nc, args, outs)
    r = _run(nc, [arrays], core_ids=[0])
    return tuple(r.results[0][f"out_{i}"] for i in range(len(_OUTS)))
```
